# Optimizing a Trainium2 kernel written in Bass

```python
import math
import jax
import jax.numpy as jnp
from jax import lax
import numpy as np
import jax, jax.numpy as jnp

D_MODEL = 1024
BATCH = 1
SEQ = 256
DEPTH = 1

CHUNK = 64
EPS = 1e-6
ROPE_THETA = 10000.0
A_HEADS = 8
A_DK = 64
A_DV = 64
CONV_K = 4
B_HEADS = 8
B_KV_HEADS = 2
B_HD = 64
IDX_HEADS = 8
IDX_HD = 64
TOPK_MAX = 256
N_GROUPS = 4
EXPERTS_PER_GROUP = 4
N_EXPERTS = N_GROUPS * EXPERTS_PER_GROUP
TOPK_IN_GROUP = 2
D_EXPERT = 256

A_QK_W = A_HEADS * A_DK
A_V_W = A_HEADS * A_DV
B_Q_W = B_HEADS * B_HD
B_KV_W = B_KV_HEADS * B_HD
CONV_W = 2 * A_QK_W + A_V_W
IN_SPLITS = (
    ("a_q", A_QK_W), ("a_k", A_QK_W), ("a_v", A_V_W), ("a_z", A_V_W),
    ("a_beta", A_HEADS), ("a_alpha", A_HEADS),
    ("b_q", B_Q_W), ("b_k", B_KV_W), ("b_v", B_KV_W),
    ("i_q", IDX_HEADS * IDX_HD), ("i_k", IDX_HD), ("i_w", IDX_HEADS),
    ("gate_a", D_MODEL), ("gate_b", D_MODEL),
)
D_IN = sum(n for _, n in IN_SPLITS)


def rmsnorm(x, g):
    xf = x.astype(jnp.float32)
    y = xf * lax.rsqrt(jnp.mean(xf * xf, axis=-1, keepdims=True) + EPS)
    return (y * g.astype(jnp.float32)).astype(x.dtype)

def l2norm(x):
    xf = x.astype(jnp.float32)
    return xf * lax.rsqrt(jnp.sum(xf * xf, axis=-1, keepdims=True) + EPS)

def split_cols(z):
    parts, off = {}, 0
    for name, n in IN_SPLITS:
        parts[name] = z[..., off:off + n]
        off += n
    return parts

def rope(x, pos):
    half = x.shape[-1] // 2
    inv = ROPE_THETA ** (-jnp.arange(half, dtype=jnp.float32) / half)
    ang = pos.astype(jnp.float32)[..., None] * inv
    cos = jnp.cos(ang)[:, :, None, :]
    sin = jnp.sin(ang)[:, :, None, :]
    xf = x.astype(jnp.float32)
    x1, x2 = xf[..., :half], xf[..., half:]
    return jnp.concatenate([x1 * cos - x2 * sin, x2 * cos + x1 * sin], axis=-1).astype(x.dtype)

def causal_dwconv(x, w):
    c = x.shape[-1]
    return lax.conv_general_dilated(
        x, w[:, None, :].astype(x.dtype), window_strides=(1,), padding=[(CONV_K - 1, 0)],
        dimension_numbers=("NWC", "WIO", "NWC"), feature_group_count=c)

def gated_delta_rule(q, k, v, g, beta):
    b, s, h, dk = q.shape
    dv = v.shape[-1]
    n = s // CHUNK

    def chunks(t):
        return jnp.moveaxis(t.reshape((b, n, CHUNK, h) + t.shape[3:]), 3, 1)

    qc, kc, vc, gc, bc = chunks(q), chunks(k), chunks(v), chunks(g), chunks(beta)
    G = jnp.cumsum(gc, axis=-1)
    idx = jnp.arange(CHUNK)
    incl = idx[:, None] >= idx[None, :]
    strict = idx[:, None] > idx[None, :]
    decay = jnp.exp(jnp.where(incl, G[..., :, None] - G[..., None, :], -jnp.inf))
    kk = jnp.einsum("bhnid,bhnjd->bhnij", kc, kc)
    a_mat = jnp.where(strict, bc[..., :, None] * kk * decay, 0.0) + jnp.eye(CHUNK, dtype=jnp.float32)
    rhs = jnp.concatenate([vc * bc[..., None], kc * (bc * jnp.exp(G))[..., None]], axis=-1)
    sol = lax.linalg.triangular_solve(a_mat, rhs, left_side=True, lower=True, unit_diagonal=True)
    u, w = sol[..., :dv], sol[..., dv:]
    qk = jnp.einsum("bhnid,bhnjd->bhnij", qc, kc) * decay
    q_dec = qc * jnp.exp(G)[..., None]
    k_dec = kc * jnp.exp(G[..., -1:] - G)[..., None]
    g_last = jnp.exp(G[..., -1])

    def step(state, xs):
        u_n, w_n, q_n, qk_n, k_n, gl_n = xs
        v_new = u_n - jnp.einsum("bhck,bhkv->bhcv", w_n, state)
        o_n = jnp.einsum("bhck,bhkv->bhcv", q_n, state) + jnp.einsum("bhij,bhjv->bhiv", qk_n, v_new)
        state = state * gl_n[..., None, None] + jnp.einsum("bhck,bhcv->bhkv", k_n, v_new)
        return state, o_n

    xs = tuple(jnp.moveaxis(t, 2, 0) for t in (u, w, q_dec, qk, k_dec, g_last))
    s0 = jnp.zeros((b, h, dk, dv), jnp.float32)
    _, o = lax.scan(step, s0, xs)
    return jnp.transpose(o, (1, 0, 3, 2, 4)).reshape(b, s, h, dv)

def dsa_attention(q, k, v, qi, ki, wi):
    b, s, hq, d = q.shape
    hk = k.shape[2]
    grp = hq // hk
    n = s // CHUNK
    topk = min(TOPK_MAX, s // 4)
    kf = k.reshape(b, s, hk * d)
    vf = v.reshape(b, s, hk * d)
    kif = ki.astype(jnp.float32)
    key_pos = jnp.arange(s)
    gather = jax.vmap(lambda table, ids: table[ids])

    def to_blocks(t):
        return jnp.moveaxis(t.reshape((b, n, CHUNK) + t.shape[2:]), 1, 0)

    def block(args):
        q_b, qi_b, wi_b, blk = args
        limit = (blk + 1) * CHUNK
        rel = jax.nn.relu(jnp.einsum("bthd,bsd->bths", qi_b.astype(jnp.float32), kif))
        score = jnp.einsum("bth,bths->bts", wi_b.astype(jnp.float32), rel)
        score = jnp.where(key_pos < limit, score, -jnp.inf)
        _, sel = lax.top_k(score, topk)
        valid = sel < limit
        ks = gather(kf, sel).reshape(b, CHUNK, topk, hk, d)
        vs = gather(vf, sel).reshape(b, CHUNK, topk, hk, d)
        qg = q_b.reshape(b, CHUNK, hk, grp, d)
        logits = jnp.einsum("btkgd,btjkd->btkgj", qg, ks).astype(jnp.float32) * (d ** -0.5)
        logits = jnp.where(valid[:, :, None, None, :], logits, -jnp.inf)
        p = jax.nn.softmax(logits, axis=-1).astype(v.dtype)
        o = jnp.einsum("btkgj,btjkd->btkgd", p, vs)
        return o.reshape(b, CHUNK, hq * d)

    out = lax.map(block, (to_blocks(q), to_blocks(qi), to_blocks(wi), jnp.arange(n)))
    return jnp.moveaxis(out, 0, 1).reshape(b, s, hq * d)

def hier_moe(h, w_rg, b_rg, w_re, b_re, w1, w3, w2):
    bsz, s, d = h.shape
    xt = h.reshape(-1, d)
    glog = (xt @ w_rg + b_rg).astype(jnp.float32)
    gp = jax.nn.softmax(glog, axis=-1)
    gsel = jnp.argmax(glog, axis=-1)
    ggate = jnp.take_along_axis(gp, gsel[:, None], axis=-1)
    elog = (xt @ w_re + b_re).astype(jnp.float32).reshape(-1, N_GROUPS, EXPERTS_PER_GROUP)
    elog_g = jnp.take_along_axis(elog, gsel[:, None, None], axis=1)[:, 0]
    ep = jax.nn.softmax(elog_g, axis=-1)
    top_p, top_i = lax.top_k(ep, TOPK_IN_GROUP)
    top_p = top_p / jnp.sum(top_p, axis=-1, keepdims=True)
    wts = ggate * top_p
    eid = gsel[:, None] * EXPERTS_PER_GROUP + top_i
    comb = jnp.sum(jax.nn.one_hot(eid, N_EXPERTS, dtype=jnp.float32) * wts[..., None], axis=1)
    act = jax.nn.silu(jnp.einsum("nd,edf->nef", xt, w1)) * jnp.einsum("nd,edf->nef", xt, w3)
    act = act * comb[:, :, None].astype(act.dtype)
    y = jnp.einsum("nef,efd->nd", act, w2)
    return y.reshape(bsz, s, d)

def first_inputs(seed: int = 0) -> dict:
    key = jax.random.key(seed)
    ks = jax.random.split(key, 24)
    f32 = jnp.float32

    def nrm(k, shape, fan):
        return jax.random.normal(k, shape, f32) * (fan ** -0.5)

    def gain(k, shape):
        return 1.0 + 0.02 * jax.random.normal(k, shape, f32)

    x = jax.random.normal(ks[0], (BATCH, SEQ, D_MODEL), f32)
    offs = jax.random.randint(ks[1], (BATCH, 1), 0, 64) * CHUNK
    positions = (offs + jnp.arange(SEQ, dtype=jnp.int32)[None, :]).astype(jnp.int32)
    norm1_g = gain(ks[2], (DEPTH, D_MODEL))
    w_in = nrm(ks[3], (DEPTH, D_MODEL, D_IN), D_MODEL)
    b_gate = 0.02 * jax.random.normal(ks[4], (DEPTH, 2 * D_MODEL), f32)
    conv_w = nrm(ks[5], (DEPTH, CONV_K, CONV_W), CONV_K)
    a_log = jnp.log(jax.random.uniform(ks[6], (DEPTH, A_HEADS), f32, 1.0, 16.0))
    dt = jnp.exp(jax.random.uniform(ks[7], (DEPTH, A_HEADS), f32, math.log(1e-3), math.log(1e-1)))
    dt_bias = dt + jnp.log(-jnp.expm1(-dt))
    a_norm_g = gain(ks[8], (DEPTH, A_DV))
    w_proj_a = nrm(ks[9], (DEPTH, A_V_W, D_MODEL), A_V_W)
    w_proj_b = nrm(ks[10], (DEPTH, B_Q_W, D_MODEL), B_Q_W)
    w_out = nrm(ks[11], (DEPTH, D_MODEL, D_MODEL), D_MODEL)
    norm2_g = gain(ks[12], (DEPTH, D_MODEL))
    w_router_group = nrm(ks[13], (DEPTH, D_MODEL, N_GROUPS), D_MODEL)
    b_router_group = 0.01 * jax.random.normal(ks[14], (DEPTH, N_GROUPS), f32)
    w_router_expert = nrm(ks[15], (DEPTH, D_MODEL, N_EXPERTS), D_MODEL)
    b_router_expert = 0.01 * jax.random.normal(ks[16], (DEPTH, N_EXPERTS), f32)
    w_exp_gate = nrm(ks[17], (DEPTH, N_EXPERTS, D_MODEL, D_EXPERT), D_MODEL)
    w_exp_up = nrm(ks[18], (DEPTH, N_EXPERTS, D_MODEL, D_EXPERT), D_MODEL)
    w_exp_down = nrm(ks[19], (DEPTH, N_EXPERTS, D_EXPERT, D_MODEL), D_EXPERT)
    final_norm_g = gain(ks[20], (D_MODEL,))
    return {
        "x": x, "positions": positions, "norm1_g": norm1_g, "w_in": w_in, "b_gate": b_gate,
        "conv_w": conv_w, "a_log": a_log, "dt_bias": dt_bias, "a_norm_g": a_norm_g,
        "w_proj_a": w_proj_a, "w_proj_b": w_proj_b, "w_out": w_out, "norm2_g": norm2_g,
        "w_router_group": w_router_group, "b_router_group": b_router_group,
        "w_router_expert": w_router_expert, "b_router_expert": b_router_expert,
        "w_exp_gate": w_exp_gate, "w_exp_up": w_exp_up, "w_exp_down": w_exp_down,
        "final_norm_g": final_norm_g,
    }

def first_block(x, positions, norm1_g, w_in, b_gate, conv_w, a_log, dt_bias, a_norm_g,
              w_proj_a, w_proj_b, w_out, norm2_g, w_router_group, b_router_group,
              w_router_expert, b_router_expert, w_exp_gate, w_exp_up, w_exp_down, final_norm_g):
    b, s, _ = x.shape
    for l in range(DEPTH):
        h = rmsnorm(x, norm1_g[l])
        parts = split_cols(h @ w_in[l])

        qkv = jnp.concatenate([parts["a_q"], parts["a_k"], parts["a_v"]], axis=-1)
        qkv = jax.nn.silu(causal_dwconv(qkv, conv_w[l]))
        aq = l2norm(qkv[..., :A_QK_W].reshape(b, s, A_HEADS, A_DK)) * (A_DK ** -0.5)
        ak = l2norm(qkv[..., A_QK_W:2 * A_QK_W].reshape(b, s, A_HEADS, A_DK))
        av = qkv[..., 2 * A_QK_W:].reshape(b, s, A_HEADS, A_DV).astype(jnp.float32)
        beta = jax.nn.sigmoid(parts["a_beta"].astype(jnp.float32))
        g = -jnp.exp(a_log[l].astype(jnp.float32)) * jax.nn.softplus(
            parts["a_alpha"].astype(jnp.float32) + dt_bias[l].astype(jnp.float32))
        o_a = gated_delta_rule(aq, ak, av, g, beta)
        o_a = rmsnorm(o_a, a_norm_g[l]) * jax.nn.silu(
            parts["a_z"].reshape(b, s, A_HEADS, A_DV).astype(jnp.float32))
        o_a = o_a.reshape(b, s, A_V_W).astype(x.dtype)

        bq = rope(parts["b_q"].reshape(b, s, B_HEADS, B_HD), positions)
        bk = rope(parts["b_k"].reshape(b, s, B_KV_HEADS, B_HD), positions)
        bv = parts["b_v"].reshape(b, s, B_KV_HEADS, B_HD)
        iq = rope(parts["i_q"].reshape(b, s, IDX_HEADS, IDX_HD), positions)
        ik = rope(parts["i_k"][:, :, None, :], positions)[:, :, 0, :]
        iw = parts["i_w"] * ((IDX_HEADS ** -0.5) * (IDX_HD ** -0.5))
        o_b = dsa_attention(bq, bk, bv, iq, ik, iw)

        gate_a = jax.nn.sigmoid(parts["gate_a"] + b_gate[l][:D_MODEL])
        gate_b = jax.nn.sigmoid(parts["gate_b"] + b_gate[l][D_MODEL:])
        merged = gate_a * (o_a @ w_proj_a[l]) + gate_b * (o_b @ w_proj_b[l])
        x = x + merged @ w_out[l]

        x = x + hier_moe(rmsnorm(x, norm2_g[l]), w_router_group[l], b_router_group[l],
                         w_router_expert[l], b_router_expert[l],
                         w_exp_gate[l], w_exp_up[l], w_exp_down[l])
    return rmsnorm(x, final_norm_g)


PLE_DIM = 256
HG_HEADS = 4
HG_DK = 128
HG_DV = 128
HG_KW = HG_HEADS * HG_DK
HG_VW = HG_HEADS * HG_DV
HG_CHUNK = 64
FOX_HEADS = 8
FOX_DH = 64
FOX_W = FOX_HEADS * FOX_DH
FOX_BLOCK = 128
D_FF = ((-(-8 * D_MODEL // 3) + 255) // 256) * 256

OFF_HG_Q = 0
OFF_HG_F = OFF_HG_Q + HG_KW
OFF_HG_I = OFF_HG_F + HG_KW
OFF_HG_G = OFF_HG_I + HG_VW
OFF_FOX_Q = OFF_HG_G + HG_VW
OFF_FOX_K = OFF_FOX_Q + FOX_W
OFF_FOX_V = OFF_FOX_K + FOX_W
OFF_FOX_F = OFF_FOX_V + FOX_W
OFF_GATE = OFF_FOX_F + FOX_HEADS
IN_COLS = OFF_GATE + 2 * D_MODEL


def rms_norm(x, g):
    xf = x.astype(jnp.float32)
    y = xf * lax.rsqrt(jnp.mean(xf * xf, axis=-1, keepdims=True) + EPS)
    return (y * g.astype(jnp.float32)).astype(x.dtype)

def hgrn2_mixer(q, f_logit, i, g, lb, o_gain):
    B, S, _ = q.shape
    f32 = jnp.float32
    qf = jax.nn.silu(q.astype(f32))
    fg = lb + (1.0 - lb) * jax.nn.sigmoid(f_logit.astype(f32))
    kf = 1.0 - fg
    logf = jnp.log(fg)
    vf = i.astype(f32)
    n = S // HG_CHUNK

    def to_chunks(t, d):
        return t.reshape(B, n, HG_CHUNK, HG_HEADS, d).transpose(1, 0, 3, 2, 4)

    qc = to_chunks(qf, HG_DK)
    kc = to_chunks(kf, HG_DK)
    vc = to_chunks(vf, HG_DV)
    bc = jnp.cumsum(to_chunks(logf, HG_DK), axis=3)
    causal = jnp.tril(jnp.ones((HG_CHUNK, HG_CHUNK), dtype=bool))[:, :, None]

    def step(state, xs):
        qt, kt, vt, bt = xs
        inter = jnp.einsum('bhtc,bhcv->bhtv', qt * jnp.exp(bt), state)
        diff = bt[:, :, :, None, :] - bt[:, :, None, :, :]
        decay = jnp.exp(jnp.where(causal, diff, -jnp.inf))
        scores = jnp.einsum('bhtc,bhsc,bhtsc->bhts', qt, kt, decay)
        intra = jnp.einsum('bhts,bhsv->bhtv', scores, vt)
        b_last = bt[:, :, -1:, :]
        new_state = (jnp.exp(b_last[:, :, 0, :])[..., None] * state
                     + jnp.einsum('bhsc,bhsv->bhcv', kt * jnp.exp(b_last - bt), vt))
        return new_state, inter + intra

    s0 = jnp.zeros((B, HG_HEADS, HG_DK, HG_DV), f32)
    _, o = lax.scan(step, s0, (qc, kc, vc, bc))
    o = o.transpose(1, 0, 3, 2, 4).reshape(B, S, HG_HEADS, HG_DV)
    o = rms_norm(o, o_gain).reshape(B, S, HG_VW)
    o = o * jax.nn.silu(g.astype(f32))
    return o.astype(q.dtype)

def forgetting_attention(q, k, v, f_logit, f_bias, q_gain, k_gain):
    B, S, _ = q.shape
    f32 = jnp.float32

    def heads(t):
        return t.reshape(B, S, FOX_HEADS, FOX_DH).transpose(0, 2, 1, 3)

    qh = rms_norm(heads(q), q_gain).astype(f32)
    kh = rms_norm(heads(k), k_gain).astype(f32)
    vh = heads(v)
    logf = jax.nn.log_sigmoid(f_logit.astype(f32) + f_bias.astype(f32))
    c = jnp.cumsum(logf, axis=1).transpose(0, 2, 1)
    scale = FOX_DH ** -0.5
    outs = []
    for blk in range(S // FOX_BLOCK):
        t0 = blk * FOX_BLOCK
        t1 = t0 + FOX_BLOCK
        s = jnp.einsum('bhtd,bhsd->bhts', qh[:, :, t0:t1], kh[:, :, :t1]) * scale
        s = s + c[:, :, t0:t1, None] - c[:, :, None, :t1]
        mask = (t0 + jnp.arange(FOX_BLOCK))[:, None] >= jnp.arange(t1)[None, :]
        s = jnp.where(mask, s, -jnp.inf)
        pr = jax.nn.softmax(s, axis=-1).astype(vh.dtype)
        outs.append(jnp.einsum('bhts,bhsd->bhtd', pr, vh[:, :, :t1]))
    o = jnp.concatenate(outs, axis=2)
    return o.transpose(0, 2, 1, 3).reshape(B, S, FOX_W)

def second_inputs(seed: int = 0) -> dict:
    key = jax.random.key(seed)
    ks = jax.random.split(key, 24)
    f32 = jnp.float32

    def w(k, shape, fan_in):
        return jax.random.normal(k, shape, f32) * (fan_in ** -0.5)

    def gain(k, shape):
        return 1.0 + 0.02 * jax.random.normal(k, shape, f32)

    return {
        "x": jax.random.normal(ks[0], (BATCH, SEQ, D_MODEL), f32),
        "p": jax.random.normal(ks[1], (DEPTH, BATCH, SEQ, PLE_DIM), f32),
        "norm_mix_g": gain(ks[2], (DEPTH, D_MODEL)),
        "w_in": w(ks[3], (DEPTH, D_MODEL, IN_COLS), D_MODEL),
        "hg_lb_logits": 0.1 * jax.random.normal(ks[4], (DEPTH + 1, HG_KW), f32),
        "hg_onorm_g": gain(ks[5], (DEPTH, HG_DV)),
        "fox_f_bias": jax.random.uniform(ks[6], (DEPTH, FOX_HEADS), f32, minval=1.0, maxval=4.0),
        "fox_q_norm_g": gain(ks[7], (DEPTH, FOX_DH)),
        "fox_k_norm_g": gain(ks[8], (DEPTH, FOX_DH)),
        "w_branch_a": w(ks[9], (DEPTH, HG_VW, D_MODEL), HG_VW),
        "w_branch_b": w(ks[10], (DEPTH, FOX_W, D_MODEL), FOX_W),
        "w_out": w(ks[11], (DEPTH, D_MODEL, D_MODEL), D_MODEL),
        "norm_ffn_g": gain(ks[12], (DEPTH, D_MODEL)),
        "w_ffn_gate": w(ks[13], (DEPTH, D_MODEL, D_FF), D_MODEL),
        "w_ffn_up": w(ks[14], (DEPTH, D_MODEL, D_FF), D_MODEL),
        "w_ffn_down": w(ks[15], (DEPTH, D_FF, D_MODEL), D_FF),
        "norm_ple_g": gain(ks[16], (DEPTH, D_MODEL)),
        "w_ple_gate": w(ks[17], (DEPTH, D_MODEL, D_MODEL), D_MODEL),
        "w_ple_proj": w(ks[18], (DEPTH, PLE_DIM, D_MODEL), PLE_DIM),
    }

def second_block(x, p, norm_mix_g, w_in, hg_lb_logits, hg_onorm_g, fox_f_bias, fox_q_norm_g,
              fox_k_norm_g, w_branch_a, w_branch_b, w_out, norm_ffn_g, w_ffn_gate, w_ffn_up,
              w_ffn_down, norm_ple_g, w_ple_gate, w_ple_proj):
    lower_bounds = jnp.cumsum(jax.nn.softmax(hg_lb_logits.astype(jnp.float32), axis=0), axis=0)
    for layer in range(DEPTH):
        h = rms_norm(x, norm_mix_g[layer])
        z = h @ w_in[layer]
        y_a = hgrn2_mixer(z[..., OFF_HG_Q:OFF_HG_F], z[..., OFF_HG_F:OFF_HG_I],
                          z[..., OFF_HG_I:OFF_HG_G], z[..., OFF_HG_G:OFF_FOX_Q],
                          lower_bounds[layer], hg_onorm_g[layer])
        y_b = forgetting_attention(z[..., OFF_FOX_Q:OFF_FOX_K], z[..., OFF_FOX_K:OFF_FOX_V],
                                   z[..., OFF_FOX_V:OFF_FOX_F], z[..., OFF_FOX_F:OFF_GATE],
                                   fox_f_bias[layer], fox_q_norm_g[layer], fox_k_norm_g[layer])
        gate_a = jax.nn.sigmoid(z[..., OFF_GATE:OFF_GATE + D_MODEL])
        gate_b = jax.nn.sigmoid(z[..., OFF_GATE + D_MODEL:IN_COLS])
        merged = gate_a * (y_a @ w_branch_a[layer]) + gate_b * (y_b @ w_branch_b[layer])
        x = x + merged @ w_out[layer]
        hf = rms_norm(x, norm_ffn_g[layer])
        x = x + (jax.nn.silu(hf @ w_ffn_gate[layer]) * (hf @ w_ffn_up[layer])) @ w_ffn_down[layer]
        hp = rms_norm(x, norm_ple_g[layer])
        x = x + jax.nn.sigmoid(hp @ w_ple_gate[layer]) * (p[layer] @ w_ple_proj[layer])
    return x


def setup_inputs(seed=0):
    out = dict(first_inputs(seed))
    for name, value in second_inputs(seed + 1).items():
        if name != "x":
            out[name + "_2"] = value
    return out


def reference(
    x, positions, norm1_g, w_in, b_gate, conv_w, a_log, dt_bias, a_norm_g, w_proj_a, w_proj_b,
    w_out, norm2_g, w_router_group, b_router_group, w_router_expert, b_router_expert,
    w_exp_gate, w_exp_up, w_exp_down, final_norm_g, p_2, norm_mix_g_2, w_in_2, hg_lb_logits_2,
    hg_onorm_g_2, fox_f_bias_2, fox_q_norm_g_2, fox_k_norm_g_2, w_branch_a_2, w_branch_b_2,
    w_out_2, norm_ffn_g_2, w_ffn_gate_2, w_ffn_up_2, w_ffn_down_2, norm_ple_g_2, w_ple_gate_2,
    w_ple_proj_2,
):
    x = first_block(
        x, positions, norm1_g, w_in, b_gate, conv_w, a_log, dt_bias, a_norm_g, w_proj_a,
        w_proj_b, w_out, norm2_g, w_router_group, b_router_group, w_router_expert,
        b_router_expert, w_exp_gate, w_exp_up, w_exp_down, final_norm_g,
    )
    return second_block(
        x, p_2, norm_mix_g_2, w_in_2, hg_lb_logits_2, hg_onorm_g_2, fox_f_bias_2,
        fox_q_norm_g_2, fox_k_norm_g_2, w_branch_a_2, w_branch_b_2, w_out_2, norm_ffn_g_2,
        w_ffn_gate_2, w_ffn_up_2, w_ffn_down_2, norm_ple_g_2, w_ple_gate_2, w_ple_proj_2,
    )


_drawn_inputs = setup_inputs


def setup_inputs(seed=0):
    import zlib

    import numpy as np

    out = dict(_drawn_inputs(seed))
    spreads = {}
    factors = {'b_gate': 7.952,
     'a_norm_g': 3.815,
     'norm2_g': 2.89,
     'b_router_expert': 4.98,
     'norm_mix_g_2': 5.257,
     'hg_lb_logits_2': 8.0,
     'hg_onorm_g_2': 8.0,
     'fox_q_norm_g_2': 8.0,
     'fox_k_norm_g_2': 8.0,
     'norm_ffn_g_2': 15.409,
     'norm_ple_g_2': 200.0,
     'w_ple_gate_2': 23.808,
     'p_2': 8.0,
     'w_ple_proj_2': 8.0}
    for name, (base, spread) in spreads.items():
        noise = np.random.default_rng([zlib.crc32(name.encode()), seed]).standard_normal(out[name].shape)
        drawn = base * np.exp(spread * noise) if base else spread * noise
        out[name] = jnp.asarray(drawn.astype(out[name].dtype))
    for name, factor in factors.items():
        out[name] = (out[name] * factor).astype(out[name].dtype)
    return out
```

```python
from contextlib import ExitStack

import concourse.bass as bass
from concourse import mybir

F32 = mybir.dt.float32
F32R = mybir.dt.float32r
BF16 = mybir.dt.bfloat16
I32 = mybir.dt.int32
ALU = mybir.AluOpType
ACT = mybir.ActivationFunctionType
X = mybir.AxisListType.X

P = 128
S = 256
NT = S // P
DM = 1024
KD = DM // P
EPS = 1e-6
BIG = 1e30
TAKEN = -3e38

A_W = 512
CONV_W = 3 * A_W
TOK0 = CONV_W
Z_Z, Z_BETA, Z_ALPHA, Z_BQ, Z_BV, Z_IQ, Z_IW, TOK_W = 0, 512, 520, 528, 1168, 1296, 1872, 1880
GATE0 = TOK0 + TOK_W
TOK_BLK = 470
N_TOK_BLK = TOK_W // TOK_BLK
HEADS, HD = 8, 64
KV_HEADS = 2
TOPK = 64
CHUNK = 64
N_GROUPS, PER_GROUP, D_EXP = 4, 4, 256
N_EXP = N_GROUPS * PER_GROUP
HG_HEADS, HG_D = 4, 128
TOK0_2 = 1024
TOK_W2 = 2568
Z2_I, Z2_G, Z2_Q, Z2_K, Z2_V, Z2_F = 0, 512, 1024, 1536, 2048, 2560
GATE0_2 = TOK0_2 + TOK_W2
D_FF = 2816
FF_PAIRS = D_FF // 256
PLE = 256

CH = 2048
RAW = 4
SPL = 3
LEVELS = [1, 2, 4, 8, 16, 32, 64]

R_N1, R_N2, R_NMIX, R_NFFN, R_NPLE, R_BG, R_CONV, R_LB, R_ALL = 0, 8, 16, 24, 32, 40, 56, 104, 112
C_FIN, C_ALOG, C_DT, C_ANORM, C_RB, C_ONORM, C_FB, C_QN, C_KN, C_ALL = (
    0, 1024, 1032, 1040, 1104, 1124, 1252, 1260, 1324, 1388)


def two_block_program(nc, x, positions, norm1_g, w_in, b_gate, conv_w, a_log, dt_bias, a_norm_g,
                      w_proj_a, w_proj_b, w_out, norm2_g, w_router_group, b_router_group,
                      w_router_expert, b_router_expert, w_exp_gate, w_exp_up, w_exp_down,
                      final_norm_g, p_2, norm_mix_g_2, w_in_2, hg_lb_logits_2, hg_onorm_g_2,
                      fox_f_bias_2, fox_q_norm_g_2, fox_k_norm_g_2, w_branch_a_2, w_branch_b_2,
                      w_out_2, norm_ffn_g_2, w_ffn_gate_2, w_ffn_up_2, w_ffn_down_2,
                      norm_ple_g_2, w_ple_gate_2, w_ple_proj_2, rope_freq, out, dbg=None):
    ctx = ExitStack()
    with ctx:
        def sb(name, shape, dt=F32):
            return ctx.enter_context(nc.sbuf_tensor(name, shape, dt))

        def sem(name):
            return ctx.enter_context(nc.semaphore(name))

        chunks = []

        def rows_by(w, cols):
            return w[:, cols].rearrange("(k p) n -> p k n", p=P)

        def half_rows(w, half, cols):
            return w[half * 512:(half + 1) * 512, cols].rearrange("(k p) n -> p k n", p=P)

        def add(src):
            chunks.append((src, src.shape[1], src.shape[2]))
            return len(chunks) - 1

        wi, wi2 = w_in[0], w_in_2[0]
        CONV = [add(rows_by(wi, slice(256 * c, 256 * c + 256))) for c in range(6)]
        TOK = [[add(half_rows(wi, k, slice(TOK0 + TOK_BLK * b, TOK0 + TOK_BLK * (b + 1))))
                for k in range(2)] for b in range(N_TOK_BLK)]
        GATE = [add(rows_by(wi, slice(GATE0 + 256 * c, GATE0 + 256 * c + 256))) for c in range(8)]
        PROJ = [[add(rows_by(w[0], slice(512 * c, 512 * c + 512))) for w in (w_proj_a, w_proj_b)]
                for c in range(2)]
        OUT = [[add(half_rows(w_out[0], k, slice(512 * c, 512 * c + 512))) for k in range(2)]
               for c in range(2)]
        EXP = [[None] * 3 for _ in range(N_EXP)]
        for e in range(N_EXP + 1):
            if e < N_EXP:
                EXP[e][0] = add(w_exp_gate[0, e].rearrange("(k p) n -> p k n", p=P))
                EXP[e][1] = add(w_exp_up[0, e].rearrange("(k p) n -> p k n", p=P))
            if e >= 1:
                EXP[e - 1][2] = add(w_exp_down[0, e - 1].rearrange("(k p) n -> p k n", p=P))
        HGQF = [add(rows_by(wi2, slice(256 * c, 256 * c + 256))) for c in range(4)]
        TOK2 = [[add(half_rows(wi2, k, slice(TOK0_2 + 512 * b, TOK0_2 + 512 * (b + 1))))
                 for k in range(2)] for b in range(5)]
        GATE2 = [add(rows_by(wi2, slice(GATE0_2 + 256 * c, GATE0_2 + 256 * c + 256)))
                 for c in range(8)]
        PROJ2 = [[add(rows_by(w[0], slice(512 * c, 512 * c + 512)))
                  for w in (w_branch_a_2, w_branch_b_2)] for c in range(2)]
        OUT2 = [[add(half_rows(w_out_2[0], k, slice(512 * c, 512 * c + 512))) for k in range(2)]
                for c in range(2)]
        FFN = [[None] * 3 for _ in range(FF_PAIRS)]
        for e in range(FF_PAIRS + 1):
            if e < FF_PAIRS:
                FFN[e][0] = add(rows_by(w_ffn_gate_2[0], slice(256 * e, 256 * e + 256)))
                FFN[e][1] = add(rows_by(w_ffn_up_2[0], slice(256 * e, 256 * e + 256)))
            if e >= 1:
                FFN[e - 1][2] = add(w_ffn_down_2[0, 256 * (e - 1):256 * e, :]
                                    .rearrange("(k p) n -> p k n", p=P))
        PLEG = [[add(half_rows(w_ple_gate_2[0], k, slice(512 * c, 512 * c + 512)))
                 for k in range(2)] for c in range(2)]
        PLEP = add(rows_by(w_ple_proj_2[0], slice(0, DM)))
        N_CH = len(chunks)

        raw = sb("raw", [P, RAW, CH])
        w_hi = sb("w_hi", [P, SPL, CH], F32R)
        w_lo = sb("w_lo", [P, SPL, CH], F32R)
        x_tok = sb("x_tok", [P, NT, DM])
        h_hi = sb("h_hi", [P, KD, S], F32R)
        h_lo = sb("h_lo", [P, KD, S], F32R)
        o_hi = sb("o_hi", [P, 8, S], F32R)
        o_lo = sb("o_lo", [P, 8, S], F32R)
        rt_hi = sb("rt_hi", [P, KD, 28], F32R)
        rt_lo = sb("rt_lo", [P, KD, 28], F32R)
        rt_raw = sb("rt_raw", [P, KD, 28])
        ident = sb("ident", [P, P])
        upto = sb("upto", [P, P])
        after = sb("after", [P, P])
        ones = sb("ones", [P, P])
        ident_bf = sb("ident_bf", [P, P], BF16)
        future_bf = sb("future_bf", [P, P], BF16)
        lvl = sb("lvl", [P, len(LEVELS), P])
        rows = sb("rows", [R_ALL, P])
        chan = sb("chan", [P, R_ALL])
        rep_row = sb("rep_row", [1, C_ALL])
        rep = sb("rep", [P, C_ALL])
        pos_i = sb("pos_i", [P, NT], I32)
        pos_f = sb("pos_f", [P, NT])
        freq_row = sb("freq_row", [1, 32])
        cs = sb("cs", [P, 2, NT, 32])
        small = sb("small", [P, 640])
        arena = sb("arena", [P, 18900])
        ps = ctx.enter_context(nc.psum_tensor("ps", [P, 8 * 512], F32))

        def bank(b, n=1):
            return ps[:, 512 * b:512 * (b + n)]

        def view(off, *shape):
            n = 1
            for s in shape:
                n *= s
            v = arena[:, off:off + n]
            if len(shape) == 2:
                v = v.rearrange("p (a b) -> p a b", a=shape[0])
            if len(shape) == 3:
                v = v.rearrange("p (a b c) -> p a b c", a=shape[0], b=shape[1])
            if len(shape) == 4:
                v = v.rearrange("p (a b c d) -> p a b c d", a=shape[0], b=shape[1], c=shape[2])
            return v

        def mid(ap, n):
            return ap.unsqueeze(1).broadcast_to([ap.shape[0], n, ap.shape[1]])

        def last(ap, n):
            return ap.unsqueeze(len(ap.shape)).broadcast_to(list(ap.shape) + [n])

        def split3(ap, a):
            return ap.rearrange("p (a b) -> p a b", a=a)

        def split4(ap, a, b):
            return ap.rearrange("p (a b c) -> p a b c", a=a, b=b)

        xn = view(0, NT, DM)
        junk = view(2048, NT, DM)
        z_tok = view(0, NT, TOK_W)
        z_t = view(3760, 12, S + 3)
        y_t = view(6868, 12, S)
        qkv = view(9940, NT, CONV_W)
        q_t, k_t, kb_t = view(6868, 4, S), view(7892, 4, S), view(8916, 4, S)
        v_b, k_b, kb_g, k_dec = view(3760, NT, 512), view(4784, NT, 512), view(5808, 512), view(6320, 512)
        q_dec, q_dec_t = view(13012, 512), view(13524, 4, P)
        g_mask, dec, a_t = view(9940, NT, 4, P), view(10964, NT, 4, P), view(11988, NT, 4, P)
        lev, w_t = view(9940, NT, 4, P), view(9940, 2, P)
        inv, inv_t, prod, qk_t = (view(14036 + 1024 * n, NT, 4, P) for n in range(4))
        v_new, o_tok = view(16084, NT, 512), view(4784, NT, 512)
        state = view(18132, 2, HD)
        sq = view(14036, NT, DM)
        roped = view(3760, NT, 19, HD)
        k_dup, ik_dup = view(6192, NT, 2, 2, HD), view(6704, NT, 2, HD)
        ro_t = view(6960, 11, S)
        score, work = view(9776, NT, S), view(10288, NT, S)
        prob = view(10800, NT, HEADS, S)
        rel = view(10800, NT, HEADS, S)
        prob_t = view(14896, 24, P)
        rt1, rt2 = view(14896, NT, 19, 32), view(16112, NT, 19, 32)
        gate = view(0, 16, S)
        ga, gb = view(4096, 4, S), view(5120, 4, S)
        comb_rep = view(0, N_EXP, S)
        act_s = view(4096, 2, 2, S)
        act_p = view(5120, 2, 2, S)
        comb_t = view(6200, S)
        sel_e = view(6500, N_EXP, P)
        z2 = view(0, NT, TOK_W2)
        hq, hk, hb, hd, he = (view(5136 + 1024 * n, 8, P) for n in range(5))
        hx = view(10256, 2, 8, P)
        hsc = view(12304, 8, P)
        hqb, hkd, hkd_t, hs0 = (view(13328 + 512 * n, 4, P) for n in range(4))
        ho, hsq = view(15376, NT, 512), view(16400, NT, 512)
        fsq = view(17424, 1024)
        qk2_t = view(5136, 8, S)
        f_mask = view(7184, NT, HEADS, P)
        prob2 = view(9232, NT, HEADS, S)
        prob2_t = view(13328, 24, P)
        p_tok = view(8192, NT, PLE)
        res = view(4096, NT, DM)

        ssq, rms, rstd = small[:, 0:2], small[:, 2:4], small[:, 4:6]
        sp1, sp2, sp3 = split3(small[:, 16:32], 2), split3(small[:, 32:48], 2), split3(small[:, 48:64], 2)
        beta, glog = split3(small[:, 64:80], 2), split3(small[:, 80:96], 2)
        e_g, e_gl = split3(small[:, 96:112], 2), split3(small[:, 112:128], 2)
        nrm = split3(small[:, 128:160], 2)
        mx, nmx, den, rden = (split3(small[:, 160 + 16 * n:176 + 16 * n], 2) for n in range(4))
        top8 = small[:, 224:232]
        iw = split3(small[:, 232:248], 2)
        rl = split3(small[:, 248:288], 2)
        ga1, ga2 = split3(small[:, 288:296], 2), split3(small[:, 296:304], 2)
        gs1, gs2, gs3 = small[:, 304:306], small[:, 306:308], small[:, 308:310]
        el, e1h, e2h, ea = (split3(small[:, 312 + 8 * n:320 + 8 * n], 2) for n in range(4))
        tie = small[:, 344:348]
        comb = split3(small[:, 352:384], 2)
        lb, lbc, lbt = small[:, 384:388], small[:, 388:392], small[:, 392:396]
        alog = small[:, 396:404]
        sp4 = split3(small[:, 408:424], 2)
        ttmp = split4(small[:, 424:456], 2, 4)
        turns = split3(small[:, 512:576], 2)
        over = split3(small[:, 576:640], 2)
        top8b = small[:, 464:472]

        w_in_sem = [sem(f"chunk_loaded_{i}") for i in range(RAW)]
        w_high, w_ready, w_used = sem("w_high"), sem("w_ready"), sem("w_used")
        s_x, s_rows, s_rep, s_pos, s_rt = sem("x_loaded"), sem("rows_loaded"), sem("rep_loaded"), sem("pos_loaded"), sem("router_loaded")
        s_p = sem("p_loaded")
        s_pool, s_const = sem("pool_step"), sem("constants_ready")
        s_act, s_dve = sem("act_step"), sem("dve_step")
        s_chan_ps, s_chan = sem("channel_vectors_in_psum"), sem("channel_vectors_ready")
        s_rep_ps = sem("repeated_vectors_in_psum")
        s_rt_hi, s_rt_lo = sem("router_high"), sem("router_split")
        s_sq, s_ms, s_rt_n, s_xn, s_xt, s_hhi, s_h = (sem(n) for n in (
            "squares_summed", "mean_square", "root", "x_normed", "x_transposed", "h_high", "h_ready"))

        (s_conv_ev, s_tap, s_conv, s_silu_y, s_tok_ps, s_tok_ev, s_yt, s_qkv, s_beta, s_spe,
         s_spx, s_spl, s_spm, s_glog, s_gsum, s_eg, s_l2s, s_l2r, s_qn, s_heads_ps, s_heads,
         s_gmask, s_dps, s_dexp, s_kkqk, s_at, s_inv0, s_inv0_ps, s_inv0_ev, s_lev,          s_prod_ps, s_prod, s_dinv, s_inv, s_wt_ps, s_wt, s_u0, s_v0, s_st_ps, s_st, s_u1, s_v1,
         s_o_ps, s_o, s_ors, s_orr, s_zs, s_on, s_ot_ps, s_ohi, s_o_ready) = (sem(n) for n in (
            "conv_in_sbuf", "tap_step", "taps_done", "conv_silu_done", "tok_in_psum",
            "tok_in_sbuf", "conv_transposed", "qkv_ready", "beta_ready", "softplus_arg",
            "softplus_exp", "softplus_arg2", "softplus_ln", "log_decay_ready", "decay_sums_in_psum",
            "decay_exps_ready", "head_squares", "head_roots", "heads_normed", "head_tiles_in_psum",
            "head_tiles_ready", "decay_operand_ready", "decay_in_psum", "decay_exp_done",
            "scores_in_psum", "scores_ready", "inverse_start", "inverse_start_in_psum",
            "inverse_start_turned", "level_ready", "product_in_psum",
            "product_ready", "correction_in_psum", "inverse_updated", "w_in_psum", "w_turned",
            "u0_in_psum", "v0_ready", "state_in_psum", "state_ready", "v1_in_psum", "v1_ready",
            "delta_out_in_psum", "delta_out_ready", "out_squares", "out_roots", "z_silu_ready",
            "out_normed", "out_transposed", "out_high", "out_ready"))
        (s_trig, s_sin, s_roped, s_ro_ps, s_ro, s_rel_ps, s_rel, s_log_ps, s_msk, s_nmx, s_exp,
         s_prob, s_pt_ps, s_pt, s_pv_ps, s_pv_hi, s_bout) = (sem(n) for n in (
            "angles_ready", "trig_ready", "roped", "rope_turned", "rope_tiles_ready",
            "index_scores_in_psum", "index_relu_ready", "logits_in_psum", "logits_masked",
            "row_max_ready", "exp_ready", "prob_ready", "prob_turned", "prob_tiles_ready",
            "attention_in_psum", "attention_high", "attention_ready"))
        (s_gate, s_merge, s_merge_hi, s_merged, s_x_ready,
         s_rl_ps, s_rlm, s_rle, s_comb, s_ct_ps, s_ct, s_cr_ps, s_cr, s_sel, s_silu, s_prod2,
         s_ahi, s_a, ) = (sem(n) for n in (
            "gate_ready", "merge_ready", "merge_high",
            "merged_ready", "x_ready", "router_in_psum", "router_shifted",
            "router_exps", "comb_ready", "comb_turned", "comb_rows_ready", "comb_rep_in_psum",
            "comb_rep_ready", "selectors_ready", "silu_ready", "product2_ready",
            "act_high", "act_ready", ))
        (s_hev, s_lbe, s_lbs, s_fg, s_logf, s_hd, s_he, s_hx, s_hsc_ps, s_hsc, s_hio, s_hie,
         s_hkd, s_hkt_ps, s_hkt, s_hs_ps, s_hs, s_ho_ps, s_ho) = (sem(n) for n in (
            "hg_in_sbuf", "lb_shifted", "lb_exps", "forget_ready", "log_forget_ready",
            "level_distance", "level_decay", "level_operand", "level_scores_in_psum",
            "level_scores_taken", "edge_distance", "edge_decay", "edge_operands", "kd_turned",
            "kd_ready", "hg_state_in_psum", "hg_state_ready", "hg_out_in_psum", "hg_out_ready"))
        (s_fq_ps, s_fq, s_fmask, s_fl_ps, s_p_ps, s_p_hi, s_p_ready, s_plg,          s_result, s_out) = (sem(n) for n in (
            "fox_heads_in_psum", "fox_heads_ready", "forget_operand", "fox_logits_in_psum",
            "p_turned", "p_high", "p_ready", "ple_gate_ready",
            "result_ready", "result_stored"))

        def by_keys(j):
            if j < 2:
                return 0, slice(j, 8, 2)
            h0 = (j - 2) % 2 + 4 * ((j - 2) // 2)
            return 1, slice(h0, h0 + 3, 2)

        def heads_of(j):
            return list(range(8))[by_keys(j)[1]]

        def key_bank(t, h):
            return (h % 2, h // 2) if t == 0 else (2 + h % 2 + 2 * (h // 4), (h % 4) // 2)

        block = ctx.enter_context(nc.Block())

        @block.sync
        def _(sp):
            sp.dma_start(x_tok[:, :, :], x[0].rearrange("(t p) d -> p t d", p=P)).then_inc(s_x, 16)
            for i, (src, kt, n) in enumerate(chunks):
                slot = i % RAW
                if i >= RAW:
                    sp.wait_ge(w_ready, i - RAW + 1)
                dst = raw[:, slot, 0:kt * n].rearrange("p (k n) -> p k n", k=kt)
                sp.dma_start(dst, src).then_inc(w_in_sem[slot], 16)
            sp.wait_ge(s_result, 2)
            sp.dma_start(out[0].rearrange("(t p) d -> p t d", p=P), res).then_inc(s_out, 16)
            sp.wait_ge(s_out, 16)

        @block.gpsimd
        def _(pool):
            n_pool = [0]

            def step(ins):
                n_pool[0] += 1
                ins.then_inc(s_pool, 1)
                pool.wait_ge(s_pool, n_pool[0])

            step(pool.memset(ident[:, :], 0.0))
            step(pool.affine_select(out=ident[:, :], in_=ident[:, :], compare_op=ALU.not_equal,
                                    fill=1.0, base=0, pattern=[[-1, P]], channel_multiplier=1))
            pool.tensor_copy(ident_bf[:, :], ident[:, :]).then_inc(s_const, 1)
            step(pool.memset(ones[:, :], 1.0))
            pool.affine_select(out=upto[:, :], in_=ones[:, :], compare_op=ALU.is_ge, fill=0.0,
                               base=0, pattern=[[1, P]], channel_multiplier=-1).then_inc(s_const, 1)
            pool.affine_select(out=after[:, :], in_=ones[:, :], compare_op=ALU.is_gt, fill=0.0,
                               base=0, pattern=[[-1, P]], channel_multiplier=1).then_inc(s_const, 1)
            step(pool.memset(future_bf[:, :], 0.0))
            pool.affine_select(out=future_bf[:, :], in_=future_bf[:, :], compare_op=ALU.is_ge,
                               fill=-BIG, base=0, pattern=[[-1, P]],
                               channel_multiplier=1).then_inc(s_const, 1)
            for n, s in enumerate(LEVELS):
                blocks = P // (2 * s)
                m = lvl[:, n, :].rearrange("p (b h r) -> p b h r", b=blocks, h=2)
                pool.memset(m[:, :, 0, :], 0.0)
                step(pool.memset(m[:, :, 1, :], 1.0))
                step(pool.affine_select(out=lvl[:, n, :], in_=lvl[:, n, :], compare_op=ALU.is_ge,
                                        fill=0.0, base=0, pattern=[[-2 * s, blocks], [0, 2 * s]],
                                        channel_multiplier=1))
                pool.affine_select(out=lvl[:, n, :], in_=lvl[:, n, :], compare_op=ALU.is_ge,
                                   fill=0.0, base=s - 1, pattern=[[2 * s, blocks], [0, 2 * s]],
                                   channel_multiplier=-1).then_inc(s_const, 1)
            for gr in range(2):
                pool.wait_ge(s_at, gr + 1)
                for n in range(1, len(LEVELS)):
                    if n >= 2:
                        pool.wait_ge(s_prod_ps, 2 * (6 * gr + n - 1))
                    for t in range(NT):
                        pool.tensor_tensor(lev[:, t], a_t[:, t], mid(lvl[:, n, :], 4),
                                           ALU.mult).then_inc(s_lev, 1)
            pool.wait_ge(s_x_ready, 1)
            step(pool.memset(sel_e[0:16], 0.0))
            pool.affine_select(out=sel_e[0:16], in_=sel_e[0:16], compare_op=ALU.not_equal,
                               fill=1.0, base=0, pattern=[[-1, N_EXP], [0, P]],
                               channel_multiplier=1).then_inc(s_sel, 1)

        @block.scalar
        def _(act):
            n_act, split_at = [0], [0]

            def step(ins):
                n_act[0] += 1
                ins.then_inc(s_act, 1)
                act.wait_ge(s_act, n_act[0])

            def ahead(i):
                while split_at[0] <= min(i + SPL - 1, N_CH - 1):
                    j = split_at[0]
                    _, kt, n = chunks[j]
                    act.wait_ge(w_in_sem[j % RAW], 16 * (j // RAW + 1))
                    if j >= SPL:
                        act.wait_ge(w_used, j - SPL + 1)
                    act.activation(w_hi[:, j % SPL, 0:kt * n], raw[:, j % RAW, 0:kt * n],
                                   ACT.Copy).then_inc(w_high, 1)
                    split_at[0] += 1

            def norm(n, turn, row):
                if n == 0:
                    act.wait_ge(s_x, 16)
                else:
                    act.wait_ge(s_x_ready, n)
                for t in range(NT):
                    act.activation(junk[:, t], x_tok[:, t], ACT.Square,
                                   accum_out=ssq[:, t:t + 1]).then_inc(s_sq, 1)
                act.wait_ge(s_ms, n + 1)
                act.activation(rms, rms, ACT.Sqrt).then_inc(s_rt_n, 1)
                if turn is None:
                    return
                if n == 0:
                    act.wait_ge(s_chan, 1)
                for b in range(4):
                    act.wait_ge(s_xt, 4 * turn + b + 1)
                    for k in (2 * b, 2 * b + 1):
                        act.activation(h_hi[:, k, :], split3(bank(b), 2)[:, k % 2, :], ACT.Copy,
                                       scale=chan[:, row + k:row + k + 1]).then_inc(s_hhi, 1)

            for r, v in ((R_N1, norm1_g), (R_N2, norm2_g), (R_NMIX, norm_mix_g_2),
                         (R_NFFN, norm_ffn_g_2), (R_NPLE, norm_ple_g_2), (R_BG, b_gate)):
                n = v.shape[1] // P
                act.dma_start(rows[r:r + n, :], v[0].rearrange("(r p) -> r p", p=P)).then_inc(s_rows, 16)
            act.dma_start(rows[R_CONV:R_CONV + 48, :],
                          conv_w[0].rearrange("k (c p) -> (k c) p", p=P)).then_inc(s_rows, 16)
            act.dma_start(rows[R_LB:R_LB + 8, :],
                          hg_lb_logits_2.rearrange("k (c p) -> (k c) p", p=P)).then_inc(s_rows, 16)
            for c, v in ((C_FIN, final_norm_g.unsqueeze(0)), (C_ALOG, a_log), (C_DT, dt_bias),
                         (C_ANORM, a_norm_g), (C_RB, b_router_group), (C_RB + 4, b_router_expert),
                         (C_ONORM, hg_onorm_g_2), (C_FB, fox_f_bias_2), (C_QN, fox_q_norm_g_2),
                         (C_KN, fox_k_norm_g_2)):
                act.dma_start(rep_row[0:1, c:c + v.shape[1]], v).then_inc(s_rep, 16)
            act.dma_start(freq_row[0:1, :], rope_freq).then_inc(s_rep, 16)
            with nc.allow_non_contiguous_dma("256 positions, one word each"):
                act.dma_start(pos_i[:, :], positions[0].rearrange("(t p) -> p t", p=P)).then_inc(s_pos, 16)
            act.dma_start(rt_raw[:, :, 0:4], w_router_group[0].rearrange("(k p) n -> p k n", p=P)).then_inc(s_rt, 16)
            act.dma_start(rt_raw[:, :, 4:20], w_router_expert[0].rearrange("(k p) n -> p k n", p=P)).then_inc(s_rt, 16)
            act.dma_start(rt_raw[:, :, 20:28],
                          wi2[:, TOK0_2 + Z2_F:GATE0_2].rearrange("(k p) n -> p k n", p=P)).then_inc(s_rt, 16)

            norm(0, 0, R_N1)
            ahead(0)
            act.wait_ge(s_trig, 1)
            act.activation(cs[:, :, :, :], cs[:, :, :, :], ACT.Sin).then_inc(s_sin, 1)

            def conv_silu(c):
                act.wait_ge(s_conv, c + 1)
                act.activation(y_t[:, 2 * c:2 * c + 2, :], y_t[:, 2 * c:2 * c + 2, :],
                               ACT.Silu).then_inc(s_silu_y, 1)

            for c in range(6):
                ahead(CONV[c])
                act.wait_ge(w_used, CONV[c] + 1)
                act.activation(z_t[:, 2 * c:2 * c + 2, 3:S + 3], split3(bank(c % 4), 2),
                               ACT.Copy).then_inc(s_conv_ev, 1)
                if c:
                    conv_silu(c - 1)
            conv_silu(5)
            for b in range(N_TOK_BLK):
                ahead(TOK[b][0])
                ahead(TOK[b][1])
                act.wait_ge(w_used, TOK[b][1] + 1)
                act.activation(z_tok[:, :, TOK_BLK * b:TOK_BLK * (b + 1)],
                               split3(bank(4 + 2 * (b % 2), 2), 2)[:, :, 0:TOK_BLK],
                               ACT.Copy).then_inc(s_tok_ev, 1)

            act.wait_ge(s_rt, 48)
            act.activation(rt_hi[:, :, :], rt_raw[:, :, :], ACT.Copy).then_inc(s_rt_hi, 1)
            for j in range(6):
                act.wait_ge(s_yt, j + 1)
                t, g = j // 3, j % 3
                act.activation(qkv[:, t, 512 * g:512 * g + 512], bank(j), ACT.Copy).then_inc(s_qkv, 1)
            act.activation(beta, z_tok[:, :, Z_BETA:Z_BETA + 8], ACT.Sigmoid).then_inc(s_beta, 1)
            act.activation(z_tok[:, :, Z_Z:Z_Z + 512], z_tok[:, :, Z_Z:Z_Z + 512],
                           ACT.Silu).then_inc(s_zs, 1)

            def softplus(n):
                act.wait_ge(s_spe, n + 1)
                act.activation(sp2, sp2, ACT.Exp).then_inc(s_spx, 1)
                act.wait_ge(s_spl, n + 1)
                act.activation(sp3, sp3, ACT.Ln).then_inc(s_spm, 1)

            softplus(0)
            act.activation(alog, rep[:, C_ALOG:C_ALOG + 8], ACT.Exp).then_inc(s_spm, 1)
            act.wait_ge(s_l2s, 1)
            act.activation(nrm, nrm, ACT.Sqrt).then_inc(s_l2r, 1)
            act.wait_ge(s_gsum, 1)
            act.activation(small[:, 96:128], bank(6)[:, 0:32], ACT.Exp).then_inc(s_eg, 1)

            def turned(dst, n, first_bank, sig, done):
                for j in range(n):
                    act.wait_ge(sig, j + 1)
                    act.activation(dst(j), bank(first_bank(j)), ACT.Copy).then_inc(done, 1)

            def head_tile(j):
                if j == 6:
                    return q_dec_t.rearrange("p a b -> p (a b)")
                return (q_t, k_t, kb_t)[j // 2][:, 2 * (j % 2):2 * (j % 2) + 2, :].rearrange("p a b -> p (a b)")
            turned(head_tile, 7, lambda j: j, s_heads_ps, s_heads)

            for gr in range(2):
                for t in range(NT):
                    act.wait_ge(s_dps, 2 * gr + t + 1)
                    act.activation(dec[:, t].rearrange("p a b -> p (a b)"), bank(t),
                                   ACT.Exp).then_inc(s_dexp, 1)
                for t in range(NT):
                    act.wait_ge(s_inv0_ps, 2 * gr + t + 1)
                    act.activation(inv[:, t].rearrange("p a b -> p (a b)"), bank(t),
                                   ACT.Copy).then_inc(s_inv0_ev, 1)
                for n in range(1, len(LEVELS)):
                    for t in range(NT):
                        act.wait_ge(s_prod_ps, 12 * gr + 2 * (n - 1) + t + 1)
                        if n >= 2 or gr:
                            act.wait_ge(s_dinv, 12 * gr + 2 * (n - 2) + t + 1)
                        act.activation(prod[:, t].rearrange("p a b -> p (a b)"), bank(2 + t),
                                       ACT.Copy).then_inc(s_prod, 1)
                act.wait_ge(s_wt_ps, gr + 1)
                act.activation(w_t.rearrange("p a b -> p (a b)"), bank(2)[:, 0:256], ACT.Copy,
                               scale=-1.0).then_inc(s_wt, 1)
                act.wait_ge(s_u0, gr + 1)
                act.activation(v_new[:, 0, 256 * gr:256 * gr + 256], bank(0)[:, 0:256],
                               ACT.Copy).then_inc(s_v0, 1)
                act.wait_ge(s_st_ps, gr + 1)
                act.activation(state.rearrange("p a b -> p (a b)"), bank(3)[:, 0:128],
                               ACT.Copy).then_inc(s_st, 1)
                act.wait_ge(s_u1, gr + 1)
                for odd, b in ((0, 1), (1, 6)):
                    dst = v_new[:, 1, 256 * gr:256 * gr + 256].rearrange("p (a b d) -> p a b d", a=2, b=2)
                    act.activation(dst[:, :, odd, :], split3(bank(b)[:, 0:128], 2), ACT.Copy).then_inc(s_v1, 1)
                act.wait_ge(s_o_ps, gr + 1)
                act.activation(o_tok[:, 0, 256 * gr:256 * gr + 256], bank(4)[:, 0:256],
                               ACT.Copy).then_inc(s_o, 1)
                for odd, b in ((0, 5), (1, 7)):
                    dst = o_tok[:, 1, 256 * gr:256 * gr + 256].rearrange("p (a b d) -> p a b d", a=2, b=2)
                    act.activation(dst[:, :, odd, :], split3(bank(b)[:, 0:128], 2), ACT.Copy).then_inc(s_o, 1)
            act.wait_ge(s_ors, 1)
            act.activation(nrm[:, :, 0:8], nrm[:, :, 0:8], ACT.Sqrt).then_inc(s_orr, 1)

            def out_high(first, n):
                for b in range(2):
                    act.wait_ge(s_ot_ps, 2 * n + b + 1)
                    act.activation(o_hi[:, first + 2 * b:first + 2 * b + 2, :], split3(bank(b), 2),
                                   ACT.Copy).then_inc(s_ohi, 1)
            out_high(0, 0)

            for j in range(6):
                act.wait_ge(s_ro_ps, j + 1)
                n = 2 if j < 5 else 1
                act.activation(ro_t[:, 2 * j:2 * j + n, :], split3(bank(2 + j), 2)[:, 0:n, :],
                               ACT.Copy).then_inc(s_ro, 1)
            for j in range(6):
                act.wait_ge(s_rel_ps, j + 1)
                t, hs = by_keys(j)
                act.activation(rel[:, t, hs, 0:P * (t + 1)], split3(bank(j), 4 if j < 2 else 2), ACT.Relu).then_inc(s_rel, 1)

            def exps(prb, src, scale, base):
                for t in range(NT):
                    act.wait_ge(s_nmx, base + t + 1)
                    for h in range(HEADS):
                        act.activation(prb[:, t, h, 0:P * (t + 1)], src(t, h), ACT.Exp,
                                       bias=nmx[:, t, h:h + 1], scale=scale,
                                       accum_out=den[:, t, h:h + 1]).then_inc(s_exp, 1)

            def prob_tiles(dst, base):
                for j in range(6):
                    act.wait_ge(s_pt_ps, base + j + 1)
                    act.activation(dst[:, 4 * j:4 * j + 4, :].rearrange("p a b -> p (a b)"),
                                   bank((4 + j) % 8), ACT.Copy).then_inc(s_pt, 1)

            def attention_high(base):
                for b in range(2):
                    act.wait_ge(s_pv_ps, base + b + 1)
                    act.activation(o_hi[:, 4 + 2 * b:6 + 2 * b, :], split3(bank(2 + b), 2),
                                   ACT.Copy).then_inc(s_pv_hi, 1)

            exps(prob, lambda t, h: prob[:, t, h, 0:P * (t + 1)], HD ** -0.5, 0)
            prob_tiles(prob_t, 0)
            attention_high(0)

            def gates(G, first, biased):
                for c in range(8):
                    ahead(G[c])
                    act.wait_ge(w_used, G[c] + 1)
                    src = split3(bank(4 + c % 4), 2)
                    if biased:
                        for j in range(2):
                            k = R_BG + 2 * c + j
                            act.activation(gate[:, 2 * c + j, :], src[:, j, :], ACT.Sigmoid,
                                           bias=chan[:, k:k + 1]).then_inc(s_gate, 1)
                    else:
                        act.activation(gate[:, 2 * c:2 * c + 2, :], src,
                                       ACT.Sigmoid).then_inc(s_gate, 2)

            def merge_high(PR, first):
                for c in range(2):
                    ahead(PR[c][0])
                    ahead(PR[c][1])
                    act.wait_ge(s_merge, first + c + 1)
                    act.activation(h_hi[:, 4 * c:4 * c + 4, :], ga, ACT.Copy).then_inc(s_merge_hi, 1)

            def keep(ch):
                for c in ch:
                    for i in c:
                        ahead(i)

            def ffn(F, first):
                for e in range(len(F)):
                    ahead(F[e][0])
                    act.wait_ge(w_used, F[e][0] + 1)
                    act.activation(act_s[:, e % 2], split3(bank(4 + 2 * (e % 2)), 2),
                                   ACT.Silu).then_inc(s_silu, 1)
                    ahead(F[e][1])
                    act.wait_ge(s_prod2, first + e + 1)
                    b = 2 * (e % 2)
                    act.activation(o_hi[:, b:b + 2, :], act_p[:, e % 2], ACT.Copy).then_inc(s_ahi, 1)
                ahead(F[-1][2])

            gates(GATE, 0, True)
            merge_high(PROJ, 0)
            keep(OUT)
            norm(1, 1, R_N2)
            act.wait_ge(s_rlm, 1)
            act.activation(rl[:, :, 0:4], rl[:, :, 0:4], ACT.Exp).then_inc(s_rle, 1)
            act.wait_ge(s_rlm, 2)
            act.activation(el, el, ACT.Exp).then_inc(s_rle, 1)
            act.wait_ge(s_ct_ps, 1)
            act.activation(comb_t[0:16, :], bank(5)[0:16, 0:S], ACT.Copy).then_inc(s_ct, 1)
            for b in range(0, 8, 2):
                act.wait_ge(s_cr_ps, b + 1)
                act.activation(comb_rep[:, 2 * b:2 * b + 2, :], split3(bank(b), 2),
                               ACT.Copy).then_inc(s_cr, 1)
            ffn(EXP, 0)
            norm(2, None, None)

            norm(3, 2, R_NMIX)
            for c in range(4):
                ahead(HGQF[c])
                act.wait_ge(w_used, HGQF[c] + 1)
                dst = (hq if c < 2 else hk).rearrange("p a b -> p (a b)")[:, 512 * (c % 2):512 * (c % 2) + 512]
                act.activation(dst, bank(c), ACT.Silu if c < 2 else ACT.Sigmoid).then_inc(s_hev, 1)
            for b in range(5):
                ahead(TOK2[b][0])
                ahead(TOK2[b][1])
                act.wait_ge(w_used, TOK2[b][1] + 1)
                act.activation(z2[:, :, 512 * b:512 * b + 512], split3(bank(4 + 2 * (b % 2), 2), 2),
                               ACT.Copy).then_inc(s_tok_ev, 1)
            act.wait_ge(s_tok_ps, 1)
            act.activation(z2[:, :, Z2_F:Z2_F + 8], split3(bank(0)[:, 0:16], 2),
                           ACT.Copy).then_inc(s_tok_ev, 1)
            act.activation(z2[:, :, Z2_G:Z2_G + 512], z2[:, :, Z2_G:Z2_G + 512],
                           ACT.Silu).then_inc(s_zs, 1)
            act.wait_ge(s_lbs, 1)
            act.activation(small[:, 384:392], small[:, 384:392], ACT.Exp).then_inc(s_lbe, 1)
            act.wait_ge(s_fg, 1)
            act.activation(hd, hk, ACT.Ln).then_inc(s_logf, 1)
            for n in range(len(LEVELS)):
                act.wait_ge(s_hd, n + 1)
                act.activation(he, hd, ACT.Exp).then_inc(s_he, 1)
            act.wait_ge(s_hio, 1)
            act.activation(he, he, ACT.Exp).then_inc(s_hie, 1)
            act.wait_ge(s_hkt_ps, 1)
            act.activation(hkd_t.rearrange("p a b -> p (a b)"), bank(4), ACT.Copy).then_inc(s_hkt, 1)
            act.wait_ge(s_hs_ps, 1)
            act.activation(hs0.rearrange("p a b -> p (a b)"), bank(5), ACT.Copy).then_inc(s_hs, 1)
            act.wait_ge(s_ho_ps, 1)
            act.activation(ho, split3(bank(6, 2), 2), ACT.Copy).then_inc(s_ho, 1)
            act.wait_ge(s_ors, 2)
            act.activation(nrm[:, :, 0:4], nrm[:, :, 0:4], ACT.Sqrt).then_inc(s_orr, 1)
            out_high(0, 1)
            softplus(1)
            act.wait_ge(s_l2s, 2)
            act.activation(nrm, nrm, ACT.Sqrt).then_inc(s_l2r, 1)
            for j in range(4):
                act.wait_ge(s_fq_ps, j + 1)
                act.activation(qk2_t[:, 2 * j:2 * j + 2, :], split3(bank(2 + j), 2),
                               ACT.Copy).then_inc(s_fq, 1)
            def logits_in_psum(t, h):
                b, n = key_bank(t, h)
                return split3(bank(b), 4 if t == 0 else 2)[:, n, :]
            exps(prob2, logits_in_psum, 1.0, 2)
            prob_tiles(prob2_t, 6)
            attention_high(2)
            gates(GATE2, 8, False)
            merge_high(PROJ2, 2)
            keep(OUT2)
            norm(4, 3, R_NFFN)
            act.dma_start(p_tok, p_2[0, 0].rearrange("(t p) d -> p t d", p=P)).then_inc(s_p, 16)
            ffn(FFN, N_EXP)
            norm(5, 4, R_NPLE)
            act.wait_ge(s_p_ps, 1)
            act.activation(o_hi[:, 0:2, :], split3(bank(4), 2), ACT.Copy).then_inc(s_p_hi, 1)
            for c in range(2):
                ahead(PLEG[c][0])
                ahead(PLEG[c][1])
                act.wait_ge(w_used, PLEG[c][1] + 1)
                act.activation(res[:, :, 512 * c:512 * c + 512], split3(bank(2 * c, 2), 2),
                               ACT.Sigmoid).then_inc(s_plg, 1)

        @block.tensor
        def _(pe):
            def chunk(i):
                pe.wait_ge(w_ready, i + 1)
                _, kt, n = chunks[i]
                return [w[:, i % SPL, 0:kt * n].rearrange("p (k n) -> p k n", k=kt) for w in (w_hi, w_lo)]

            def weights_still(i, outs, a_hi, a_lo):
                hi, lo = chunk(i)
                kt = chunks[i][1]
                for c, o in enumerate(outs):
                    cols = slice(P * c, P * c + P)
                    for k in range(kt):
                        pe.matmul(o, hi[:, k, cols], a_hi[:, k, :], start=(k == 0), stop=False)
                        pe.matmul(o, hi[:, k, cols], a_lo[:, k, :], start=False, stop=False)
                        last_mm = pe.matmul(o, lo[:, k, cols], a_hi[:, k, :], start=False,
                                            stop=(k == kt - 1))
                last_mm.then_inc(w_used, 1)

            def weights_move(i, outs, a_hi, a_lo, first, end):
                hi, lo = chunk(i)
                kt, n = chunks[i][1:]
                for (t, c), o in outs.items():
                    tok = slice(P * t, P * t + P)
                    cols = slice(512 * c, min(n, 512 * c + 512))
                    for k in range(kt):
                        pe.matmul(o, a_hi[:, k, tok], hi[:, k, cols], start=(first and k == 0), stop=False)
                        pe.matmul(o, a_hi[:, k, tok], lo[:, k, cols], start=False, stop=False)
                        last_mm = pe.matmul(o, a_lo[:, k, tok], hi[:, k, cols], start=False,
                                            stop=(end and k == kt - 1))
                last_mm.then_inc(w_used, 1)

            def turn_x(turn):
                pe.wait_ge(s_xn, turn + 1)
                for b in range(4):
                    for k in (2 * b, 2 * b + 1):
                        for t in range(NT):
                            m = pe.transpose(split3(bank(b), 2)[:, k % 2, P * t:P * t + P],
                                             xn[:, t, P * k:P * k + P], ident[:, :])
                    m.then_inc(s_xt, 1)
                pe.wait_ge(s_h, 8 * (turn + 1))

            pe.wait_ge(s_const, 11)
            pe.wait_ge(s_rows, 128)
            pe.transpose(bank(7)[:, 0:R_ALL], rows[:, :], ident[0:R_ALL, 0:R_ALL]).then_inc(s_chan_ps, 1)
            pe.wait_ge(s_rep, 176)
            for c in range(3):
                n = min(512, C_ALL - 512 * c)
                m = pe.matmul(bank(4 + c)[:, 0:n], ones[0:1, :], rep_row[0:1, 512 * c:512 * c + n],
                              start=True, stop=True)
            m.then_inc(s_rep_ps, 1)
            pe.matmul(bank(6)[:, 400:432], ones[0:1, :], freq_row[0:1, :], start=True,
                      stop=True).then_inc(s_rep_ps, 1)
            turn_x(0)

            for c in range(6):
                if c >= 4:
                    pe.wait_ge(s_conv_ev, c - 3)
                b = split3(bank(c % 4), 2)
                weights_still(CONV[c], [b[:, 0, :], b[:, 1, :]], h_hi, h_lo)

            def tok_block(T, b, width, base):
                if base + b >= 2:
                    pe.wait_ge(s_tok_ev, base + b - 1)
                outs = {(t, 0): bank(4 + 2 * (b % 2) + t)[:, 0:width] for t in range(NT)}
                weights_move(T[b][0], outs, h_hi, h_lo, True, False)
                weights_move(T[b][1], outs, h_hi[:, 4:8], h_lo[:, 4:8], False, True)

            pe.wait_ge(s_chan, 5)
            for b in range(N_TOK_BLK):
                tok_block(TOK, b, TOK_BLK, 0)

            pe.wait_ge(s_silu_y, 6)
            pe.wait_ge(s_tok_ev, N_TOK_BLK)
            pe.wait_ge(s_conv_ev, 6)
            for j in range(6):
                t, g = j // 3, j % 3
                for c in range(4):
                    m = pe.transpose(bank(j)[:, P * c:P * c + P],
                                     y_t[:, 4 * g + c, P * t:P * t + P], ident[:, :])
                m.then_inc(s_yt, 1)
            pe.wait_ge(s_glog, 1)
            for n, mask in enumerate((upto, after)):
                for t in range(NT):
                    o = 16 * n + 8 * t
                    m = pe.matmul(bank(6)[:, o:o + 8], mask[:, :], glog[:, t, :], start=True, stop=True)
            m.then_inc(s_gsum, 1)
            pe.wait_ge(s_qn, 1)
            pe.wait_ge(s_qkv, 6)
            for j in range(6):
                for c in range(4):
                    pair, t = 2 * (j % 2) + c // 2, c % 2
                    src = (qkv[:, t, P * pair:P * pair + P], qkv[:, t, 512 + P * pair:640 + P * pair],
                           k_b[:, t, P * pair:P * pair + P])[j // 2]
                    m = pe.transpose(bank(j)[:, P * c:P * c + P], src, ident[:, :])
                m.then_inc(s_heads_ps, 1)
            pe.wait_ge(s_qn, 2)
            pe.wait_ge(s_eg, 1)
            for c in range(4):
                m = pe.transpose(bank(6)[:, P * c:P * c + P], q_dec[:, P * c:P * c + P], ident[:, :])
            m.then_inc(s_heads_ps, 1)

            def head(tile, h, t):
                r = 64 * (h % 2)
                return tile[r:r + 64, h // 2, P * t:P * t + P]

            for gr in range(2):
                pe.wait_ge(s_gmask, gr + 1)
                pe.wait_ge(s_heads, 7)
                if gr:
                    pe.wait_ge(s_v1, 2 * gr)
                for t in range(NT):
                    for u in range(4):
                        m = pe.matmul(bank(t)[:, P * u:P * u + P], g_mask[:, t, u, :], upto[:, :],
                                      start=True, stop=True)
                    m.then_inc(s_dps, 1)
                if gr:
                    pe.wait_ge(s_o, 3 * gr)
                for n, right in enumerate((kb_t, q_t)):
                    for odd in range(2):
                        for t in range(NT):
                            for pl in range(2):
                                h = 4 * gr + 2 * pl + odd
                                o = bank(2 + 2 * n + odd)[:, P * (2 * t + pl):P * (2 * t + pl) + P]
                                m = pe.matmul(o, head(k_t, h, t), head(right, h, t), start=True, stop=True)
                m.then_inc(s_kkqk, 1)
                pe.wait_ge(s_inv0, gr + 1)
                for t in range(NT):
                    for u in range(4):
                        m = pe.transpose(bank(t)[:, P * u:P * u + P], inv_t[:, t, u, :], ident[:, :])
                    m.then_inc(s_inv0_ps, 1)
                for n in range(1, len(LEVELS)):
                    for t in range(NT):
                        pe.wait_ge(s_lev, 12 * gr + 2 * (n - 1) + t + 1)
                        if n == 1:
                            pe.wait_ge(s_inv0_ev, 2 * gr + t + 1)
                        else:
                            pe.wait_ge(s_inv, 12 * gr + 2 * (n - 2) + t + 1)
                            pe.wait_ge(s_prod, 12 * gr + 2 * (n - 2) + t + 1)
                        for u in range(4):
                            m = pe.matmul(bank(2 + t)[:, P * u:P * u + P], lev[:, t, u, :],
                                          inv[:, t, u, :], start=True, stop=True)
                        m.then_inc(s_prod_ps, 1)
                    for t in range(NT):
                        pe.wait_ge(s_prod, 12 * gr + 2 * (n - 1) + t + 1)
                        for u in range(4):
                            if n < len(LEVELS) - 1:
                                pe.matmul(bank(4 + t)[:, P * u:P * u + P], inv_t[:, t, u, :],
                                          prod[:, t, u, :], start=True, stop=True)
                        for u in range(4):
                            m = pe.matmul(bank(6 + t)[:, P * u:P * u + P], prod[:, t, u, :],
                                          inv_t[:, t, u, :], start=True, stop=True)
                        m.then_inc(s_dinv, 1)
                pe.wait_ge(s_inv, 12 * gr + 12)
                for u in range(4):
                    h = 4 * gr + u
                    m = pe.matmul(bank(2)[64 * (h % 2):64 * (h % 2) + 64, P * (u // 2):P * (u // 2) + P],
                                  kb_g[:, HD * h:HD * h + HD], inv_t[:, 1, u, :], start=True, stop=True)
                m.then_inc(s_wt_ps, 1)
                for u in range(4):
                    h = 4 * gr + u
                    m = pe.matmul(bank(0)[:, HD * u:HD * u + HD], inv_t[:, 0, u, :],
                                  v_b[:, 0, HD * h:HD * h + HD], start=True, stop=True)
                m.then_inc(s_u0, 1)
                pe.wait_ge(s_v0, gr + 1)
                for u in range(4):
                    h = 4 * gr + u
                    m = pe.matmul(bank(3)[64 * (h % 2):64 * (h % 2) + 64, HD * (u // 2):HD * (u // 2) + HD],
                                  k_dec[:, HD * h:HD * h + HD], v_new[:, 0, HD * h:HD * h + HD],
                                  start=True, stop=True)
                m.then_inc(s_st_ps, 1)
                pe.wait_ge(s_st, gr + 1)
                pe.wait_ge(s_wt, gr + 1)
                for u in range(4):
                    h = 4 * gr + u
                    r = 64 * (h % 2)
                    o = bank(1 if r == 0 else 6)[:, HD * (u // 2):HD * (u // 2) + HD]
                    pe.matmul(o, inv_t[:, 1, u, :], v_b[:, 1, HD * h:HD * h + HD], start=True, stop=False)
                    m = pe.matmul(o, w_t[r:r + 64, u // 2, :], state[r:r + 64, u // 2, :],
                                  start=False, stop=True)
                m.then_inc(s_u1, 1)
                for u in range(4):
                    h = 4 * gr + u
                    pe.matmul(bank(4)[:, HD * u:HD * u + HD], qk_t[:, 0, u, :],
                              v_new[:, 0, HD * h:HD * h + HD], start=True, stop=True)
                pe.wait_ge(s_v1, 2 * gr + 2)
                for u in range(4):
                    h = 4 * gr + u
                    r = 64 * (h % 2)
                    o = bank(5 if r == 0 else 7)[:, HD * (u // 2):HD * (u // 2) + HD]
                    pe.matmul(o, q_dec_t[r:r + 64, h // 2, :], state[r:r + 64, u // 2, :],
                              start=True, stop=False)
                    m = pe.matmul(o, qk_t[:, 1, u, :], v_new[:, 1, HD * h:HD * h + HD],
                                  start=False, stop=True)
                m.then_inc(s_o_ps, 1)

            def turn_out(o):
                for b in range(2):
                    for c in (2 * b, 2 * b + 1):
                        for t in range(NT):
                            m = pe.transpose(split3(bank(b), 2)[:, c % 2, P * t:P * t + P],
                                             o[:, t, P * c:P * c + P], ident[:, :])
                    m.then_inc(s_ot_ps, 1)
            pe.wait_ge(s_on, 1)
            turn_out(o_tok)

            pe.wait_ge(s_roped, 1)
            for j in range(6):
                for c in range(2 if j < 5 else 1):
                    b = 2 * j + c
                    for t in range(NT):
                        if b < 4:
                            src = roped[:, t, 2 * b:2 * b + 2, :].rearrange("p a b -> p (a b)")
                        elif b < 6:
                            src = k_dup[:, t, b - 4].rearrange("p a b -> p (a b)")
                        elif b < 10:
                            src = roped[:, t, 2 * b - 2:2 * b, :].rearrange("p a b -> p (a b)")
                        else:
                            src = ik_dup[:, t].rearrange("p a b -> p (a b)")
                        m = pe.transpose(split3(bank(2 + j), 2)[:, c, P * t:P * t + P], src, ident[:, :])
                m.then_inc(s_ro_ps, 1)
            pe.wait_ge(s_ro, 6)
            pe.wait_ge(s_o_ready, 2)

            for j in range(6):
                t = by_keys(j)[0]
                hs = heads_of(j)
                for n, h in enumerate(hs):
                    r = 64 * (h % 2)
                    m = pe.matmul(split3(bank(j), len(hs))[:, n, :], ro_t[r:r + 64, 6 + h // 2, P * t:P * t + P],
                                  ro_t[r:r + 64, 10, 0:P * (t + 1)], start=True, stop=True)
                m.then_inc(s_rel_ps, 1)
            for j in range(6):
                t = by_keys(j)[0]
                hs = heads_of(j)
                if j >= 2:
                    pe.wait_ge(s_rel, j - 1)
                for n, h in enumerate(hs):
                    r = 64 * (h % 2)
                    m = pe.matmul(split3(bank((6 + j) % 8), len(hs))[:, n, :],
                                  ro_t[r:r + 64, h // 2, P * t:P * t + P],
                                  ro_t[r:r + 64, 4 + h // 4, 0:P * (t + 1)], start=True, stop=True)
                m.then_inc(s_log_ps, 1)

            def turn_probs(prb, base):
                for j in range(6):
                    pe.wait_ge(s_prob, base + (1 if j < 2 else 2))
                    for c in range(4):
                        n = 4 * j + c
                        src = prb[:, 0, n, 0:P] if j < 2 else prb[:, 1, (n - 8) // 2, P * (n % 2):P * (n % 2) + P]
                        m = pe.transpose(bank((4 + j) % 8)[:, P * c:P * c + P], src, ident[:, :])
                    m.then_inc(s_pt_ps, 1)

            def prob_times_v(prb_t, v, base):
                pe.wait_ge(s_pt, base + 6)
                for b in range(2):
                    for h in range(4 * b, 4 * b + 4):
                        r = 64 * (h % 2)
                        for t in range(NT):
                            o = split3(bank(2 + b), 2)[r:r + 64, (h // 2) % 2, P * t:P * t + P]
                            for s in range(t + 1):
                                m = pe.matmul(o, v(s, h), prb_t[:, h if t == 0 else 8 + 2 * h + s, :],
                                              start=(s == 0), stop=(s == t))
                    m.then_inc(s_pv_ps, 1)

            pe.wait_ge(s_msk, 6)
            turn_probs(prob, 0)
            prob_times_v(prob_t, lambda s, h: z_tok[:, s, Z_BV + HD * (h // 4):Z_BV + HD * (h // 4) + HD], 0)

            def gates(G, first):
                for c in range(8):
                    if c >= 4:
                        pe.wait_ge(s_gate, 2 * (first + c - 3))
                    b = split3(bank(4 + c % 4), 2)
                    weights_still(G[c], [b[:, 0, :], b[:, 1, :]], h_hi, h_lo)

            def mix(PR, OU, n):
                for c in range(2):
                    if c == 1:
                        pe.wait_ge(s_gate, 16 * (n + 1))
                    for j in range(2):
                        outs = [split3(bank(4 * c + 2 * j + q // 2), 2)[:, q % 2, :] for q in range(4)]
                        weights_still(PR[c][j], outs, o_hi[:, 4 * j:4 * j + 4], o_lo[:, 4 * j:4 * j + 4])
                pe.wait_ge(s_merged, 2 * n + 1)
                for c in range(2):
                    outs = {(t, 0): bank(2 * c + t) for t in range(NT)}
                    for k in range(2):
                        if k == 1:
                            pe.wait_ge(s_merged, 2 * n + 2)
                        weights_move(OU[c][k], outs, h_hi[:, 4 * k:4 * k + 4], h_lo[:, 4 * k:4 * k + 4],
                                         k == 0, k == 1)

            pe.wait_ge(s_bout, 2)
            gates(GATE, 0)
            mix(PROJ, OUT, 0)
            turn_x(1)

            pe.wait_ge(s_rt_lo, 1)
            for t in range(NT):
                tok = slice(P * t, P * t + P)
                for k in range(KD):
                    o = bank(4)[:, 20 * t:20 * t + 20]
                    pe.matmul(o, h_hi[:, k, tok], rt_hi[:, k, 0:20], start=(k == 0), stop=False)
                    pe.matmul(o, h_hi[:, k, tok], rt_lo[:, k, 0:20], start=False, stop=False)
                    m = pe.matmul(o, h_lo[:, k, tok], rt_hi[:, k, 0:20], start=False, stop=(k == KD - 1))
            m.then_inc(s_rl_ps, 1)
            pe.wait_ge(s_comb, 1)
            for t in range(NT):
                m = pe.transpose(bank(5)[0:16, P * t:P * t + P], comb[:, t, :], ident[:, :])
            m.then_inc(s_ct_ps, 1)
            pe.wait_ge(s_ct, 1)
            pe.wait_ge(s_sel, 1)
            for b in range(8):
                for c in range(2):
                    m = pe.matmul(split3(bank(b), 2)[:, c, :], sel_e[0:16, 2 * b + c, :], comb_t[0:16, :],
                                  start=True, stop=True)
                m.then_inc(s_cr_ps, 1)

            def ffn(F, first):
                for e in range(len(F) + 1):
                    if e < len(F):
                        if e >= 2:
                            pe.wait_ge(s_prod2, first + e - 1)
                        for j in range(2):
                            b = split3(bank(4 + 2 * (e % 2) + j), 2)
                            weights_still(F[e][j], [b[:, 0, :], b[:, 1, :]], h_hi, h_lo)
                    if e >= 1:
                        pe.wait_ge(s_a, first + e)
                        b = 2 * ((e - 1) % 2)
                        outs = {(t, c): bank(2 * t + c) for t in range(NT) for c in range(2)}
                        weights_move(F[e - 1][2], outs, o_hi[:, b:b + 2], o_lo[:, b:b + 2],
                                         e == 1, e == len(F))

            pe.wait_ge(s_cr, 8)
            ffn(EXP, 0)
            turn_x(2)

            for c in range(4):
                b = split3(bank(c), 2)
                weights_still(HGQF[c], [b[:, 0, :], b[:, 1, :]], h_hi, h_lo)
            for b in range(5):
                tok_block(TOK2, b, 512, N_TOK_BLK)
            pe.wait_ge(s_hev, 4)
            for t in range(NT):
                tok = slice(P * t, P * t + P)
                for k in range(KD):
                    o = bank(0)[:, 8 * t:8 * t + 8]
                    pe.matmul(o, h_hi[:, k, tok], rt_hi[:, k, 20:28], start=(k == 0), stop=False)
                    pe.matmul(o, h_hi[:, k, tok], rt_lo[:, k, 20:28], start=False, stop=False)
                    m = pe.matmul(o, h_lo[:, k, tok], rt_hi[:, k, 20:28], start=False, stop=(k == KD - 1))
            m.then_inc(s_tok_ps, 1)
            pe.wait_ge(s_tok_ev, N_TOK_BLK + 6)
            pe.wait_ge(s_fg, 2)
            for n in range(len(LEVELS) + 1):
                if n:
                    pe.wait_ge(s_hx, n)
                if n >= 2:
                    pe.wait_ge(s_hsc, n - 1)
                for u in range(8):
                    b = bank(2 * (n % 2) + u // 4)[:, P * (u % 4):P * (u % 4) + P]
                    left, right = (hk[:, u, :], hq[:, u, :]) if n == 0 else (hx[:, n % 2, u, :],) * 2
                    m = pe.matmul(b, left, right, start=True, stop=True)
                m.then_inc(s_hsc_ps, 1)
            pe.wait_ge(s_hkd, 1)
            for h in range(HG_HEADS):
                m = pe.transpose(bank(4)[:, P * h:P * h + P], hkd[:, h, :], ident[:, :])
            m.then_inc(s_hkt_ps, 1)
            pe.wait_ge(s_hkt, 1)
            for h in range(HG_HEADS):
                m = pe.matmul(bank(5)[:, P * h:P * h + P], hkd_t[:, h, :],
                              z2[:, 0, Z2_I + P * h:Z2_I + P * h + P], start=True, stop=True)
            m.then_inc(s_hs_ps, 1)
            pe.wait_ge(s_hs, 1)
            pe.wait_ge(s_hsc, 8)
            for h in range(HG_HEADS):
                v = [z2[:, t, Z2_I + P * h:Z2_I + P * h + P] for t in range(NT)]
                pe.matmul(bank(6)[:, P * h:P * h + P], hsc[:, 2 * h, :], v[0], start=True, stop=True)
                pe.matmul(bank(7)[:, P * h:P * h + P], hqb[:, h, :], hs0[:, h, :], start=True, stop=False)
                m = pe.matmul(bank(7)[:, P * h:P * h + P], hsc[:, 2 * h + 1, :], v[1], start=False, stop=True)
            m.then_inc(s_ho_ps, 1)
            pe.wait_ge(s_on, 2)
            turn_out(ho)
            pe.wait_ge(s_qn, 3)
            for j in range(4):
                for c in range(4):
                    b, t = 2 * j + c // 2, c % 2
                    m = pe.transpose(bank(2 + j)[:, P * c:P * c + P],
                                     z2[:, t, Z2_Q + P * b:Z2_Q + P * b + P], ident[:, :])
                m.then_inc(s_fq_ps, 1)
            pe.wait_ge(s_fq, 4)
            pe.wait_ge(s_fmask, 1)
            pe.wait_ge(s_o_ready, 4)
            for j in range(6):
                t = by_keys(j)[0]
                hs = heads_of(j)
                for n, h in enumerate(hs):
                    r = 64 * (h % 2)
                    o = split3(bank(j), len(hs))[:, n, :]
                    pe.matmul(o, qk2_t[r:r + 64, h // 2, P * t:P * t + P],
                              qk2_t[r:r + 64, 4 + h // 2, 0:P * (t + 1)], start=True, stop=False)
                    if t == 1:
                        pe.matmul(o[:, 0:P], ones[:, :], f_mask[:, 0, h, :], start=False, stop=False)
                        pe.matmul(o[:, 0:P], upto[:, :], last(glog[:, 1, h], P),
                                  start=False, stop=False)
                    own = o[:, P * t:P * t + P]
                    pe.matmul(own, upto[:, :], f_mask[:, t, h, :], start=False, stop=False)
                    m = pe.matmul(own, ident_bf[:, :], future_bf[:, :], start=False, stop=True)
                m.then_inc(s_fl_ps, 1)
            pe.wait_ge(s_prob, 4)
            turn_probs(prob2, 2)
            prob_times_v(prob2_t, lambda s, h: z2[:, s, Z2_V + HD * h:Z2_V + HD * h + HD], 6)
            pe.wait_ge(s_bout, 4)
            gates(GATE2, 8)
            mix(PROJ2, OUT2, 1)
            turn_x(3)
            ffn(FFN, N_EXP)
            turn_x(4)
            pe.wait_ge(s_p, 16)
            for k in range(2):
                for t in range(NT):
                    m = pe.transpose(split3(bank(4), 2)[:, k, P * t:P * t + P],
                                     p_tok[:, t, P * k:P * k + P], ident[:, :])
            m.then_inc(s_p_ps, 1)
            for c in range(2):
                outs = {(t, 0): bank(2 * c + t) for t in range(NT)}
                weights_move(PLEG[c][0], outs, h_hi, h_lo, True, False)
                weights_move(PLEG[c][1], outs, h_hi[:, 4:8], h_lo[:, 4:8], False, True)
            pe.wait_ge(s_p_ready, 1)
            outs = {(t, c): bank(4 + 2 * c + t) for c in range(2) for t in range(NT)}
            weights_move(PLEP, outs, o_hi[:, 0:2], o_lo[:, 0:2], True, True)

        @block.vector
        def _(dve):
            n_dve, split_at = [0], [0]
            mult, add_, sub = ALU.mult, ALU.add, ALU.subtract

            def step(ins):
                n_dve[0] += 1
                ins.then_inc(s_dve, 1)
                dve.wait_ge(s_dve, n_dve[0])

            def mark(ins):
                n_dve[0] += 1
                ins.then_inc(s_dve, 1)
                return n_dve[0]

            def ahead(i):
                while split_at[0] <= min(i + SPL - 1, N_CH - 1):
                    j = split_at[0]
                    _, kt, n = chunks[j]
                    dve.wait_ge(w_high, j + 1)
                    dve.tensor_tensor(w_lo[:, j % SPL, 0:kt * n], raw[:, j % RAW, 0:kt * n],
                                      w_hi[:, j % SPL, 0:kt * n].bitcast(F32), sub).then_inc(w_ready, 1)
                    split_at[0] += 1

            def norm(n, turn, row):
                dve.wait_ge(s_sq, 2 * (n + 1))
                dve.tensor_scalar(rms, ssq, 1.0 / DM, EPS, mult, add_).then_inc(s_ms, 1)
                dve.wait_ge(s_rt_n, n + 1)
                step(dve.reciprocal(rstd, rms))
                if turn is None:
                    for t in range(NT):
                        dve.scalar_tensor_tensor(x_tok[:, t], x_tok[:, t], rstd[:, t:t + 1],
                                                 rep[:, C_FIN:C_FIN + DM], mult, mult)\
                           .then_inc(s_dve, 1)
                        n_dve[0] += 1
                    dve.wait_ge(s_dve, n_dve[0])
                    dve.nop().then_inc(s_x_ready, 1)
                    return
                for t in range(NT):
                    m = dve.tensor_scalar(xn[:, t], x_tok[:, t], rstd[:, t:t + 1], None, mult)
                m.then_inc(s_xn, 1)
                for b in range(4):
                    dve.wait_ge(s_hhi, 8 * turn + 2 * b + 2)
                    for k in (2 * b, 2 * b + 1):
                        dve.scalar_tensor_tensor(h_lo[:, k, :], split3(bank(b), 2)[:, k % 2, :],
                                                 chan[:, row + k:row + k + 1],
                                                 h_hi[:, k, :].bitcast(F32), mult, sub).then_inc(s_h, 1)

            dve.wait_ge(s_chan_ps, 1)
            dve.tensor_copy(chan[:, :], bank(7)[:, 0:R_ALL]).then_inc(s_chan, 1)
            dve.wait_ge(s_rep_ps, 2)
            for c in range(3):
                n = min(512, C_ALL - 512 * c)
                dve.tensor_copy(rep[:, 512 * c:512 * c + n], bank(4 + c)[:, 0:n]).then_inc(s_chan, 1)
            dve.tensor_copy(over[:, 0, :], bank(6)[:, 400:432]).then_inc(s_chan, 1)
            dve.wait_ge(s_chan, 5)
            norm(0, 0, R_N1)
            dve.wait_ge(s_pos, 16)
            step(dve.tensor_copy(pos_f[:, :], pos_i[:, :]))
            step(dve.tensor_tensor(cs[:, 1], last(pos_f[:, :], 32), mid(over[:, 0, :], 2), mult))
            magic = 12582912.0
            step(dve.tensor_scalar(turns, cs[:, 1], 0.15915494309189535, magic, mult, add_))
            step(dve.tensor_scalar(turns, turns, magic, None, sub))
            for part in (6.28125, 0.0019350051879882812, 3.0199159819567e-07):
                step(dve.scalar_tensor_tensor(cs[:, 1], turns, -part, cs[:, 1], mult, add_))
            step(dve.tensor_scalar(cs[:, 0], cs[:, 1], 1.5707963267948966, None, add_))
            step(dve.tensor_scalar(over, cs[:, 0], 3.141592653589793, -6.283185307179586,
                                   ALU.is_gt, mult))
            step(dve.tensor_tensor(cs[:, 0], cs[:, 0], over, add_))
            dve.tensor_scalar(cs[:, :, :, :], cs[:, :, :, :], 3.1415925, -3.1415925, ALU.min,
                              ALU.max).then_inc(s_trig, 1)
            ahead(0)

            step(dve.memset(z_t[:, :, 0:3], 0.0))
            for c in range(6):
                ahead(CONV[c])
                dve.wait_ge(s_conv_ev, c + 1)
                for k in range(4):
                    for ct in (2 * c, 2 * c + 1):
                        w = chan[:, R_CONV + 12 * k + ct:R_CONV + 12 * k + ct + 1]
                        taps = z_t[:, ct, k:k + S]
                        if k == 0:
                            m = dve.tensor_scalar(y_t[:, ct, :], taps, w, None, mult)
                        else:
                            dve.wait_ge(s_tap, 8 * c + 2 * (k - 1) + ct % 2 + 1)
                            m = dve.scalar_tensor_tensor(y_t[:, ct, :], taps, w, y_t[:, ct, :], mult, add_)
                        m.then_inc(s_tap, 1)
                dve.wait_ge(s_tap, 8 * c + 8)
                dve.nop().then_inc(s_conv, 1)
            for b in range(N_TOK_BLK):
                ahead(TOK[b][0])
                ahead(TOK[b][1])
            dve.wait_ge(s_rt_hi, 1)
            dve.tensor_tensor(rt_lo[:, :, :], rt_raw[:, :, :], rt_hi[:, :, :].bitcast(F32),
                              sub).then_inc(s_rt_lo, 1)

            def softplus(n, ln_count):
                dve.scalar_tensor_tensor(sp2, sp1, -1.0, sp1, mult, ALU.min).then_inc(s_spe, 1)
                dve.wait_ge(s_spx, n + 1)
                dve.tensor_scalar(sp3, sp2, 1.0, None, add_).then_inc(s_spl, 1)
                dve.wait_ge(s_spm, ln_count)
                step(dve.scalar_tensor_tensor(sp1, sp1, 0.0, sp3, ALU.max, add_))

            dve.wait_ge(s_tok_ev, N_TOK_BLK)
            step(dve.tensor_tensor(sp1, z_tok[:, :, Z_ALPHA:Z_ALPHA + 8],
                                   mid(rep[:, C_DT:C_DT + 8], 2), add_))
            softplus(0, 2)
            dve.scalar_tensor_tensor(glog, sp1, -1.0, mid(alog, 2), mult, mult).then_inc(s_glog, 1)
            dve.wait_ge(s_qkv, 6)
            step(dve.tensor_tensor(sq, qkv[:, :, 0:DM], qkv[:, :, 0:DM], mult))
            nrm_all = small[:, 128:160]
            step(dve.tensor_reduce(nrm_all, sq.rearrange("p t (h d) -> p (t h) d", d=HD), X, add_))
            dve.tensor_scalar(nrm_all, nrm_all, EPS, None, add_).then_inc(s_l2s, 1)
            dve.wait_ge(s_l2r, 1)
            step(dve.reciprocal(nrm_all, nrm_all))
            step(dve.tensor_scalar(nrm[:, :, 0:8], nrm[:, :, 0:8], HD ** -0.5, None, mult))
            for t in range(NT):
                heads = qkv[:, t, 0:DM].rearrange("p (h d) -> p h d", d=HD)
                m = mark(dve.tensor_tensor(heads, heads, last(nrm[:, t, :], HD), mult))
            dve.wait_ge(s_beta, 1)
            dve.wait_ge(s_dve, m)

            def h64(ap):
                return ap.rearrange("p (h d) -> p h d", d=HD)
            for t in range(NT):
                dve.tensor_tensor(h64(v_b[:, t]), h64(qkv[:, t, 1024:1536]), last(beta[:, t], HD), mult)
                m = dve.tensor_tensor(h64(k_b[:, t]), h64(qkv[:, t, 512:1024]), last(beta[:, t], HD), mult)
            m.then_inc(s_qn, 1)
            dve.wait_ge(s_eg, 1)
            dve.wait_ge(s_qn, 1)
            dve.tensor_tensor(h64(q_dec), h64(qkv[:, 1, 0:512]), last(e_g[:, 1], HD), mult)
            dve.tensor_tensor(h64(k_dec), h64(qkv[:, 0, 512:1024]), last(e_gl[:, 0], HD), mult)
            dve.tensor_tensor(h64(kb_g), h64(k_b[:, 1]), last(e_g[:, 1], HD), mult).then_inc(s_qn, 1)

            for gr in range(2):
                if gr == 0:
                    dve.wait_ge(s_heads_ps, 6)
                    dve.wait_ge(s_qn, 2)
                else:
                    dve.wait_ge(s_o_ps, gr)
                for t in range(NT):
                    m = dve.tensor_tensor(g_mask[:, t], mid(after[:, :], 4),
                                          last(glog[:, t, 4 * gr:4 * gr + 4], P), mult)
                m.then_inc(s_gmask, 1)
                dve.wait_ge(s_dexp, 2 * gr + 2)
                d8, a8, p8, t8 = (v.rearrange("p t u i -> p (t u) i") for v in (dec, a_t, prod, inv_t))
                step(dve.tensor_tensor(d8, d8, mid(upto[:, :], 8), mult))
                dve.wait_ge(s_kkqk, gr + 1)
                for dst, first in ((qk_t, 4), (a_t, 2)):
                    for odd in range(2):
                        of = [v.rearrange("p t (a b) i -> p (t a) b i", b=2)[:, :, odd, :] for v in (dst, dec)]
                        m = dve.tensor_tensor(of[0], split3(bank(first + odd), 4), of[1], mult)
                m.then_inc(s_at, 1)
                dve.wait_ge(s_at, gr + 1)
                step(dve.tensor_tensor(p8, a8, mid(lvl[:, 0, :], 8), mult))
                step(dve.tensor_tensor(t8, mid(ident[:, :], 8), p8, sub))
                dve.nop().then_inc(s_inv0, 1)
                for n in range(1, len(LEVELS)):
                    for t in range(NT):
                        k = 12 * gr + 2 * (n - 1) + t + 1
                        if n == 1:
                            dve.wait_ge(s_inv0_ev, 2 * gr + t + 1)
                        dve.wait_ge(s_dinv, k)
                        if n < len(LEVELS) - 1:
                            dve.tensor_tensor(inv[:, t], inv[:, t], split3(bank(4 + t), 4), sub)
                        dve.tensor_tensor(inv_t[:, t], inv_t[:, t], split3(bank(6 + t), 4),
                                          sub).then_inc(s_inv, 1)
                        dve.wait_ge(s_inv, k)

            def o_norm(o, o_sq, n, heads, dim, gain, z, k):
                o3 = o.rearrange("p t (h d) -> p (t h) d", d=dim)
                dve.wait_ge(s_o if n == 0 else s_ho, 6 if n == 0 else 1)
                step(dve.tensor_tensor(o_sq, o, o, mult))
                nr = nrm[:, :, 0:heads]
                step(dve.tensor_reduce(nr, o_sq.rearrange("p t (h d) -> p t h d", d=dim), X, add_))
                dve.tensor_scalar(nr, nr, 1.0 / dim, EPS, mult, add_).then_inc(s_ors, 1)
                dve.wait_ge(s_orr, n + 1)
                step(dve.reciprocal(nr, nr))
                for t in range(NT):
                    ot = o[:, t].rearrange("p (h d) -> p h d", d=dim)
                    m = mark(dve.tensor_tensor(ot, ot, last(nrm[:, t, 0:heads], dim), mult))
                dve.wait_ge(s_dve, m)
                step(dve.tensor_tensor(o3, o3, mid(gain, 2 * heads), mult))
                dve.wait_ge(s_zs, n + 1)
                dve.tensor_tensor(o, o, z, mult).then_inc(s_on, 1)
                for b in range(2):
                    dve.wait_ge(s_ohi, 2 * n + b + 1)
                    dve.tensor_tensor(o_lo[:, 2 * b:2 * b + 2, :], split3(bank(b), 2),
                                      o_hi[:, 2 * b:2 * b + 2, :].bitcast(F32), sub).then_inc(s_o_ready, 1)

            o_norm(o_tok, view(14036, NT, 512), 0, HEADS, HD, rep[:, C_ANORM:C_ANORM + HD],
                   z_tok[:, :, Z_Z:Z_Z + 512], 0)

            dve.wait_ge(s_sin, 1)
            qk_in = z_tok[:, :, Z_BQ:Z_BV].rearrange("p t (h d) -> p t h d", d=HD)
            ix_in = z_tok[:, :, Z_IQ:Z_IW].rearrange("p t (h d) -> p t h d", d=HD)
            parts = ((qk_in, 0, 10), (ix_in, 10, 19))

            def turn_by(dst, half, trig):
                for src, a, b in parts:
                    w = cs[:, trig].unsqueeze(2).broadcast_to([P, NT, b - a, 32])
                    m = mark(dve.tensor_tensor(dst[:, :, a:b, :], src[:, :, :, 32 * half:32 * half + 32], w, mult))
                return m
            turn_by(rt1, 0, 0)
            dve.wait_ge(s_dve, turn_by(rt2, 1, 1))
            def both(out_half, op):
                for t in range(NT):
                    m = mark(dve.tensor_tensor(roped[:, t, :, 32 * out_half:32 * out_half + 32],
                                               rt1[:, t], rt2[:, t], op))
                dve.wait_ge(s_dve, m)
            both(0, sub)
            turn_by(rt1, 1, 0)
            dve.wait_ge(s_dve, turn_by(rt2, 0, 1))
            both(1, add_)
            for t in range(NT):
                dve.tensor_copy(k_dup[:, t], roped[:, t, 8:10, :].unsqueeze(2).broadcast_to([P, 2, 2, HD]))
                m = dve.tensor_copy(ik_dup[:, t], mid(roped[:, t, 18, :], 2))
            m.then_inc(s_roped, 1)
            step(dve.tensor_scalar(iw, z_tok[:, :, Z_IW:Z_IW + 8], (HEADS ** -0.5) * (HD ** -0.5), None, mult))
            for h in range(HEADS):
                for t in range(NT):
                    k = P * (t + 1)
                    dve.wait_ge(s_rel, key_bank(t, h)[0] + 1)
                    if h == 0:
                        m = mark(dve.tensor_scalar(score[:, t, 0:k], rel[:, t, h, 0:k], iw[:, t, h:h + 1], None, mult))
                    else:
                        dve.wait_ge(s_dve, n_dve[0] - 1)
                        m = mark(dve.scalar_tensor_tensor(score[:, t, 0:k], rel[:, t, h, 0:k], iw[:, t, h:h + 1],
                                                          score[:, t, 0:k], mult, add_))
            dve.wait_ge(s_dve, m)
            for t in range(NT):
                m = mark(dve.memset(score[0:CHUNK, t, P * t + CHUNK:P * t + P], -BIG))
            dve.wait_ge(s_dve, m)
            tops = (top8, top8b)
            for r in range(TOPK // 8):
                for t in range(NT):
                    src = (score if r == 0 else work)[:, t, 0:P * (t + 1)]
                    if r:
                        dve.wait_ge(s_dve, n_dve[0] - 1 + t)
                    m = mark(dve.max(tops[t], src))
                for t in range(NT):
                    src = (score if r == 0 else work)[:, t, 0:P * (t + 1)]
                    dve.wait_ge(s_dve, m - 1 + t)
                    mark(dve.match_replace(work[:, t, 0:P * (t + 1)], tops[t], src, TAKEN))
            dve.wait_ge(s_dve, n_dve[0])
            for t in range(NT):
                k = P * (t + 1)
                m = mark(dve.tensor_scalar(work[:, t, 0:k], work[:, t, 0:k], -2e38, -BIG, ALU.is_gt, mult))
            dve.wait_ge(s_dve, m)
            for j in range(6):
                t, hs = by_keys(j)
                k, n = P * (t + 1), len(heads_of(j))
                dve.wait_ge(s_log_ps, j + 1)
                dve.tensor_tensor(prob[:, t, hs, 0:k], split3(bank((6 + j) % 8), n),
                                  mid(work[:, t, 0:k], n), add_).then_inc(s_msk, 1)

            def softmax(prb, srcs, scale, base):
                for t in range(NT):
                    for hs, src, wait in srcs(t):
                        wait()
                        m = mark(dve.reduce_max(mx[:, t, hs], src, X))
                    dve.wait_ge(s_dve, m)
                    dve.tensor_scalar(nmx[:, t, 0:8], mx[:, t, 0:8], -scale, None, mult).then_inc(s_nmx, 1)
                for t in range(NT):
                    k = P * (t + 1)
                    dve.wait_ge(s_exp, 8 * (base + t + 1))
                    step(dve.reciprocal(rden[:, t, 0:8], den[:, t, 0:8]))
                    dve.tensor_tensor(prb[:, t, :, 0:k], prb[:, t, :, 0:k], last(rden[:, t, 0:8], k),
                                      mult).then_inc(s_prob, 1)

            softmax(prob, lambda t: [(slice(0, 8), prob[:, t, :, 0:P * (t + 1)],
                                      lambda: dve.wait_ge(s_msk, 2 if t == 0 else 6))], HD ** -0.5, 0)

            def attention_low(n):
                for b in range(2):
                    dve.wait_ge(s_pv_hi, 2 * n + b + 1)
                    dve.tensor_tensor(o_lo[:, 4 + 2 * b:6 + 2 * b, :], split3(bank(2 + b), 2),
                                      o_hi[:, 4 + 2 * b:6 + 2 * b, :].bitcast(F32), sub).then_inc(s_bout, 1)
            attention_low(0)

            def mix(G, PR, OU, n):
                for c in range(8):
                    ahead(G[c])
                for c in range(2):
                    ahead(PR[c][0])
                    ahead(PR[c][1])
                    dve.wait_ge(w_used, PR[c][1] + 1)
                    dve.wait_ge(s_gate, 16 * (n + 1))
                    if c:
                        dve.wait_ge(s_merged, 2 * n + 1)
                    dve.tensor_tensor(ga, gate[:, 4 * c:4 * c + 4], split3(bank(4 * c, 2), 4), mult)
                    step(dve.tensor_tensor(gb, gate[:, 8 + 4 * c:12 + 4 * c], split3(bank(4 * c + 2, 2), 4), mult))
                    dve.tensor_tensor(ga, ga, gb, add_).then_inc(s_merge, 1)
                    dve.wait_ge(s_merge_hi, 2 * n + c + 1)
                    dve.tensor_tensor(h_lo[:, 4 * c:4 * c + 4, :], ga, h_hi[:, 4 * c:4 * c + 4, :].bitcast(F32),
                                      sub).then_inc(s_merged, 1)
                for c in range(2):
                    ahead(OU[c][0])
                    ahead(OU[c][1])
                    dve.wait_ge(w_used, OU[c][1] + 1)
                    cols = slice(512 * c, 512 * c + 512)
                    m = mark(dve.tensor_tensor(x_tok[:, :, cols], x_tok[:, :, cols], split3(bank(2 * c, 2), 2), add_))
                dve.wait_ge(s_dve, m)
                dve.nop().then_inc(s_x_ready, 1)

            def ffn(F, first, weighted):
                for e in range(len(F)):
                    ahead(F[e][1])
                    dve.wait_ge(w_used, F[e][1] + 1)
                    dve.wait_ge(s_silu, first + e + 1)
                    if e >= 2:
                        dve.wait_ge(s_a, first + e - 1)
                    up = split3(bank(5 + 2 * (e % 2)), 2)
                    m = dve.tensor_tensor(act_p[:, e % 2], act_s[:, e % 2], up, mult)
                    if weighted:
                        step(m)
                        m = dve.tensor_tensor(act_p[:, e % 2], act_p[:, e % 2], mid(comb_rep[:, e, :], 2), mult)
                    m.then_inc(s_prod2, 1)
                    ahead(F[e][1] + 1)
                    dve.wait_ge(s_ahi, first + e + 1)
                    b = 2 * (e % 2)
                    dve.tensor_tensor(o_lo[:, b:b + 2, :], act_p[:, e % 2], o_hi[:, b:b + 2, :].bitcast(F32),
                                      sub).then_inc(s_a, 1)
                ahead(F[-1][2])
                dve.wait_ge(w_used, F[-1][2] + 1)
                step(dve.tensor_tensor(x_tok[:, :, :], x_tok[:, :, :], split3(bank(0, 4), 2), add_))
                dve.nop().then_inc(s_x_ready, 1)

            mix(GATE, PROJ, OUT, 0)
            norm(1, 1, R_N2)
            for j in range(4):
                m = mark(dve.memset(tie[:, j:j + 1], float(4 - j)))
            dve.wait_ge(s_dve, m)

            def one_hot(dst, src, top):
                step(dve.tensor_reduce(top, src, X, ALU.max))
                step(dve.tensor_tensor(dst, src, last(top, 4), ALU.is_equal))
                step(dve.tensor_tensor(dst, dst, mid(tie, 2), mult))
                step(dve.tensor_reduce(gs2, dst, X, ALU.max))
                step(dve.tensor_tensor(dst, dst, last(gs2, 4), ALU.is_equal))

            dve.wait_ge(s_rl_ps, 1)
            step(dve.tensor_tensor(rl, split3(bank(4)[:, 0:40], 2), mid(rep[:, C_RB:C_RB + 20], 2), add_))
            gl = rl[:, :, 0:4]
            one_hot(ga1, gl, gs1)
            step(dve.tensor_tensor(ttmp, rl[:, :, 4:20].rearrange("p t (g j) -> p t g j", j=4), last(ga1, 4), mult))
            step(dve.tensor_reduce(el, ttmp.rearrange("p t g j -> p t j g"), X, add_))
            dve.tensor_tensor(gl, gl, last(gs1, 4), sub).then_inc(s_rlm, 1)
            step(dve.tensor_reduce(gs3, el, X, ALU.max))
            dve.tensor_tensor(el, el, last(gs3, 4), sub).then_inc(s_rlm, 1)
            dve.wait_ge(s_rle, 2)
            step(dve.tensor_reduce(gs3, gl, X, add_))
            step(dve.reciprocal(gs3, gs3))
            one_hot(e1h, el, gs1)
            step(dve.scalar_tensor_tensor(ea, e1h, -4.0, el, mult, add_))
            one_hot(e2h, ea, gs1)
            step(dve.tensor_tensor(e1h, e1h, e2h, add_))
            step(dve.tensor_tensor(e1h, e1h, el, mult))
            step(dve.tensor_reduce(gs1, e1h, X, add_))
            step(dve.reciprocal(gs1, gs1))
            step(dve.tensor_tensor(gs1, gs1, gs3, mult))
            step(dve.tensor_tensor(e1h, e1h, last(gs1, 4), mult))
            dve.tensor_tensor(comb.rearrange("p t (g j) -> p t g j", j=4), last(ga1, 4),
                              e1h.unsqueeze(2).broadcast_to([P, NT, 4, 4]), mult).then_inc(s_comb, 1)
            for b in range(1, 8, 2):
                dve.wait_ge(s_cr_ps, b + 1)
                dve.tensor_copy(comb_rep[:, 2 * b:2 * b + 2, :], split3(bank(b), 2)).then_inc(s_cr, 1)
            dve.wait_ge(s_cr, 8)
            ffn(EXP, 0, True)
            norm(2, None, None)

            norm(3, 2, R_NMIX)
            l0, l1 = chan[:, R_LB:R_LB + 4], chan[:, R_LB + 4:R_LB + 8]
            step(dve.tensor_tensor(lbt, l0, l1, ALU.max))
            dve.tensor_tensor(lb, l0, lbt, sub)
            dve.tensor_tensor(lbc, l1, lbt, sub).then_inc(s_lbs, 1)
            for c in range(4):
                ahead(HGQF[c])
            for b in range(5):
                ahead(TOK2[b][0])
                ahead(TOK2[b][1])
            dve.wait_ge(s_lbe, 1)
            step(dve.tensor_tensor(lbt, lb, lbc, add_))
            step(dve.reciprocal(lbt, lbt))
            step(dve.tensor_tensor(lb, lb, lbt, mult))
            step(dve.tensor_tensor(lbc, lbc, lbt, mult))
            dve.wait_ge(s_hev, 4)
            for h in range(HG_HEADS):
                two = hk[:, 2 * h:2 * h + 2, :]
                m = dve.tensor_scalar(two, two, lbc[:, h:h + 1], lb[:, h:h + 1], mult, add_)
            m.then_inc(s_fg, 1)
            step(dve.memset(hsc, 0.0))
            dve.wait_ge(s_logf, 1)
            step(dve.tensor_scalar(hk, hk, -1.0, 1.0, mult, add_))
            dve.nop().then_inc(s_fg, 1)
            for u in range(8):
                m = mark(dve.tensor_tensor_scan(hb[:, u, :], ones[:, :], hd[:, u, :], 0.0, mult, add_))
            dve.wait_ge(s_dve, m)
            flat_b, flat_d, flat_e, flat_k, flat_q = (v.rearrange("p a b -> p (a b)") for v in (hb, hd, he, hk, hq))
            for n in range(len(LEVELS) + 1):
                if n < len(LEVELS):
                    s = LEVELS[n]
                    bl = split3(flat_b, 512 // s)
                    step(dve.tensor_tensor(split3(flat_d, 512 // s), bl,
                                           bl[:, :, s - 1:s].broadcast_to([P, 512 // s, 2 * s]), sub))
                    dve.scalar_tensor_tensor(flat_d, flat_d, -1.0, flat_d, mult, ALU.min).then_inc(s_hd, 1)
                dve.wait_ge(s_hsc_ps, n + 1)
                mask = ident[:, :] if n == 0 else lvl[:, n - 1, :]
                dve.copy_predicated(hsc, mid(mask, 8).bitcast(I32), split3(bank(2 * (n % 2), 2), 8)).then_inc(s_hsc, 1)
                if n < len(LEVELS):
                    dve.wait_ge(s_he, n + 1)
                    s = LEVELS[n]

                    def half(v, i):
                        return v.rearrange("p (b h r) -> p b h r", h=2, r=s)[:, :, i, :]
                    x_op = hx[:, (n + 1) % 2].rearrange("p a b -> p (a b)")
                    dve.tensor_tensor(half(x_op, 0), half(flat_k, 0), half(flat_e, 0), mult)
                    dve.tensor_tensor(half(x_op, 1), half(flat_q, 1), half(flat_e, 1), mult).then_inc(s_hx, 1)
                    if n + 1 == len(LEVELS):
                        dve.wait_ge(s_hx, n + 1)
            by_tile = [v.rearrange("p (h t) i -> p h t i", t=2) for v in (hb, he, hk, hq)]
            tb, te, tk, tq = by_tile
            dve.tensor_tensor(te[:, :, 0, :], tb[:, :, 0, P - 1:P].broadcast_to([P, HG_HEADS, P]), tb[:, :, 0, :], sub)
            dve.tensor_copy(te[:, :, 1, :], tb[:, :, 1, :]).then_inc(s_hio, 1)
            dve.wait_ge(s_hie, 1)
            dve.tensor_tensor(hqb, tq[:, :, 1, :], te[:, :, 1, :], mult)
            dve.tensor_tensor(hkd, tk[:, :, 0, :], te[:, :, 0, :], mult).then_inc(s_hkd, 1)
            o_norm(ho, hsq, 1, HG_HEADS, HG_D, rep[:, C_ONORM:C_ONORM + HG_D], z2[:, :, Z2_G:Z2_G + 512], 1)

            step(dve.tensor_tensor(sp1, z2[:, :, Z2_F:Z2_F + 8], mid(rep[:, C_FB:C_FB + 8], 2), add_))
            step(dve.tensor_scalar(sp1, sp1, -1.0, None, mult))
            softplus(1, 3)
            step(dve.tensor_scalar(glog, sp1, -1.0, None, mult))
            for t in range(NT):
                m = dve.tensor_tensor(f_mask[:, t], mid(after[:, :], 8), last(glog[:, t], P), mult)
            m.then_inc(s_fmask, 1)
            for t in range(NT):
                qk = z2[:, t, Z2_Q:Z2_V]
                step(dve.tensor_tensor(fsq, qk, qk, mult))
                step(dve.tensor_reduce(nrm[:, t, :], h64(fsq), X, add_))
            dve.tensor_scalar(nrm, nrm, 1.0 / HD, EPS, mult, add_).then_inc(s_l2s, 1)
            dve.wait_ge(s_l2r, 2)
            step(dve.reciprocal(nrm_all, nrm_all))
            step(dve.tensor_scalar(nrm[:, :, 0:8], nrm[:, :, 0:8], HD ** -0.5, None, mult))
            for t in range(NT):
                qk = h64(z2[:, t, Z2_Q:Z2_V])
                m = mark(dve.tensor_tensor(qk, qk, last(nrm[:, t, :], HD), mult))
            dve.wait_ge(s_dve, m)
            for t in range(NT):
                for first, c in ((Z2_Q, C_QN), (Z2_K, C_KN)):
                    v = h64(z2[:, t, first:first + 512])
                    m = dve.tensor_tensor(v, v, mid(rep[:, c:c + HD], 8), mult)
            m.then_inc(s_qn, 1)
            softmax(prob2, lambda t: [(by_keys(j)[1], split3(bank(j), len(heads_of(j))),
                                       lambda j=j: dve.wait_ge(s_fl_ps, j + 1))
                                      for j in range(6) if by_keys(j)[0] == t], 1.0, 2)
            attention_low(1)
            mix(GATE2, PROJ2, OUT2, 1)
            norm(4, 3, R_NFFN)
            ffn(FFN, N_EXP, False)
            norm(5, 4, R_NPLE)
            dve.wait_ge(s_p_hi, 1)
            dve.tensor_tensor(o_lo[:, 0:2, :], split3(bank(4), 2), o_hi[:, 0:2, :].bitcast(F32), sub).then_inc(s_p_ready, 1)
            for c in range(2):
                ahead(PLEG[c][0])
                ahead(PLEG[c][1])
            dve.wait_ge(w_used, PLEP + 1)
            for c in range(2):
                cols = slice(512 * c, 512 * c + 512)
                dve.wait_ge(s_plg, c + 1)
                step(dve.tensor_tensor(res[:, :, cols], res[:, :, cols], split3(bank(4 + 2 * c, 2), 2), mult))
                dve.tensor_tensor(res[:, :, cols], res[:, :, cols], x_tok[:, :, cols], add_).then_inc(s_result, 1)


_INS = ["x", "positions", "norm1_g", "w_in", "b_gate", "conv_w", "a_log", "dt_bias", "a_norm_g",
        "w_proj_a", "w_proj_b", "w_out", "norm2_g", "w_router_group", "b_router_group",
        "w_router_expert", "b_router_expert", "w_exp_gate", "w_exp_up", "w_exp_down",
        "final_norm_g", "p_2", "norm_mix_g_2", "w_in_2", "hg_lb_logits_2", "hg_onorm_g_2",
        "fox_f_bias_2", "fox_q_norm_g_2", "fox_k_norm_g_2", "w_branch_a_2", "w_branch_b_2",
        "w_out_2", "norm_ffn_g_2", "w_ffn_gate_2", "w_ffn_up_2", "w_ffn_down_2", "norm_ple_g_2",
        "w_ple_gate_2", "w_ple_proj_2"]


def kernel(**inputs):
    import numpy as np
    import concourse.bacc as bacc
    from concourse.bass_utils import run_bass_kernel_spmd

    nc = bacc.Bacc("TRN2", target_bir_lowering=False, num_devices=1,
                   dynamic_dma_scratch_size=1024)
    arrays, args = {}, []

    def give(name, a):
        arrays[f"in_{name}"] = a
        args.append(nc.dram_tensor(f"in_{name}", a.shape, mybir.dt.from_np(a.dtype),
                                   kind="ExternalInput").ap())

    for name in _INS:
        give(name, np.ascontiguousarray(inputs[name]))
    half = HD // 2
    give("rope_freq", (np.float32(10000.0) ** (-np.arange(half, dtype=np.float32) / np.float32(half)))
         .astype(np.float32).reshape(1, half))
    out = nc.dram_tensor("out", (1, S, DM), F32, kind="ExternalOutput").ap()
    two_block_program(nc, *args, out)
    r = run_bass_kernel_spmd(nc, [arrays], core_ids=[0])
    return r.results[0]["out"]
```

```python
from contextlib import ExitStack

import concourse.bass as bass
from concourse import mybir

F32 = mybir.dt.float32
F32R = mybir.dt.float32r
BF16 = mybir.dt.bfloat16
I32 = mybir.dt.int32
ALU = mybir.AluOpType
ACT = mybir.ActivationFunctionType
X = mybir.AxisListType.X

P = 128
S = 256
NT = S // P
DM = 1024
KD = DM // P
EPS = 1e-6
BIG = 1e30
TAKEN = -3e38

A_W = 512
CONV_W = 3 * A_W
TOK0 = CONV_W
Z_Z, Z_BETA, Z_ALPHA, Z_BQ, Z_BV, Z_IQ, Z_IW, TOK_W = 0, 512, 520, 528, 1168, 1296, 1872, 1880
GATE0 = TOK0 + TOK_W
TOK_BLK = 470
N_TOK_BLK = TOK_W // TOK_BLK
HEADS, HD = 8, 64
KV_HEADS = 2
TOPK = 64
CHUNK = 64
N_GROUPS, PER_GROUP, D_EXP = 4, 4, 256
N_EXP = N_GROUPS * PER_GROUP
HG_HEADS, HG_D = 4, 128
TOK0_2 = 1024
TOK_W2 = 2568
Z2_I, Z2_G, Z2_Q, Z2_K, Z2_V, Z2_F = 0, 512, 1024, 1536, 2048, 2560
GATE0_2 = TOK0_2 + TOK_W2
D_FF = 2816
FF_PAIRS = D_FF // 256
PLE = 256

CH = 2048
RAW = 4
SPL = 3
LEVELS = [1, 2, 4, 8, 16, 32, 64]

R_N1, R_N2, R_NMIX, R_NFFN, R_NPLE, R_BG, R_CONV, R_LB, R_ALL = 0, 8, 16, 24, 32, 40, 56, 104, 112
C_FIN, C_ALOG, C_DT, C_ANORM, C_RB, C_ONORM, C_FB, C_QN, C_KN, C_ALL = (
    0, 1024, 1032, 1040, 1104, 1124, 1252, 1260, 1324, 1388)


def two_block_program(nc, x, positions, norm1_g, w_in, b_gate, conv_w, a_log, dt_bias, a_norm_g,
                      w_proj_a, w_proj_b, w_out, norm2_g, w_router_group, b_router_group,
                      w_router_expert, b_router_expert, w_exp_gate, w_exp_up, w_exp_down,
                      final_norm_g, p_2, norm_mix_g_2, w_in_2, hg_lb_logits_2, hg_onorm_g_2,
                      fox_f_bias_2, fox_q_norm_g_2, fox_k_norm_g_2, w_branch_a_2, w_branch_b_2,
                      w_out_2, norm_ffn_g_2, w_ffn_gate_2, w_ffn_up_2, w_ffn_down_2,
                      norm_ple_g_2, w_ple_gate_2, w_ple_proj_2, rope_freq, out, dbg=None):
    ctx = ExitStack()
    with ctx:
        def sb(name, shape, dt=F32):
            return ctx.enter_context(nc.sbuf_tensor(name, shape, dt))

        def sem(name):
            return ctx.enter_context(nc.semaphore(name))

        chunks = []

        def rows_by(w, cols):
            return w[:, cols].rearrange("(k p) n -> p k n", p=P)

        def half_rows(w, half, cols):
            return w[half * 512:(half + 1) * 512, cols].rearrange("(k p) n -> p k n", p=P)

        def add(src):
            chunks.append((src, src.shape[1], src.shape[2]))
            return len(chunks) - 1

        wi, wi2 = w_in[0], w_in_2[0]
        CONV = [add(rows_by(wi, slice(256 * c, 256 * c + 256))) for c in range(6)]
        TOK = [[add(half_rows(wi, k, slice(TOK0 + TOK_BLK * b, TOK0 + TOK_BLK * (b + 1))))
                for k in range(2)] for b in range(N_TOK_BLK)]
        GATE = [add(rows_by(wi, slice(GATE0 + 256 * c, GATE0 + 256 * c + 256))) for c in range(8)]
        PROJ = [[add(rows_by(w[0], slice(512 * c, 512 * c + 512))) for w in (w_proj_a, w_proj_b)]
                for c in range(2)]
        OUT = [[add(half_rows(w_out[0], k, slice(512 * c, 512 * c + 512))) for k in range(2)]
               for c in range(2)]
        EXP = [[None] * 3 for _ in range(N_EXP)]
        for e in range(N_EXP + 1):
            if e < N_EXP:
                EXP[e][0] = add(w_exp_gate[0, e].rearrange("(k p) n -> p k n", p=P))
                EXP[e][1] = add(w_exp_up[0, e].rearrange("(k p) n -> p k n", p=P))
            if e >= 1:
                EXP[e - 1][2] = add(w_exp_down[0, e - 1].rearrange("(k p) n -> p k n", p=P))
        HGQF = [add(rows_by(wi2, slice(256 * c, 256 * c + 256))) for c in range(4)]
        TOK2 = [[add(half_rows(wi2, k, slice(TOK0_2 + 512 * b, TOK0_2 + 512 * (b + 1))))
                 for k in range(2)] for b in range(5)]
        GATE2 = [add(rows_by(wi2, slice(GATE0_2 + 256 * c, GATE0_2 + 256 * c + 256)))
                 for c in range(8)]
        PROJ2 = [[add(rows_by(w[0], slice(512 * c, 512 * c + 512)))
                  for w in (w_branch_a_2, w_branch_b_2)] for c in range(2)]
        OUT2 = [[add(half_rows(w_out_2[0], k, slice(512 * c, 512 * c + 512))) for k in range(2)]
                for c in range(2)]
        FFN = [[None] * 3 for _ in range(FF_PAIRS)]
        for e in range(FF_PAIRS + 1):
            if e < FF_PAIRS:
                FFN[e][0] = add(rows_by(w_ffn_gate_2[0], slice(256 * e, 256 * e + 256)))
                FFN[e][1] = add(rows_by(w_ffn_up_2[0], slice(256 * e, 256 * e + 256)))
            if e >= 1:
                FFN[e - 1][2] = add(w_ffn_down_2[0, 256 * (e - 1):256 * e, :]
                                    .rearrange("(k p) n -> p k n", p=P))
        PLEG = [[add(half_rows(w_ple_gate_2[0], k, slice(512 * c, 512 * c + 512)))
                 for k in range(2)] for c in range(2)]
        PLEP = add(rows_by(w_ple_proj_2[0], slice(0, DM)))
        N_CH = len(chunks)

        LVL2 = [TOK2[1 + n // 2][n % 2] for n in range(8)]

        raw = sb("raw", [P, RAW, CH])
        w_hi = sb("w_hi", [P, SPL, CH], F32R)
        w_lo = sb("w_lo", [P, SPL, CH], F32R)
        x_tok = sb("x_tok", [P, NT, DM])
        h_hi = sb("h_hi", [P, KD, S], F32R)
        h_lo = sb("h_lo", [P, KD, S], F32R)
        o_hi = sb("o_hi", [P, 8, S], F32R)
        o_lo = sb("o_lo", [P, 8, S], F32R)
        rt_hi = sb("rt_hi", [P, KD, 28], F32R)
        rt_lo = sb("rt_lo", [P, KD, 28], F32R)
        rt_raw = sb("rt_raw", [P, KD, 28])
        ident = sb("ident", [P, P])
        upto = sb("upto", [P, P])
        after = sb("after", [P, P])
        ones = sb("ones", [P, P])
        ident_bf = sb("ident_bf", [P, P], BF16)
        future_bf = sb("future_bf", [P, P], BF16)
        lvl = sb("lvl", [P, len(LEVELS), P])
        rows = sb("rows", [R_ALL, P])
        chan = sb("chan", [P, R_ALL])
        rep = sb("rep", [P, C_ALL])
        pos_i = sb("pos_i", [P, NT], I32)
        pos_f = sb("pos_f", [P, NT])
        freq_row = sb("freq_row", [1, 32])
        cs = sb("cs", [P, 2, NT, 32])
        small = sb("small", [P, 640])
        arena = sb("arena", [P, 21460])
        ps = ctx.enter_context(nc.psum_tensor("ps", [P, 8 * 512], F32))

        def bank(b, n=1):
            return ps[:, 512 * b:512 * (b + n)]

        def view(off, *shape):
            n = 1
            for s in shape:
                n *= s
            v = arena[:, off:off + n]
            if len(shape) == 2:
                v = v.rearrange("p (a b) -> p a b", a=shape[0])
            if len(shape) == 3:
                v = v.rearrange("p (a b c) -> p a b c", a=shape[0], b=shape[1])
            if len(shape) == 4:
                v = v.rearrange("p (a b c d) -> p a b c d", a=shape[0], b=shape[1], c=shape[2])
            return v

        def mid(ap, n):
            return ap.unsqueeze(1).broadcast_to([ap.shape[0], n, ap.shape[1]])

        def last(ap, n):
            return ap.unsqueeze(len(ap.shape)).broadcast_to(list(ap.shape) + [n])

        def split3(ap, a):
            return ap.rearrange("p (a b) -> p a b", a=a)

        def split4(ap, a, b):
            return ap.rearrange("p (a b c) -> p a b c", a=a, b=b)

        xn = view(0, NT, DM)
        junk = view(2048, NT, DM)
        rep_row = view(9940, C_ALL)[0:1]
        z_tok = view(0, NT, TOK_W)
        z_t = view(3760, 12, S + 3)
        y_t = view(6868, 12, S)
        qkv = view(9940, NT, CONV_W)
        q_t, k_t, kb_t = ([view(first + 512 * n, 2, S) for first in (14036, 19924)] for n in range(3))
        qk_t = view(18900, NT, 4, P)
        v_b, k_b, kb_g, k_dec = view(3760, NT, 512), view(4784, NT, 512), view(5808, 512), view(6320, 512)
        gate = view(6868, 16, S)
        q_dec, q_dec_t = view(13012, 512), view(17108, 4, P)
        g_mask, dec, a_t = view(10964, NT, 4, P), view(11988, NT, 4, P), view(13012, NT, 4, P)
        lev = view(10964, NT, 4, P)
        inv, inv_t, prod = (view(14036 + 1024 * n, NT, 4, P) for n in range(3))
        v_new, o_tok = view(16084, NT, 512), view(4784, NT, 512)
        w_t, state = view(17620, 2, P), view(17876, 2, HD)
        sq = view(14036, NT, DM)
        o_sq = view(5808, NT, 512)
        rt1, rt2 = view(17620, 10, 32), view(17940, 10, 32)
        k_dup, ik_dup = view(18132, NT, 2, 2, HD), view(18644, NT, 2, HD)
        ro_t = view(15060, 11, S)
        score, work = view(3760, NT, S), view(4272, NT, S)
        prob = view(10964, NT, HEADS, S)
        rel = view(10964, NT, HEADS, S)
        prob_t = view(15060, 24, P)
        ga, gb = view(4096, 4, S), view(5120, 4, S)
        comb_rep = view(0, N_EXP, S)
        act_s = view(4096, 2, 2, S)
        act_p = view(5120, 2, 2, S)
        comb_t = view(6200, S)
        sel_e = view(6500, N_EXP, P)
        z2 = view(0, NT, TOK_W2)
        hq, hk, hb, hd, he = (view(5136 + 1024 * n, 8, P) for n in range(5))
        hx = view(10256, 2, 8, P)
        hsc = view(12304, 8, P)
        hqb, hkd, hkd_t, hs0 = (view(10256 + 512 * n, 4, P) for n in range(4))
        ho, hsq = view(9232, NT, 512), view(8208, NT, 512)
        fsq = view(13328, 1024)
        gate2 = view(14352, 16, S)
        qk2_t = view(5136, 8, S)
        f_mask = view(7184, NT, HEADS, P)
        prob2 = view(9232, NT, HEADS, S)
        prob2_t = view(5136, 24, P)
        p_tok = view(8192, NT, PLE)
        res = view(4096, NT, DM)

        nrm2 = split3(small[:, 472:504], 2)
        ssq, rms, rstd = small[:, 0:2], small[:, 2:4], small[:, 4:6]
        sp1, sp2, sp3 = split3(small[:, 16:32], 2), split3(small[:, 32:48], 2), split3(small[:, 48:64], 2)
        beta, glog = split3(small[:, 64:80], 2), split3(small[:, 80:96], 2)
        e_g, e_gl = split3(small[:, 96:112], 2), split3(small[:, 112:128], 2)
        nrm = split3(small[:, 128:160], 2)
        mx, nmx, den, rden = (split3(small[:, 160 + 16 * n:176 + 16 * n], 2) for n in range(4))
        top8 = small[:, 224:232]
        iw = split3(small[:, 232:248], 2)
        rl = split3(small[:, 248:288], 2)
        ga1, ga2 = split3(small[:, 288:296], 2), split3(small[:, 296:304], 2)
        gs1, gs2, gs3 = small[:, 304:306], small[:, 306:308], small[:, 308:310]
        el, e1h, e2h, ea = (split3(small[:, 312 + 8 * n:320 + 8 * n], 2) for n in range(4))
        tie = small[:, 344:348]
        comb = split3(small[:, 352:384], 2)
        lb, lbc, lbt = small[:, 384:388], small[:, 388:392], small[:, 392:396]
        alog = small[:, 396:404]
        sp4 = split3(small[:, 408:424], 2)
        ttmp = split4(small[:, 424:456], 2, 4)
        turns = split3(small[:, 512:576], 2)
        over = split3(small[:, 576:640], 2)
        top8b = small[:, 464:472]

        w_in_sem = [sem(f"chunk_loaded_{i}") for i in range(RAW)]
        w_high, w_ready, w_used = sem("w_high"), sem("w_ready"), sem("w_used")
        s_x, s_rows, s_rep, s_pos, s_rt = sem("x_loaded"), sem("rows_loaded"), sem("rep_loaded"), sem("pos_loaded"), sem("router_loaded")
        s_p = sem("p_loaded")
        s_pool, s_const = sem("pool_step"), sem("constants_ready")
        s_act, s_dve = sem("act_step"), sem("dve_step")
        s_chan_ps, s_chan = sem("channel_vectors_in_psum"), sem("channel_vectors_ready")
        s_rep_ps = sem("repeated_vectors_in_psum")
        s_rt_hi, s_rt_lo = sem("router_high"), sem("router_split")
        s_sq, s_ms, s_rt_n, s_xn, s_xt, s_hhi, s_h = (sem(n) for n in (
            "squares_summed", "mean_square", "root", "x_normed", "x_transposed", "h_high", "h_ready"))

        (s_conv_ev, s_tap, s_conv, s_silu_y, s_tok_ps, s_tok_ev, s_yt, s_qkv, s_beta, s_spe,
         s_spx, s_spl, s_spm, s_glog, s_gsum, s_eg, s_l2s, s_l2r, s_qn, s_heads_ps, s_heads,
         s_gmask, s_dps, s_dexp, s_kkqk, s_at, s_inv0, s_inv0_ps, s_inv0_ev, s_lev,          s_prod_ps, s_prod, s_dinv, s_inv, s_wt_ps, s_wt, s_u0, s_v0, s_st_ps, s_st, s_u1, s_v1,
         s_o_ps, s_o, s_ors, s_orr, s_zs, s_on, s_ot_ps, s_ohi, s_o_ready) = (sem(n) for n in (
            "conv_in_sbuf", "tap_step", "taps_done", "conv_silu_done", "tok_in_psum",
            "tok_in_sbuf", "conv_transposed", "qkv_ready", "beta_ready", "softplus_arg",
            "softplus_exp", "softplus_arg2", "softplus_ln", "log_decay_ready", "decay_sums_in_psum",
            "decay_exps_ready", "head_squares", "head_roots", "heads_normed", "head_tiles_in_psum",
            "head_tiles_ready", "decay_operand_ready", "decay_in_psum", "decay_exp_done",
            "scores_in_psum", "scores_ready", "inverse_start", "inverse_start_in_psum",
            "inverse_start_turned", "level_ready", "product_in_psum",
            "product_ready", "correction_in_psum", "inverse_updated", "w_in_psum", "w_turned",
            "u0_in_psum", "v0_ready", "state_in_psum", "state_ready", "v1_in_psum", "v1_ready",
            "delta_out_in_psum", "delta_out_ready", "out_squares", "out_roots", "z_silu_ready",
            "out_normed", "out_transposed", "out_high", "out_ready"))
        (s_trig, s_sin, s_roped, s_ro_ps, s_ro, s_rel_ps, s_rel, s_log_ps, s_msk, s_nmx, s_exp,
         s_prob, s_pt_ps, s_pt, s_pv_ps, s_pv_hi, s_bout) = (sem(n) for n in (
            "angles_ready", "trig_ready", "roped", "rope_turned", "rope_tiles_ready",
            "index_scores_in_psum", "index_relu_ready", "logits_in_psum", "logits_masked",
            "row_max_ready", "exp_ready", "prob_ready", "prob_turned", "prob_tiles_ready",
            "attention_in_psum", "attention_high", "attention_ready"))
        (s_gate, s_merge, s_merge_hi, s_merged, s_x_ready,
         s_rl_ps, s_rlm, s_rle, s_comb, s_ct_ps, s_ct, s_cr_ps, s_cr, s_sel, s_silu, s_prod2,
         s_ahi, s_a, ) = (sem(n) for n in (
            "gate_ready", "merge_ready", "merge_high",
            "merged_ready", "x_ready", "router_in_psum", "router_shifted",
            "router_exps", "comb_ready", "comb_turned", "comb_rows_ready", "comb_rep_in_psum",
            "comb_rep_ready", "selectors_ready", "silu_ready", "product2_ready",
            "act_high", "act_ready", ))
        (s_hev, s_lbe, s_lbs, s_fg, s_logf, s_hd, s_he, s_hx, s_hsc_ps, s_hsc, s_hio, s_hie,
         s_hkd, s_hkt_ps, s_hkt, s_hs_ps, s_hs, s_ho_ps, s_ho) = (sem(n) for n in (
            "hg_in_sbuf", "lb_shifted", "lb_exps", "forget_ready", "log_forget_ready",
            "level_distance", "level_decay", "level_operand", "level_scores_in_psum",
            "level_scores_taken", "edge_distance", "edge_decay", "edge_operands", "kd_turned",
            "kd_ready", "hg_state_in_psum", "hg_state_ready", "hg_out_in_psum", "hg_out_ready"))
        s_ff, s_gate_ev, s_gate_ev2 = (sem(n) for n in (
            "forget_logits_in_sbuf", "gate_logits_in_sbuf", "gate_logits_in_sbuf_2"))
        (s_fq_ps, s_fq, s_fmask, s_fl_ps, s_p_ps, s_p_hi, s_p_ready, s_plg,          s_result, s_out) = (sem(n) for n in (
            "fox_heads_in_psum", "fox_heads_ready", "forget_operand", "fox_logits_in_psum",
            "p_turned", "p_high", "p_ready", "ple_gate_ready",
            "result_ready", "result_stored"))

        def by_keys(j):
            if j < 2:
                return 0, slice(j, 8, 2)
            h0 = (j - 2) % 2 + 4 * ((j - 2) // 2)
            return 1, slice(h0, h0 + 3, 2)

        def heads_of(j):
            return list(range(8))[by_keys(j)[1]]

        def key_bank(t, h):
            return (h % 2, h // 2) if t == 0 else (2 + h % 2 + 2 * (h // 4), (h % 4) // 2)

        block = ctx.enter_context(nc.Block())

        @block.sync
        def _(sp):
            sp.dma_start(x_tok[:, :, :], x[0].rearrange("(t p) d -> p t d", p=P)).then_inc(s_x, 16)
            for i, (src, kt, n) in enumerate(chunks):
                slot = i % RAW
                if i >= RAW:
                    sp.wait_ge(w_ready, i - RAW + 1)
                dst = raw[:, slot, 0:kt * n].rearrange("p (k n) -> p k n", k=kt)
                sp.dma_start(dst, src).then_inc(w_in_sem[slot], 16)
            sp.wait_ge(s_result, 2)
            sp.dma_start(out[0].rearrange("(t p) d -> p t d", p=P), res).then_inc(s_out, 16)
            sp.wait_ge(s_out, 16)

        @block.gpsimd
        def _(pool):
            n_pool = [0]

            def step(ins):
                n_pool[0] += 1
                ins.then_inc(s_pool, 1)
                pool.wait_ge(s_pool, n_pool[0])

            step(pool.memset(ident[:, :], 0.0))
            step(pool.affine_select(out=ident[:, :], in_=ident[:, :], compare_op=ALU.not_equal,
                                    fill=1.0, base=0, pattern=[[-1, P]], channel_multiplier=1))
            pool.tensor_copy(ident_bf[:, :], ident[:, :]).then_inc(s_const, 1)
            step(pool.memset(ones[:, :], 1.0))
            pool.affine_select(out=upto[:, :], in_=ones[:, :], compare_op=ALU.is_ge, fill=0.0,
                               base=0, pattern=[[1, P]], channel_multiplier=-1).then_inc(s_const, 1)
            pool.affine_select(out=after[:, :], in_=ones[:, :], compare_op=ALU.is_gt, fill=0.0,
                               base=0, pattern=[[-1, P]], channel_multiplier=1).then_inc(s_const, 1)
            step(pool.memset(future_bf[:, :], 0.0))
            pool.affine_select(out=future_bf[:, :], in_=future_bf[:, :], compare_op=ALU.is_ge,
                               fill=-BIG, base=0, pattern=[[-1, P]],
                               channel_multiplier=1).then_inc(s_const, 1)
            for n, s in enumerate(LEVELS):
                blocks = P // (2 * s)
                m = lvl[:, n, :].rearrange("p (b h r) -> p b h r", b=blocks, h=2)
                pool.memset(m[:, :, 0, :], 0.0)
                step(pool.memset(m[:, :, 1, :], 1.0))
                step(pool.affine_select(out=lvl[:, n, :], in_=lvl[:, n, :], compare_op=ALU.is_ge,
                                        fill=0.0, base=0, pattern=[[-2 * s, blocks], [0, 2 * s]],
                                        channel_multiplier=1))
                pool.affine_select(out=lvl[:, n, :], in_=lvl[:, n, :], compare_op=ALU.is_ge,
                                   fill=0.0, base=s - 1, pattern=[[2 * s, blocks], [0, 2 * s]],
                                   channel_multiplier=-1).then_inc(s_const, 1)
            for gr in range(2):
                pool.wait_ge(s_at, gr + 1)
                for n in range(1, len(LEVELS)):
                    if n >= 2:
                        pool.wait_ge(s_prod_ps, 2 * (6 * gr + n - 1))
                    for t in range(NT):
                        pool.tensor_tensor(lev[:, t], a_t[:, t], mid(lvl[:, n, :], 4),
                                           ALU.mult).then_inc(s_lev, 1)
            pool.wait_ge(s_x_ready, 1)
            step(pool.memset(sel_e[0:16], 0.0))
            pool.affine_select(out=sel_e[0:16], in_=sel_e[0:16], compare_op=ALU.not_equal,
                               fill=1.0, base=0, pattern=[[-1, N_EXP], [0, P]],
                               channel_multiplier=1).then_inc(s_sel, 1)

        @block.scalar
        def _(act):
            n_act, split_at = [0], [0]

            def step(ins):
                n_act[0] += 1
                ins.then_inc(s_act, 1)
                act.wait_ge(s_act, n_act[0])

            def ahead(i):
                while split_at[0] <= min(i + SPL - 1, N_CH - 1):
                    j = split_at[0]
                    _, kt, n = chunks[j]
                    act.wait_ge(w_in_sem[j % RAW], 16 * (j // RAW + 1))
                    if j >= SPL:
                        act.wait_ge(w_used, j - SPL + 1)
                    act.activation(w_hi[:, j % SPL, 0:kt * n], raw[:, j % RAW, 0:kt * n],
                                   ACT.Copy).then_inc(w_high, 1)
                    split_at[0] += 1

            def norm(n, turn, row):
                if n == 0:
                    act.wait_ge(s_x, 16)
                else:
                    act.wait_ge(s_x_ready, n)
                for t in range(NT):
                    act.activation(junk[:, t], x_tok[:, t], ACT.Square,
                                   accum_out=ssq[:, t:t + 1]).then_inc(s_sq, 1)
                act.wait_ge(s_ms, n + 1)
                act.activation(rms, rms, ACT.Sqrt).then_inc(s_rt_n, 1)
                if turn is None:
                    return
                if n == 0:
                    act.wait_ge(s_chan, 1)
                for b in range(4):
                    act.wait_ge(s_xt, 4 * turn + b + 1)
                    for k in (2 * b, 2 * b + 1):
                        act.activation(h_hi[:, k, :], split3(bank(b), 2)[:, k % 2, :], ACT.Copy,
                                       scale=chan[:, row + k:row + k + 1]).then_inc(s_hhi, 1)

            for r, v in ((R_N1, norm1_g), (R_N2, norm2_g), (R_NMIX, norm_mix_g_2),
                         (R_NFFN, norm_ffn_g_2), (R_NPLE, norm_ple_g_2), (R_BG, b_gate)):
                n = v.shape[1] // P
                act.dma_start(rows[r:r + n, :], v[0].rearrange("(r p) -> r p", p=P)).then_inc(s_rows, 16)
            act.dma_start(rows[R_CONV:R_CONV + 48, :],
                          conv_w[0].rearrange("k (c p) -> (k c) p", p=P)).then_inc(s_rows, 16)
            act.dma_start(rows[R_LB:R_LB + 8, :],
                          hg_lb_logits_2.rearrange("k (c p) -> (k c) p", p=P)).then_inc(s_rows, 16)
            for c, v in ((C_FIN, final_norm_g.unsqueeze(0)), (C_ALOG, a_log), (C_DT, dt_bias),
                         (C_ANORM, a_norm_g), (C_RB, b_router_group), (C_RB + 4, b_router_expert),
                         (C_ONORM, hg_onorm_g_2), (C_FB, fox_f_bias_2), (C_QN, fox_q_norm_g_2),
                         (C_KN, fox_k_norm_g_2)):
                act.dma_start(rep_row[0:1, c:c + v.shape[1]], v).then_inc(s_rep, 16)
            act.dma_start(freq_row[0:1, :], rope_freq).then_inc(s_rep, 16)
            with nc.allow_non_contiguous_dma("256 positions, one word each"):
                act.dma_start(pos_i[:, :], positions[0].rearrange("(t p) -> p t", p=P)).then_inc(s_pos, 16)
            act.dma_start(rt_raw[:, :, 0:4], w_router_group[0].rearrange("(k p) n -> p k n", p=P)).then_inc(s_rt, 16)
            act.dma_start(rt_raw[:, :, 4:20], w_router_expert[0].rearrange("(k p) n -> p k n", p=P)).then_inc(s_rt, 16)
            act.dma_start(rt_raw[:, :, 20:28],
                          wi2[:, TOK0_2 + Z2_F:GATE0_2].rearrange("(k p) n -> p k n", p=P)).then_inc(s_rt, 16)

            norm(0, 0, R_N1)
            ahead(0)
            act.wait_ge(s_trig, 1)
            act.activation(cs[:, :, :, :], cs[:, :, :, :], ACT.Sin).then_inc(s_sin, 1)

            def conv_silu(c):
                act.wait_ge(s_conv, c + 1)
                act.activation(y_t[:, 2 * c:2 * c + 2, :], y_t[:, 2 * c:2 * c + 2, :],
                               ACT.Silu).then_inc(s_silu_y, 1)

            for c in range(6):
                ahead(CONV[c])
                act.wait_ge(w_used, CONV[c] + 1)
                act.activation(z_t[:, 2 * c:2 * c + 2, 3:S + 3], split3(bank(c % 4), 2),
                               ACT.Copy).then_inc(s_conv_ev, 1)
                if c:
                    conv_silu(c - 1)
            conv_silu(5)
            act.wait_ge(s_rt, 48)
            act.activation(rt_hi[:, :, :], rt_raw[:, :, :], ACT.Copy).then_inc(s_rt_hi, 1)

            def tok_in(b):
                act.wait_ge(w_used, TOK[b][1] + 1)
                act.activation(z_tok[:, :, TOK_BLK * b:TOK_BLK * (b + 1)],
                               split3(bank(4 + 2 * (b % 2), 2), 2)[:, :, 0:TOK_BLK],
                               ACT.Copy).then_inc(s_tok_ev, 1)

            def softplus(n):
                act.wait_ge(s_spe, n + 1)
                act.activation(sp2, sp2, ACT.Exp).then_inc(s_spx, 1)
                act.wait_ge(s_spl, n + 1)
                act.activation(sp3, sp3, ACT.Ln).then_inc(s_spm, 1)

            def gate_out(G, c, dst, ev):
                act.wait_ge(w_used, G[c] + 1)
                act.activation(dst[:, 2 * c:2 * c + 2, :], split3(bank(6 + c % 2), 2),
                               ACT.Copy).then_inc(ev, 1)
                if c < 7:
                    ahead(G[c + 1])

            ahead(TOK[0][0])
            ahead(TOK[0][1])
            tok_in(0)
            ahead(TOK[1][0])
            for j in range(6):
                act.wait_ge(s_yt, j + 1)
                t, g = j // 3, j % 3
                act.activation(qkv[:, t, 512 * g:512 * g + 512], bank(j % 4), ACT.Copy).then_inc(s_qkv, 1)
            ahead(TOK[1][1])
            act.wait_ge(s_l2s, 1)
            act.activation(nrm, nrm, ACT.Sqrt).then_inc(s_l2r, 1)
            tok_in(1)
            ahead(TOK[2][0])
            act.wait_ge(s_tok_ev, 2)
            act.activation(beta, z_tok[:, :, Z_BETA:Z_BETA + 8], ACT.Sigmoid).then_inc(s_beta, 1)
            softplus(0)
            act.activation(alog, rep[:, C_ALOG:C_ALOG + 8], ACT.Exp).then_inc(s_spm, 1)
            ahead(TOK[2][1])
            tok_in(2)
            ahead(TOK[3][0])
            act.wait_ge(s_gsum, 1)
            act.activation(small[:, 96:128], bank(2)[:, 0:32], ACT.Exp).then_inc(s_eg, 1)
            tok_in(3)
            ahead(TOK[3][1])

            def turned(dst, n, first_bank, sig, done):
                for j in range(n):
                    act.wait_ge(sig, j + 1)
                    act.activation(dst(j), bank(first_bank(j)), ACT.Copy).then_inc(done, 1)

            def head_tile(j):
                if j == 6:
                    return q_dec_t.rearrange("p a b -> p (a b)")
                return (q_t, k_t, kb_t)[j // 2][j % 2].rearrange("p a b -> p (a b)")
            turned(head_tile, 7, lambda j: j % 6, s_heads_ps, s_heads)
            act.activation(z_tok[:, :, Z_Z:Z_Z + 512], z_tok[:, :, Z_Z:Z_Z + 512],
                           ACT.Silu).then_inc(s_zs, 1)
            ahead(GATE[0])
            gate_out(GATE, 0, gate, s_gate_ev)

            def decays(gr):
                for t in range(NT):
                    act.wait_ge(s_dps, 2 * gr + t + 1)
                    act.activation(dec[:, t].rearrange("p a b -> p (a b)"), bank(t),
                                   ACT.Exp).then_inc(s_dexp, 1)

            decays(0)
            for gr in range(2):
                gate_out(GATE, gr + 1, gate, s_gate_ev)
                for t in range(NT):
                    act.wait_ge(s_inv0_ps, 2 * gr + t + 1)
                    act.activation(inv[:, t].rearrange("p a b -> p (a b)"), bank(t),
                                   ACT.Copy).then_inc(s_inv0_ev, 1)
                for n in range(1, len(LEVELS)):
                    for t in range(NT):
                        act.wait_ge(s_prod_ps, 12 * gr + 2 * (n - 1) + t + 1)
                        if n >= 2 or gr:
                            act.wait_ge(s_dinv, 12 * gr + 2 * (n - 2) + t + 1)
                        act.activation(prod[:, t].rearrange("p a b -> p (a b)"), bank(t),
                                       ACT.Copy).then_inc(s_prod, 1)
                act.wait_ge(s_wt_ps, gr + 1)
                act.activation(w_t.rearrange("p a b -> p (a b)"), bank(2)[:, 0:256], ACT.Copy,
                               scale=-1.0).then_inc(s_wt, 1)
                act.wait_ge(s_u0, gr + 1)
                act.activation(v_new[:, 0, 256 * gr:256 * gr + 256], bank(3)[:, 0:256],
                               ACT.Copy).then_inc(s_v0, 1)
                act.wait_ge(s_st_ps, gr + 1)
                act.activation(state.rearrange("p a b -> p (a b)"), bank(4)[:, 0:128],
                               ACT.Copy).then_inc(s_st, 1)
                act.wait_ge(s_u1, gr + 1)
                for odd, b in ((0, 5), (1, 3)):
                    dst = v_new[:, 1, 256 * gr:256 * gr + 256].rearrange("p (a b d) -> p a b d", a=2, b=2)
                    act.activation(dst[:, :, odd, :], split3(bank(b)[:, 0:128], 2), ACT.Copy).then_inc(s_v1, 1)
                if gr == 0:
                    decays(1)
                act.wait_ge(s_o_ps, gr + 1)
                act.activation(o_tok[:, 0, 256 * gr:256 * gr + 256], bank(2)[:, 0:256],
                               ACT.Copy).then_inc(s_o, 1)
                for odd, b in ((0, 4), (1, 5)):
                    dst = o_tok[:, 1, 256 * gr:256 * gr + 256].rearrange("p (a b d) -> p a b d", a=2, b=2)
                    act.activation(dst[:, :, odd, :], split3(bank(b)[:, 0:128], 2), ACT.Copy).then_inc(s_o, 1)

            def out_high(n, first_bank):
                for b in range(2):
                    act.wait_ge(s_ot_ps, 2 * n + b + 1)
                    act.activation(o_hi[:, 2 * b:2 * b + 2, :], split3(bank(first_bank + b), 2),
                                   ACT.Copy).then_inc(s_ohi, 1)

            for j in range(6):
                act.wait_ge(s_ro_ps, j + 1)
                n = 2 if j < 5 else 1
                act.activation(ro_t[:, 2 * j:2 * j + n, :], split3(bank(j), 2)[:, 0:n, :],
                               ACT.Copy).then_inc(s_ro, 1)
            gate_out(GATE, 3, gate, s_gate_ev)
            act.wait_ge(s_ors, 1)
            act.activation(nrm[:, :, 0:8], nrm[:, :, 0:8], ACT.Sqrt).then_inc(s_orr, 1)
            for j in range(6):
                act.wait_ge(s_rel_ps, j + 1)
                t, hs = by_keys(j)
                act.activation(rel[:, t, hs, 0:P * (t + 1)], split3(bank(j), 4 if j < 2 else 2), ACT.Relu).then_inc(s_rel, 1)
            gate_out(GATE, 4, gate, s_gate_ev)
            out_high(0, 0)
            gate_out(GATE, 5, gate, s_gate_ev)
            gate_out(GATE, 6, gate, s_gate_ev)

            def exps(prb, src, scale, base):
                for t in range(NT):
                    act.wait_ge(s_nmx, base + t + 1)
                    for h in range(HEADS):
                        act.activation(prb[:, t, h, 0:P * (t + 1)], src(t, h), ACT.Exp,
                                       bias=nmx[:, t, h:h + 1], scale=scale,
                                       accum_out=den[:, t, h:h + 1]).then_inc(s_exp, 1)

            def prob_tiles(dst, base):
                for j in range(6):
                    act.wait_ge(s_pt_ps, base + j + 1)
                    act.activation(dst[:, 4 * j:4 * j + 4, :].rearrange("p a b -> p (a b)"),
                                   bank(j), ACT.Copy).then_inc(s_pt, 1)

            def attention_high(base):
                for b in range(2):
                    act.wait_ge(s_pv_ps, base + b + 1)
                    act.activation(o_hi[:, 4 + 2 * b:6 + 2 * b, :], split3(bank(2 + b), 2),
                                   ACT.Copy).then_inc(s_pv_hi, 1)

            exps(prob, lambda t, h: prob[:, t, h, 0:P * (t + 1)], HD ** -0.5, 0)
            gate_out(GATE, 7, gate, s_gate_ev)
            prob_tiles(prob_t, 0)
            attention_high(0)

            ahead(PROJ[0][0])
            act.wait_ge(s_gate_ev, 8)
            for c in range(16):
                act.activation(gate[:, c, :], gate[:, c, :], ACT.Sigmoid,
                               bias=chan[:, R_BG + c:R_BG + c + 1]).then_inc(s_gate, 1)

            def merge_high(PR, first):
                for c in range(2):
                    ahead(PR[c][0])
                    ahead(PR[c][1])
                    act.wait_ge(s_merge, first + c + 1)
                    act.activation(h_hi[:, 4 * c:4 * c + 4, :], ga, ACT.Copy).then_inc(s_merge_hi, 1)

            def keep(ch):
                for c in ch:
                    for i in c:
                        ahead(i)

            def ffn(F, first, routed):
                for e in range(len(F)):
                    ahead(F[e][0])
                    act.wait_ge(w_used, F[e][0] + 1)
                    act.activation(act_s[:, e % 2], split3(bank(4 + 2 * (e % 2)), 2),
                                   ACT.Silu).then_inc(s_silu, 1)
                    ahead(F[e][1])
                    if e == 0 and routed:
                        ahead(F[1][1])
                        act.wait_ge(s_ct_ps, 1)
                        act.activation(comb_t[0:16, :], bank(1)[0:16, 0:S], ACT.Copy).then_inc(s_ct, 1)
                        for b in range(8):
                            act.wait_ge(s_cr_ps, b + 1)
                            act.activation(comb_rep[:, 2 * b:2 * b + 2, :], split3(bank(b % 4), 2),
                                           ACT.Copy).then_inc(s_cr, 1)
                    act.wait_ge(s_prod2, first + e + 1)
                    b = 2 * (e % 2)
                    act.activation(o_hi[:, b:b + 2, :], act_p[:, e % 2], ACT.Copy).then_inc(s_ahi, 1)
                ahead(F[-1][2])

            merge_high(PROJ, 0)
            keep(OUT)
            norm(1, 1, R_N2)
            ahead(EXP[0][1])
            act.wait_ge(s_rlm, 1)
            act.activation(rl[:, :, 0:4], rl[:, :, 0:4], ACT.Exp).then_inc(s_rle, 1)
            act.wait_ge(s_rlm, 2)
            act.activation(el, el, ACT.Exp).then_inc(s_rle, 1)
            ffn(EXP, 0, True)
            norm(2, None, None)

            norm(3, 2, R_NMIX)
            for c in range(4):
                ahead(HGQF[c])
                act.wait_ge(w_used, HGQF[c] + 1)
                dst = (hq if c < 2 else hk).rearrange("p a b -> p (a b)")[:, 512 * (c % 2):512 * (c % 2) + 512]
                act.activation(dst, bank(c), ACT.Silu if c < 2 else ACT.Sigmoid).then_inc(s_hev, 1)
            act.wait_ge(s_lbs, 1)
            act.activation(small[:, 384:392], small[:, 384:392], ACT.Exp).then_inc(s_lbe, 1)
            act.wait_ge(s_fg, 1)
            act.activation(hd, hk, ACT.Ln).then_inc(s_logf, 1)

            def tok_out(b):
                act.wait_ge(w_used, TOK2[b][1] + 1)
                act.activation(z2[:, :, 512 * b:512 * b + 512], split3(bank(4 + 2 * (b % 2), 2), 2),
                               ACT.Copy).then_inc(s_tok_ev, 1)

            ahead(TOK2[0][0])
            ahead(TOK2[0][1])
            tok_out(0)
            act.wait_ge(s_tok_ps, 1)
            act.activation(z2[:, :, Z2_F:Z2_F + 8], split3(bank(6)[:, 0:16], 2),
                           ACT.Copy).then_inc(s_ff, 1)
            for n in range(len(LEVELS)):
                act.wait_ge(s_hd, n + 1)
                act.activation(he, hd, ACT.Exp).then_inc(s_he, 1)
                ahead(LVL2[n])
                if n in (2, 4, 6):
                    tok_out(n // 2)
            act.wait_ge(s_hio, 1)
            act.activation(he, he, ACT.Exp).then_inc(s_hie, 1)
            softplus(1)
            ahead(LVL2[7])
            tok_out(4)
            act.wait_ge(s_hkt_ps, 1)
            act.activation(hkd_t.rearrange("p a b -> p (a b)"), bank(0), ACT.Copy).then_inc(s_hkt, 1)
            ahead(GATE2[0])
            act.wait_ge(s_l2s, 2)
            act.activation(nrm2, nrm2, ACT.Sqrt).then_inc(s_l2r, 1)
            act.wait_ge(s_hs_ps, 1)
            act.activation(hs0.rearrange("p a b -> p (a b)"), bank(1), ACT.Copy).then_inc(s_hs, 1)
            gate_out(GATE2, 0, gate2, s_gate_ev2)
            act.wait_ge(s_ho_ps, 1)
            act.activation(ho, split3(bank(2, 2), 2), ACT.Copy).then_inc(s_ho, 1)
            gate_out(GATE2, 1, gate2, s_gate_ev2)
            act.wait_ge(s_ors, 2)
            act.activation(nrm[:, :, 0:4], nrm[:, :, 0:4], ACT.Sqrt).then_inc(s_orr, 1)
            act.activation(z2[:, :, Z2_G:Z2_G + 512], z2[:, :, Z2_G:Z2_G + 512],
                           ACT.Silu).then_inc(s_zs, 1)
            for j in range(4):
                act.wait_ge(s_fq_ps, j + 1)
                act.activation(qk2_t[:, 2 * j:2 * j + 2, :], split3(bank((4, 5, 0, 1)[j]), 2),
                               ACT.Copy).then_inc(s_fq, 1)
            gate_out(GATE2, 2, gate2, s_gate_ev2)
            out_high(1, 2)
            gate_out(GATE2, 3, gate2, s_gate_ev2)
            gate_out(GATE2, 4, gate2, s_gate_ev2)

            def logits_in_psum(t, h):
                b, n = key_bank(t, h)
                return split3(bank(b), 4 if t == 0 else 2)[:, n, :]
            exps(prob2, logits_in_psum, 1.0, 2)
            gate_out(GATE2, 5, gate2, s_gate_ev2)
            gate_out(GATE2, 6, gate2, s_gate_ev2)
            prob_tiles(prob2_t, 6)
            gate_out(GATE2, 7, gate2, s_gate_ev2)
            attention_high(2)
            ahead(PROJ2[0][0])
            act.wait_ge(s_gate_ev2, 8)
            act.activation(gate2[:, :, :], gate2[:, :, :], ACT.Sigmoid).then_inc(s_gate, 16)
            merge_high(PROJ2, 2)
            keep(OUT2)
            norm(4, 3, R_NFFN)
            act.dma_start(p_tok, p_2[0, 0].rearrange("(t p) d -> p t d", p=P)).then_inc(s_p, 16)
            ffn(FFN, N_EXP, False)
            norm(5, 4, R_NPLE)
            act.wait_ge(s_p_ps, 1)
            act.activation(o_hi[:, 0:2, :], split3(bank(4), 2), ACT.Copy).then_inc(s_p_hi, 1)
            for c in range(2):
                ahead(PLEG[c][0])
                ahead(PLEG[c][1])
                act.wait_ge(w_used, PLEG[c][1] + 1)
                act.activation(res[:, :, 512 * c:512 * c + 512], split3(bank(2 * c, 2), 2),
                               ACT.Sigmoid).then_inc(s_plg, 1)

        @block.tensor
        def _(pe):
            def chunk(i):
                pe.wait_ge(w_ready, i + 1)
                _, kt, n = chunks[i]
                return [w[:, i % SPL, 0:kt * n].rearrange("p (k n) -> p k n", k=kt) for w in (w_hi, w_lo)]

            def weights_still(i, outs, a_hi, a_lo):
                hi, lo = chunk(i)
                kt = chunks[i][1]
                for c, o in enumerate(outs):
                    cols = slice(P * c, P * c + P)
                    for k in range(kt):
                        pe.matmul(o, hi[:, k, cols], a_hi[:, k, :], start=(k == 0), stop=False)
                        pe.matmul(o, hi[:, k, cols], a_lo[:, k, :], start=False, stop=False)
                        last_mm = pe.matmul(o, lo[:, k, cols], a_hi[:, k, :], start=False,
                                            stop=(k == kt - 1))
                last_mm.then_inc(w_used, 1)

            def weights_move(i, outs, a_hi, a_lo, first, end):
                hi, lo = chunk(i)
                kt, n = chunks[i][1:]
                for (t, c), o in outs.items():
                    tok = slice(P * t, P * t + P)
                    cols = slice(512 * c, min(n, 512 * c + 512))
                    for k in range(kt):
                        pe.matmul(o, a_hi[:, k, tok], hi[:, k, cols], start=(first and k == 0), stop=False)
                        pe.matmul(o, a_hi[:, k, tok], lo[:, k, cols], start=False, stop=False)
                        last_mm = pe.matmul(o, a_lo[:, k, tok], hi[:, k, cols], start=False,
                                            stop=(end and k == kt - 1))
                last_mm.then_inc(w_used, 1)

            def turn_x(turn):
                pe.wait_ge(s_xn, turn + 1)
                for b in range(4):
                    for k in (2 * b, 2 * b + 1):
                        for t in range(NT):
                            m = pe.transpose(split3(bank(b), 2)[:, k % 2, P * t:P * t + P],
                                             xn[:, t, P * k:P * k + P], ident[:, :])
                    m.then_inc(s_xt, 1)
                pe.wait_ge(s_h, 8 * (turn + 1))

            pe.wait_ge(s_const, 11)
            pe.wait_ge(s_rows, 128)
            pe.transpose(bank(7)[:, 0:R_ALL], rows[:, :], ident[0:R_ALL, 0:R_ALL]).then_inc(s_chan_ps, 1)
            pe.wait_ge(s_rep, 176)
            for c in range(3):
                n = min(512, C_ALL - 512 * c)
                m = pe.matmul(bank(4 + c)[:, 0:n], ones[0:1, :], rep_row[0:1, 512 * c:512 * c + n],
                              start=True, stop=True)
            m.then_inc(s_rep_ps, 1)
            pe.matmul(bank(6)[:, 400:432], ones[0:1, :], freq_row[0:1, :], start=True,
                      stop=True).then_inc(s_rep_ps, 1)
            turn_x(0)

            for c in range(6):
                if c >= 4:
                    pe.wait_ge(s_conv_ev, c - 3)
                b = split3(bank(c % 4), 2)
                weights_still(CONV[c], [b[:, 0, :], b[:, 1, :]], h_hi, h_lo)

            def tok_block(T, b, width, base):
                if base + b >= 2:
                    pe.wait_ge(s_tok_ev, base + b - 1)
                outs = {(t, 0): bank(4 + 2 * (b % 2) + t)[:, 0:width] for t in range(NT)}
                weights_move(T[b][0], outs, h_hi, h_lo, True, False)
                weights_move(T[b][1], outs, h_hi[:, 4:8], h_lo[:, 4:8], False, True)

            def gate_chunk(G, c, ev):
                if c >= 2:
                    pe.wait_ge(ev, c - 1)
                b = split3(bank(6 + c % 2), 2)
                weights_still(G[c], [b[:, 0, :], b[:, 1, :]], h_hi, h_lo)

            def turn_y(js):
                for j in js:
                    if j >= 4:
                        pe.wait_ge(s_qkv, j - 3)
                    t, g = j // 3, j % 3
                    for c in range(4):
                        m = pe.transpose(bank(j % 4)[:, P * c:P * c + P],
                                         y_t[:, 4 * g + c, P * t:P * t + P], ident[:, :])
                    m.then_inc(s_yt, 1)

            pe.wait_ge(s_chan, 5)
            tok_block(TOK, 0, TOK_BLK, 0)
            pe.wait_ge(s_silu_y, 6)
            pe.wait_ge(s_conv_ev, 6)
            turn_y(range(4))
            outs = {(t, 0): bank(6 + t)[:, 0:TOK_BLK] for t in range(NT)}
            weights_move(TOK[1][0], outs, h_hi, h_lo, True, False)
            turn_y(range(4, 6))
            weights_move(TOK[1][1], outs, h_hi[:, 4:8], h_lo[:, 4:8], False, True)
            tok_block(TOK, 2, TOK_BLK, 0)
            pe.wait_ge(s_glog, 1)
            pe.wait_ge(s_qkv, 3)
            for n, mask in enumerate((upto, after)):
                for t in range(NT):
                    o = 16 * n + 8 * t
                    m = pe.matmul(bank(2)[:, o:o + 8], mask[:, :], glog[:, t, :], start=True, stop=True)
            m.then_inc(s_gsum, 1)
            tok_block(TOK, 3, TOK_BLK, 0)
            pe.wait_ge(s_qn, 1)
            pe.wait_ge(s_qkv, 6)
            pe.wait_ge(s_eg, 1)
            pe.wait_ge(s_tok_ev, 3)
            for j in range(6):
                for c in range(4):
                    pair, t = 2 * (j % 2) + c // 2, c % 2
                    src = (qkv[:, t, P * pair:P * pair + P], qkv[:, t, 512 + P * pair:640 + P * pair],
                           k_b[:, t, P * pair:P * pair + P])[j // 2]
                    m = pe.transpose(bank(j)[:, P * c:P * c + P], src, ident[:, :])
                m.then_inc(s_heads_ps, 1)
            pe.wait_ge(s_qn, 2)
            pe.wait_ge(s_heads, 1)
            for c in range(4):
                m = pe.transpose(bank(0)[:, P * c:P * c + P], q_dec[:, P * c:P * c + P], ident[:, :])
            m.then_inc(s_heads_ps, 1)
            pe.wait_ge(s_tok_ev, N_TOK_BLK)
            gate_chunk(GATE, 0, s_gate_ev)

            def head(tile, h, t):
                r = 64 * (h % 2)
                return tile[h // 4][r:r + 64, h // 2 % 2, P * t:P * t + P]

            def decays(gr):
                pe.wait_ge(s_gmask, gr + 1)
                for t in range(NT):
                    for u in range(4):
                        m = pe.matmul(bank(t)[:, P * u:P * u + P], g_mask[:, t, u, :], upto[:, :],
                                      start=True, stop=True)
                    m.then_inc(s_dps, 1)

            pe.wait_ge(s_heads, 7)
            decays(0)
            for gr in range(2):
                if gr:
                    pe.wait_ge(s_o, 3 * gr)
                for n, right in enumerate((kb_t, q_t)):
                    for odd in range(2):
                        for t in range(NT):
                            for pl in range(2):
                                h = 4 * gr + 2 * pl + odd
                                o = bank(2 + 2 * n + odd)[:, P * (2 * t + pl):P * (2 * t + pl) + P]
                                m = pe.matmul(o, head(k_t, h, t), head(right, h, t), start=True, stop=True)
                m.then_inc(s_kkqk, 1)
                gate_chunk(GATE, gr + 1, s_gate_ev)
                pe.wait_ge(s_inv0, gr + 1)
                for t in range(NT):
                    for u in range(4):
                        m = pe.transpose(bank(t)[:, P * u:P * u + P], inv_t[:, t, u, :], ident[:, :])
                    m.then_inc(s_inv0_ps, 1)
                for n in range(1, len(LEVELS)):
                    for t in range(NT):
                        pe.wait_ge(s_lev, 12 * gr + 2 * (n - 1) + t + 1)
                        if n == 1:
                            pe.wait_ge(s_inv0_ev, 2 * gr + t + 1)
                        else:
                            pe.wait_ge(s_inv, 12 * gr + 2 * (n - 2) + t + 1)
                            pe.wait_ge(s_prod, 12 * gr + 2 * (n - 2) + t + 1)
                        for u in range(4):
                            m = pe.matmul(bank(t)[:, P * u:P * u + P], lev[:, t, u, :],
                                          inv[:, t, u, :], start=True, stop=True)
                        m.then_inc(s_prod_ps, 1)
                    for t in range(NT):
                        pe.wait_ge(s_prod, 12 * gr + 2 * (n - 1) + t + 1)
                        for u in range(4):
                            if n < len(LEVELS) - 1:
                                pe.matmul(bank(2 + t)[:, P * u:P * u + P], inv_t[:, t, u, :],
                                          prod[:, t, u, :], start=True, stop=True)
                        for u in range(4):
                            m = pe.matmul(bank(4 + t)[:, P * u:P * u + P], prod[:, t, u, :],
                                          inv_t[:, t, u, :], start=True, stop=True)
                        m.then_inc(s_dinv, 1)
                pe.wait_ge(s_inv, 12 * gr + 12)
                for u in range(4):
                    h = 4 * gr + u
                    m = pe.matmul(bank(2)[64 * (h % 2):64 * (h % 2) + 64, P * (u // 2):P * (u // 2) + P],
                                  kb_g[:, HD * h:HD * h + HD], inv_t[:, 1, u, :], start=True, stop=True)
                m.then_inc(s_wt_ps, 1)
                for u in range(4):
                    h = 4 * gr + u
                    m = pe.matmul(bank(3)[:, HD * u:HD * u + HD], inv_t[:, 0, u, :],
                                  v_b[:, 0, HD * h:HD * h + HD], start=True, stop=True)
                m.then_inc(s_u0, 1)
                pe.wait_ge(s_v0, gr + 1)
                for u in range(4):
                    h = 4 * gr + u
                    m = pe.matmul(bank(4)[64 * (h % 2):64 * (h % 2) + 64, HD * (u // 2):HD * (u // 2) + HD],
                                  k_dec[:, HD * h:HD * h + HD], v_new[:, 0, HD * h:HD * h + HD],
                                  start=True, stop=True)
                m.then_inc(s_st_ps, 1)
                pe.wait_ge(s_st, gr + 1)
                pe.wait_ge(s_wt, gr + 1)
                for u in range(4):
                    h = 4 * gr + u
                    r = 64 * (h % 2)
                    o = bank(5 if r == 0 else 3)[:, HD * (u // 2):HD * (u // 2) + HD]
                    pe.matmul(o, inv_t[:, 1, u, :], v_b[:, 1, HD * h:HD * h + HD], start=True, stop=False)
                    m = pe.matmul(o, w_t[r:r + 64, u // 2, :], state[r:r + 64, u // 2, :],
                                  start=False, stop=True)
                m.then_inc(s_u1, 1)
                if gr == 0:
                    decays(1)
                for u in range(4):
                    h = 4 * gr + u
                    pe.matmul(bank(2)[:, HD * u:HD * u + HD], qk_t[:, 0, u, :],
                              v_new[:, 0, HD * h:HD * h + HD], start=True, stop=True)
                pe.wait_ge(s_v1, 2 * gr + 2)
                for u in range(4):
                    h = 4 * gr + u
                    r = 64 * (h % 2)
                    o = bank(4 if r == 0 else 5)[:, HD * (u // 2):HD * (u // 2) + HD]
                    pe.matmul(o, q_dec_t[r:r + 64, h // 2, :], state[r:r + 64, u // 2, :],
                              start=True, stop=False)
                    m = pe.matmul(o, qk_t[:, 1, u, :], v_new[:, 1, HD * h:HD * h + HD],
                                  start=False, stop=True)
                m.then_inc(s_o_ps, 1)

            def turn_out(o, first_bank):
                for b in range(2):
                    for c in (2 * b, 2 * b + 1):
                        for t in range(NT):
                            m = pe.transpose(split3(bank(first_bank + b), 2)[:, c % 2, P * t:P * t + P],
                                             o[:, t, P * c:P * c + P], ident[:, :])
                    m.then_inc(s_ot_ps, 1)
            pe.wait_ge(s_roped, 1)
            pe.wait_ge(s_o, 6)
            for j in range(6):
                for c in range(2 if j < 5 else 1):
                    b = 2 * j + c
                    for t in range(NT):
                        if b < 4:
                            src = z_tok[:, t, Z_BQ + P * b:Z_BQ + P * b + P]
                        elif b < 6:
                            src = k_dup[:, t, b - 4].rearrange("p a b -> p (a b)")
                        elif b < 10:
                            src = z_tok[:, t, Z_IQ + P * (b - 6):Z_IQ + P * (b - 6) + P]
                        else:
                            src = ik_dup[:, t].rearrange("p a b -> p (a b)")
                        m = pe.transpose(split3(bank(j), 2)[:, c, P * t:P * t + P], src, ident[:, :])
                m.then_inc(s_ro_ps, 1)
            gate_chunk(GATE, 3, s_gate_ev)
            pe.wait_ge(s_ro, 6)
            for j in range(6):
                t = by_keys(j)[0]
                hs = heads_of(j)
                for n, h in enumerate(hs):
                    r = 64 * (h % 2)
                    m = pe.matmul(split3(bank(j), len(hs))[:, n, :], ro_t[r:r + 64, 6 + h // 2, P * t:P * t + P],
                                  ro_t[r:r + 64, 10, 0:P * (t + 1)], start=True, stop=True)
                m.then_inc(s_rel_ps, 1)
            gate_chunk(GATE, 4, s_gate_ev)
            pe.wait_ge(s_on, 1)
            pe.wait_ge(s_rel, 6)
            turn_out(o_tok, 0)
            gate_chunk(GATE, 5, s_gate_ev)
            pe.wait_ge(s_o_ready, 2)
            for j in range(6):
                t = by_keys(j)[0]
                hs = heads_of(j)
                for n, h in enumerate(hs):
                    r = 64 * (h % 2)
                    m = pe.matmul(split3(bank(j), len(hs))[:, n, :],
                                  ro_t[r:r + 64, h // 2, P * t:P * t + P],
                                  ro_t[r:r + 64, 4 + h // 4, 0:P * (t + 1)], start=True, stop=True)
                m.then_inc(s_log_ps, 1)
            gate_chunk(GATE, 6, s_gate_ev)
            gate_chunk(GATE, 7, s_gate_ev)

            def turn_probs(prb, base):
                for j in range(6):
                    pe.wait_ge(s_prob, base + (1 if j < 2 else 2))
                    for c in range(4):
                        n = 4 * j + c
                        src = prb[:, 0, n, 0:P] if j < 2 else prb[:, 1, (n - 8) // 2, P * (n % 2):P * (n % 2) + P]
                        m = pe.transpose(bank(j)[:, P * c:P * c + P], src, ident[:, :])
                    m.then_inc(s_pt_ps, 1)

            def prob_times_v(prb_t, v, base):
                pe.wait_ge(s_pt, base + 6)
                for b in range(2):
                    for h in range(4 * b, 4 * b + 4):
                        r = 64 * (h % 2)
                        for t in range(NT):
                            o = split3(bank(2 + b), 2)[r:r + 64, (h // 2) % 2, P * t:P * t + P]
                            for s in range(t + 1):
                                m = pe.matmul(o, v(s, h), prb_t[:, h if t == 0 else 8 + 2 * h + s, :],
                                              start=(s == 0), stop=(s == t))
                    m.then_inc(s_pv_ps, 1)

            pe.wait_ge(s_msk, 6)
            turn_probs(prob, 0)
            prob_times_v(prob_t, lambda s, h: z_tok[:, s, Z_BV + HD * (h // 4):Z_BV + HD * (h // 4) + HD], 0)

            def mix(PR, OU, n, gates_out):
                for c in range(2):
                    if c == 1:
                        gates_out()
                    for j in range(2):
                        if c == 0 and j == 1:
                            pe.wait_ge(s_bout, 2 * n + 2)
                        outs = [split3(bank(4 * c + 2 * j + q // 2), 2)[:, q % 2, :] for q in range(4)]
                        weights_still(PR[c][j], outs, o_hi[:, 4 * j:4 * j + 4], o_lo[:, 4 * j:4 * j + 4])
                pe.wait_ge(s_merged, 2 * n + 1)
                for c in range(2):
                    outs = {(t, 0): bank(2 * c + t) for t in range(NT)}
                    for k in range(2):
                        if k == 1:
                            pe.wait_ge(s_merged, 2 * n + 2)
                        weights_move(OU[c][k], outs, h_hi[:, 4 * k:4 * k + 4], h_lo[:, 4 * k:4 * k + 4],
                                         k == 0, k == 1)

            mix(PROJ, OUT, 0, lambda: pe.wait_ge(s_gate_ev, 8))
            turn_x(1)

            pe.wait_ge(s_rt_lo, 1)
            for t in range(NT):
                tok = slice(P * t, P * t + P)
                for k in range(KD):
                    o = bank(0)[:, 20 * t:20 * t + 20]
                    pe.matmul(o, h_hi[:, k, tok], rt_hi[:, k, 0:20], start=(k == 0), stop=False)
                    pe.matmul(o, h_hi[:, k, tok], rt_lo[:, k, 0:20], start=False, stop=False)
                    m = pe.matmul(o, h_lo[:, k, tok], rt_hi[:, k, 0:20], start=False, stop=(k == KD - 1))
            m.then_inc(s_rl_ps, 1)
            def spread_router():
                pe.wait_ge(s_comb, 1)
                for t in range(NT):
                    m = pe.transpose(bank(1)[0:16, P * t:P * t + P], comb[:, t, :], ident[:, :])
                m.then_inc(s_ct_ps, 1)
                pe.wait_ge(s_ct, 1)
                pe.wait_ge(s_sel, 1)
                for b in range(8):
                    if b >= 4:
                        pe.wait_ge(s_cr, b - 3)
                    for c in range(2):
                        m = pe.matmul(split3(bank(b % 4), 2)[:, c, :], sel_e[0:16, 2 * b + c, :],
                                      comb_t[0:16, :], start=True, stop=True)
                    m.then_inc(s_cr_ps, 1)

            def ffn(F, first, early):
                for e in range(len(F) + 1):
                    if e < len(F):
                        if e >= 2:
                            pe.wait_ge(s_prod2, first + e - 1)
                        for j in range(2):
                            b = split3(bank(4 + 2 * (e % 2) + j), 2)
                            weights_still(F[e][j], [b[:, 0, :], b[:, 1, :]], h_hi, h_lo)
                    if e == 1 and early:
                        spread_router()
                        pe.wait_ge(s_cr, 8)
                    if e >= 1:
                        pe.wait_ge(s_a, first + e)
                        b = 2 * ((e - 1) % 2)
                        outs = {(t, c): bank(2 * t + c) for t in range(NT) for c in range(2)}
                        weights_move(F[e - 1][2], outs, o_hi[:, b:b + 2], o_lo[:, b:b + 2],
                                         e == 1, e == len(F))

            ffn(EXP, 0, True)
            turn_x(2)

            for c in range(4):
                b = split3(bank(c), 2)
                weights_still(HGQF[c], [b[:, 0, :], b[:, 1, :]], h_hi, h_lo)
            tok_block(TOK2, 0, 512, N_TOK_BLK)
            for t in range(NT):
                tok = slice(P * t, P * t + P)
                for k in range(KD):
                    o = bank(6)[:, 8 * t:8 * t + 8]
                    pe.matmul(o, h_hi[:, k, tok], rt_hi[:, k, 20:28], start=(k == 0), stop=False)
                    pe.matmul(o, h_hi[:, k, tok], rt_lo[:, k, 20:28], start=False, stop=False)
                    m = pe.matmul(o, h_lo[:, k, tok], rt_hi[:, k, 20:28], start=False, stop=(k == KD - 1))
            m.then_inc(s_tok_ps, 1)
            pe.wait_ge(s_hev, 4)
            pe.wait_ge(s_fg, 2)
            for n in range(len(LEVELS) + 1):
                if n:
                    pe.wait_ge(s_hx, n)
                if n >= 2:
                    pe.wait_ge(s_hsc, n - 1)
                for u in range(8):
                    b = bank(2 * (n % 2) + u // 4)[:, P * (u % 4):P * (u % 4) + P]
                    left, right = (hk[:, u, :], hq[:, u, :]) if n == 0 else (hx[:, n % 2, u, :],) * 2
                    m = pe.matmul(b, left, right, start=True, stop=True)
                m.then_inc(s_hsc_ps, 1)
                b, k = 1 + n // 2, n % 2
                if n == 0:
                    pe.wait_ge(s_ff, 1)
                elif k == 0:
                    pe.wait_ge(s_tok_ev, N_TOK_BLK + b - 1)
                outs = {(t, 0): bank(4 + 2 * (b % 2) + t) for t in range(NT)}
                weights_move(LVL2[n], outs, h_hi[:, 4 * k:4 * k + 4], h_lo[:, 4 * k:4 * k + 4],
                             k == 0, k == 1)

            pe.wait_ge(s_hkd, 1)
            for h in range(HG_HEADS):
                m = pe.transpose(bank(0)[:, P * h:P * h + P], hkd[:, h, :], ident[:, :])
            m.then_inc(s_hkt_ps, 1)
            pe.wait_ge(s_tok_ev, N_TOK_BLK + 4)
            gate_chunk(GATE2, 0, s_gate_ev2)
            pe.wait_ge(s_hkt, 1)
            for h in range(HG_HEADS):
                m = pe.matmul(bank(1)[:, P * h:P * h + P], hkd_t[:, h, :],
                              z2[:, 0, Z2_I + P * h:Z2_I + P * h + P], start=True, stop=True)
            m.then_inc(s_hs_ps, 1)
            gate_chunk(GATE2, 1, s_gate_ev2)
            pe.wait_ge(s_hs, 1)
            pe.wait_ge(s_hsc, 8)
            for h in range(HG_HEADS):
                v = [z2[:, t, Z2_I + P * h:Z2_I + P * h + P] for t in range(NT)]
                pe.matmul(bank(2)[:, P * h:P * h + P], hsc[:, 2 * h, :], v[0], start=True, stop=True)
                pe.matmul(bank(3)[:, P * h:P * h + P], hqb[:, h, :], hs0[:, h, :], start=True, stop=False)
                m = pe.matmul(bank(3)[:, P * h:P * h + P], hsc[:, 2 * h + 1, :], v[1], start=False, stop=True)
            m.then_inc(s_ho_ps, 1)
            gate_chunk(GATE2, 2, s_gate_ev2)
            pe.wait_ge(s_qn, 3)
            pe.wait_ge(s_tok_ev, N_TOK_BLK + 5)
            for j in range(4):
                for c in range(4):
                    b, t = 2 * j + c // 2, c % 2
                    m = pe.transpose(bank((4, 5, 0, 1)[j])[:, P * c:P * c + P],
                                     z2[:, t, Z2_Q + P * b:Z2_Q + P * b + P], ident[:, :])
                m.then_inc(s_fq_ps, 1)
            gate_chunk(GATE2, 3, s_gate_ev2)
            pe.wait_ge(s_on, 2)
            turn_out(ho, 2)
            gate_chunk(GATE2, 4, s_gate_ev2)
            pe.wait_ge(s_fq, 4)
            pe.wait_ge(s_fmask, 1)
            pe.wait_ge(s_o_ready, 4)
            for j in range(6):
                t = by_keys(j)[0]
                hs = heads_of(j)
                for n, h in enumerate(hs):
                    r = 64 * (h % 2)
                    o = split3(bank(j), len(hs))[:, n, :]
                    pe.matmul(o, qk2_t[r:r + 64, h // 2, P * t:P * t + P],
                              qk2_t[r:r + 64, 4 + h // 2, 0:P * (t + 1)], start=True, stop=False)
                    if t == 1:
                        pe.matmul(o[:, 0:P], ones[:, :], f_mask[:, 0, h, :], start=False, stop=False)
                        pe.matmul(o[:, 0:P], upto[:, :], last(glog[:, 1, h], P),
                                  start=False, stop=False)
                    own = o[:, P * t:P * t + P]
                    pe.matmul(own, upto[:, :], f_mask[:, t, h, :], start=False, stop=False)
                    m = pe.matmul(own, ident_bf[:, :], future_bf[:, :], start=False, stop=True)
                m.then_inc(s_fl_ps, 1)
            gate_chunk(GATE2, 5, s_gate_ev2)
            gate_chunk(GATE2, 6, s_gate_ev2)
            turn_probs(prob2, 2)
            gate_chunk(GATE2, 7, s_gate_ev2)
            prob_times_v(prob2_t, lambda s, h: z2[:, s, Z2_V + HD * h:Z2_V + HD * h + HD], 6)
            mix(PROJ2, OUT2, 1, lambda: pe.wait_ge(s_gate_ev2, 8))
            turn_x(3)
            ffn(FFN, N_EXP, False)
            turn_x(4)
            pe.wait_ge(s_p, 16)
            for k in range(2):
                for t in range(NT):
                    m = pe.transpose(split3(bank(4), 2)[:, k, P * t:P * t + P],
                                     p_tok[:, t, P * k:P * k + P], ident[:, :])
            m.then_inc(s_p_ps, 1)
            for c in range(2):
                outs = {(t, 0): bank(2 * c + t) for t in range(NT)}
                weights_move(PLEG[c][0], outs, h_hi, h_lo, True, False)
                weights_move(PLEG[c][1], outs, h_hi[:, 4:8], h_lo[:, 4:8], False, True)
            pe.wait_ge(s_p_ready, 1)
            outs = {(t, c): bank(4 + 2 * c + t) for c in range(2) for t in range(NT)}
            weights_move(PLEP, outs, o_hi[:, 0:2], o_lo[:, 0:2], True, True)

        @block.vector
        def _(dve):
            n_dve, split_at = [0], [0]
            mult, add_, sub = ALU.mult, ALU.add, ALU.subtract

            def step(ins):
                n_dve[0] += 1
                ins.then_inc(s_dve, 1)
                dve.wait_ge(s_dve, n_dve[0])

            def mark(ins):
                n_dve[0] += 1
                ins.then_inc(s_dve, 1)
                return n_dve[0]

            def ahead(i):
                while split_at[0] <= min(i + SPL - 1, N_CH - 1):
                    j = split_at[0]
                    _, kt, n = chunks[j]
                    dve.wait_ge(w_high, j + 1)
                    dve.tensor_tensor(w_lo[:, j % SPL, 0:kt * n], raw[:, j % RAW, 0:kt * n],
                                      w_hi[:, j % SPL, 0:kt * n].bitcast(F32), sub).then_inc(w_ready, 1)
                    split_at[0] += 1

            def norm(n, turn, row):
                dve.wait_ge(s_sq, 2 * (n + 1))
                dve.tensor_scalar(rms, ssq, 1.0 / DM, EPS, mult, add_).then_inc(s_ms, 1)
                dve.wait_ge(s_rt_n, n + 1)
                step(dve.reciprocal(rstd, rms))
                if turn is None:
                    for t in range(NT):
                        dve.scalar_tensor_tensor(x_tok[:, t], x_tok[:, t], rstd[:, t:t + 1],
                                                 rep[:, C_FIN:C_FIN + DM], mult, mult)\
                           .then_inc(s_dve, 1)
                        n_dve[0] += 1
                    dve.wait_ge(s_dve, n_dve[0])
                    dve.nop().then_inc(s_x_ready, 1)
                    return
                for t in range(NT):
                    m = dve.tensor_scalar(xn[:, t], x_tok[:, t], rstd[:, t:t + 1], None, mult)
                m.then_inc(s_xn, 1)
                for b in range(4):
                    dve.wait_ge(s_hhi, 8 * turn + 2 * b + 2)
                    for k in (2 * b, 2 * b + 1):
                        dve.scalar_tensor_tensor(h_lo[:, k, :], split3(bank(b), 2)[:, k % 2, :],
                                                 chan[:, row + k:row + k + 1],
                                                 h_hi[:, k, :].bitcast(F32), mult, sub).then_inc(s_h, 1)

            dve.wait_ge(s_chan_ps, 1)
            dve.tensor_copy(chan[:, :], bank(7)[:, 0:R_ALL]).then_inc(s_chan, 1)
            dve.wait_ge(s_rep_ps, 2)
            for c in range(3):
                n = min(512, C_ALL - 512 * c)
                dve.tensor_copy(rep[:, 512 * c:512 * c + n], bank(4 + c)[:, 0:n]).then_inc(s_chan, 1)
            dve.tensor_copy(over[:, 0, :], bank(6)[:, 400:432]).then_inc(s_chan, 1)
            dve.wait_ge(s_chan, 5)
            norm(0, 0, R_N1)
            dve.wait_ge(s_pos, 16)
            step(dve.tensor_copy(pos_f[:, :], pos_i[:, :]))
            step(dve.tensor_tensor(cs[:, 1], last(pos_f[:, :], 32), mid(over[:, 0, :], 2), mult))
            magic = 12582912.0
            step(dve.tensor_scalar(turns, cs[:, 1], 0.15915494309189535, magic, mult, add_))
            step(dve.tensor_scalar(turns, turns, magic, None, sub))
            for part in (6.28125, 0.0019350051879882812, 3.0199159819567e-07):
                step(dve.scalar_tensor_tensor(cs[:, 1], turns, -part, cs[:, 1], mult, add_))
            step(dve.tensor_scalar(cs[:, 0], cs[:, 1], 1.5707963267948966, None, add_))
            step(dve.tensor_scalar(over, cs[:, 0], 3.141592653589793, -6.283185307179586,
                                   ALU.is_gt, mult))
            step(dve.tensor_tensor(cs[:, 0], cs[:, 0], over, add_))
            dve.tensor_scalar(cs[:, :, :, :], cs[:, :, :, :], 3.1415925, -3.1415925, ALU.min,
                              ALU.max).then_inc(s_trig, 1)
            ahead(0)

            step(dve.memset(z_t[:, :, 0:3], 0.0))
            for c in range(6):
                ahead(CONV[c])
                dve.wait_ge(s_conv_ev, c + 1)
                for k in range(4):
                    for ct in (2 * c, 2 * c + 1):
                        w = chan[:, R_CONV + 12 * k + ct:R_CONV + 12 * k + ct + 1]
                        taps = z_t[:, ct, k:k + S]
                        if k == 0:
                            m = dve.tensor_scalar(y_t[:, ct, :], taps, w, None, mult)
                        else:
                            dve.wait_ge(s_tap, 8 * c + 2 * (k - 1) + ct % 2 + 1)
                            m = dve.scalar_tensor_tensor(y_t[:, ct, :], taps, w, y_t[:, ct, :], mult, add_)
                        m.then_inc(s_tap, 1)
                dve.wait_ge(s_tap, 8 * c + 8)
                dve.nop().then_inc(s_conv, 1)
            ahead(TOK[0][0])
            ahead(TOK[0][1])
            dve.wait_ge(s_rt_hi, 1)
            dve.tensor_tensor(rt_lo[:, :, :], rt_raw[:, :, :], rt_hi[:, :, :].bitcast(F32),
                              sub).then_inc(s_rt_lo, 1)

            def softplus(n, ln_count):
                dve.scalar_tensor_tensor(sp2, sp1, -1.0, sp1, mult, ALU.min).then_inc(s_spe, 1)
                dve.wait_ge(s_spx, n + 1)
                dve.tensor_scalar(sp3, sp2, 1.0, None, add_).then_inc(s_spl, 1)
                dve.wait_ge(s_spm, ln_count)
                step(dve.scalar_tensor_tensor(sp1, sp1, 0.0, sp3, ALU.max, add_))

            ahead(TOK[1][0])
            dve.wait_ge(s_qkv, 6)
            step(dve.tensor_tensor(sq, qkv[:, :, 0:DM], qkv[:, :, 0:DM], mult))
            nrm_all = small[:, 128:160]
            step(dve.tensor_reduce(nrm_all, sq.rearrange("p t (h d) -> p (t h) d", d=HD), X, add_))
            dve.tensor_scalar(nrm_all, nrm_all, EPS, None, add_).then_inc(s_l2s, 1)
            ahead(TOK[1][1])
            dve.wait_ge(s_l2r, 1)
            step(dve.reciprocal(nrm_all, nrm_all))
            step(dve.tensor_scalar(nrm[:, :, 0:8], nrm[:, :, 0:8], HD ** -0.5, None, mult))
            for t in range(NT):
                heads = qkv[:, t, 0:DM].rearrange("p (h d) -> p h d", d=HD)
                m = mark(dve.tensor_tensor(heads, heads, last(nrm[:, t, :], HD), mult))
            dve.wait_ge(s_dve, m)
            ahead(TOK[2][0])
            dve.wait_ge(s_tok_ev, 2)
            step(dve.tensor_tensor(sp1, z_tok[:, :, Z_ALPHA:Z_ALPHA + 8],
                                   mid(rep[:, C_DT:C_DT + 8], 2), add_))
            softplus(0, 2)
            dve.scalar_tensor_tensor(glog, sp1, -1.0, mid(alog, 2), mult, mult).then_inc(s_glog, 1)
            ahead(TOK[2][1])
            dve.wait_ge(s_beta, 1)

            def h64(ap):
                return ap.rearrange("p (h d) -> p h d", d=HD)
            for t in range(NT):
                dve.tensor_tensor(h64(v_b[:, t]), h64(qkv[:, t, 1024:1536]), last(beta[:, t], HD), mult)
                m = dve.tensor_tensor(h64(k_b[:, t]), h64(qkv[:, t, 512:1024]), last(beta[:, t], HD), mult)
            m.then_inc(s_qn, 1)
            ahead(TOK[3][0])
            dve.wait_ge(s_eg, 1)
            dve.wait_ge(s_qn, 1)
            dve.tensor_tensor(h64(q_dec), h64(qkv[:, 1, 0:512]), last(e_g[:, 1], HD), mult)
            dve.tensor_tensor(h64(k_dec), h64(qkv[:, 0, 512:1024]), last(e_gl[:, 0], HD), mult)
            dve.tensor_tensor(h64(kb_g), h64(k_b[:, 1]), last(e_g[:, 1], HD), mult).then_inc(s_qn, 1)

            def rope(t, part):
                first, heads = ((Z_BQ, 10), (Z_IQ, 9))[part]
                v = h64(z_tok[:, t, first:first + HD * heads])
                a, b = v[:, :, 0:32], v[:, :, 32:64]
                cos, sin = (mid(cs[:, n, t, :], heads) for n in range(2))
                ta, tb = rt1[:, 0:heads], rt2[:, 0:heads]
                dve.tensor_tensor(ta, a, sin, mult)
                step(dve.tensor_tensor(tb, b, sin, mult))
                dve.tensor_tensor(a, a, cos, mult)
                step(dve.tensor_tensor(b, b, cos, mult))
                dve.tensor_tensor(a, a, tb, sub)
                step(dve.tensor_tensor(b, b, ta, add_))

            def decay_operand(gr):
                for t in range(NT):
                    m = dve.tensor_tensor(g_mask[:, t], mid(after[:, :], 4),
                                          last(glog[:, t, 4 * gr:4 * gr + 4], P), mult)
                m.then_inc(s_gmask, 1)

            dve.wait_ge(s_heads_ps, 6)
            dve.wait_ge(s_qn, 2)
            decay_operand(0)
            ahead(TOK[3][1])
            ahead(GATE[0])
            for gr in range(2):
                dve.wait_ge(s_dexp, 2 * gr + 2)
                d8, a8, p8, t8 = (v.rearrange("p t u i -> p (t u) i") for v in (dec, a_t, prod, inv_t))
                step(dve.tensor_tensor(d8, d8, mid(upto[:, :], 8), mult))
                dve.wait_ge(s_kkqk, gr + 1)
                for dst, first in ((qk_t, 4), (a_t, 2)):
                    for odd in range(2):
                        of = [v.rearrange("p t (a b) i -> p (t a) b i", b=2)[:, :, odd, :] for v in (dst, dec)]
                        m = dve.tensor_tensor(of[0], split3(bank(first + odd), 4), of[1], mult)
                m.then_inc(s_at, 1)
                dve.wait_ge(s_at, gr + 1)
                step(dve.tensor_tensor(p8, a8, mid(lvl[:, 0, :], 8), mult))
                step(dve.tensor_tensor(t8, mid(ident[:, :], 8), p8, sub))
                dve.nop().then_inc(s_inv0, 1)
                ahead(GATE[gr + 1])
                for n in range(1, len(LEVELS)):
                    for t in range(NT):
                        k = 12 * gr + 2 * (n - 1) + t + 1
                        if n == 1:
                            dve.wait_ge(s_inv0_ev, 2 * gr + t + 1)
                        dve.wait_ge(s_dinv, k)
                        if n < len(LEVELS) - 1:
                            dve.tensor_tensor(inv[:, t], inv[:, t], split3(bank(2 + t), 4), sub)
                        dve.tensor_tensor(inv_t[:, t], inv_t[:, t], split3(bank(4 + t), 4),
                                          sub).then_inc(s_inv, 1)
                        dve.wait_ge(s_inv, k)
                    if gr == 0 and n < 5:
                        if n == 1:
                            dve.wait_ge(s_sin, 1)
                            dve.wait_ge(s_tok_ev, N_TOK_BLK)
                        rope((n - 1) // 2, (n - 1) % 2)
                if gr == 0:
                    ahead(GATE[2])
                    decay_operand(1)

            def o_norm(o, o_sq, n, heads, dim, gain, z, middle):
                o3 = o.rearrange("p t (h d) -> p (t h) d", d=dim)
                dve.wait_ge(s_o if n == 0 else s_ho, 6 if n == 0 else 1)
                step(dve.tensor_tensor(o_sq, o, o, mult))
                nr = nrm[:, :, 0:heads]
                step(dve.tensor_reduce(nr, o_sq.rearrange("p t (h d) -> p t h d", d=dim), X, add_))
                dve.tensor_scalar(nr, nr, 1.0 / dim, EPS, mult, add_).then_inc(s_ors, 1)
                middle()
                dve.wait_ge(s_orr, n + 1)
                step(dve.reciprocal(nr, nr))
                for t in range(NT):
                    ot = o[:, t].rearrange("p (h d) -> p h d", d=dim)
                    m = mark(dve.tensor_tensor(ot, ot, last(nrm[:, t, 0:heads], dim), mult))
                dve.wait_ge(s_dve, m)
                step(dve.tensor_tensor(o3, o3, mid(gain, 2 * heads), mult))
                dve.wait_ge(s_zs, n + 1)
                dve.tensor_tensor(o, o, z, mult).then_inc(s_on, 1)

            def out_low(n, first_bank):
                for b in range(2):
                    dve.wait_ge(s_ohi, 2 * n + b + 1)
                    dve.tensor_tensor(o_lo[:, 2 * b:2 * b + 2, :], split3(bank(first_bank + b), 2),
                                      o_hi[:, 2 * b:2 * b + 2, :].bitcast(F32), sub).then_inc(s_o_ready, 1)

            for t in range(NT):
                dve.tensor_copy(k_dup[:, t], h64(z_tok[:, t, Z_BQ + 512:Z_BV]).unsqueeze(2)
                                .broadcast_to([P, 2, 2, HD]))
                m = dve.tensor_copy(ik_dup[:, t], mid(z_tok[:, t, Z_IQ + 512:Z_IW], 2))
            m.then_inc(s_roped, 1)
            o_norm(o_tok, o_sq, 0, HEADS, HD, rep[:, C_ANORM:C_ANORM + HD],
                   z_tok[:, :, Z_Z:Z_Z + 512], lambda: ahead(GATE[4]))

            step(dve.tensor_scalar(iw, z_tok[:, :, Z_IW:Z_IW + 8], (HEADS ** -0.5) * (HD ** -0.5), None, mult))
            for h in range(HEADS):
                for t in range(NT):
                    k = P * (t + 1)
                    dve.wait_ge(s_rel, key_bank(t, h)[0] + 1)
                    if h == 0:
                        m = mark(dve.tensor_scalar(score[:, t, 0:k], rel[:, t, h, 0:k], iw[:, t, h:h + 1], None, mult))
                    else:
                        dve.wait_ge(s_dve, n_dve[0] - 1)
                        m = mark(dve.scalar_tensor_tensor(score[:, t, 0:k], rel[:, t, h, 0:k], iw[:, t, h:h + 1],
                                                          score[:, t, 0:k], mult, add_))
            dve.wait_ge(s_dve, m)
            ahead(GATE[5])
            out_low(0, 0)
            ahead(GATE[6])
            for t in range(NT):
                m = mark(dve.memset(score[0:CHUNK, t, P * t + CHUNK:P * t + P], -BIG))
            dve.wait_ge(s_dve, m)
            tops = (top8, top8b)
            for r in range(TOPK // 8):
                for t in range(NT):
                    src = (score if r == 0 else work)[:, t, 0:P * (t + 1)]
                    if r:
                        dve.wait_ge(s_dve, n_dve[0] - 1 + t)
                    m = mark(dve.max(tops[t], src))
                for t in range(NT):
                    src = (score if r == 0 else work)[:, t, 0:P * (t + 1)]
                    dve.wait_ge(s_dve, m - 1 + t)
                    mark(dve.match_replace(work[:, t, 0:P * (t + 1)], tops[t], src, TAKEN))
            dve.wait_ge(s_dve, n_dve[0])
            for t in range(NT):
                k = P * (t + 1)
                m = mark(dve.tensor_scalar(work[:, t, 0:k], work[:, t, 0:k], -2e38, -BIG, ALU.is_gt, mult))
            dve.wait_ge(s_dve, m)
            for j in range(6):
                t, hs = by_keys(j)
                k, n = P * (t + 1), len(heads_of(j))
                dve.wait_ge(s_log_ps, j + 1)
                dve.tensor_tensor(prob[:, t, hs, 0:k], split3(bank(j), n),
                                  mid(work[:, t, 0:k], n), add_).then_inc(s_msk, 1)

            def softmax(prb, srcs, scale, base):
                for t in range(NT):
                    for hs, src, wait in srcs(t):
                        wait()
                        m = mark(dve.reduce_max(mx[:, t, hs], src, X))
                    dve.wait_ge(s_dve, m)
                    dve.tensor_scalar(nmx[:, t, 0:8], mx[:, t, 0:8], -scale, None, mult).then_inc(s_nmx, 1)
                for t in range(NT):
                    k = P * (t + 1)
                    dve.wait_ge(s_exp, 8 * (base + t + 1))
                    step(dve.reciprocal(rden[:, t, 0:8], den[:, t, 0:8]))
                    dve.tensor_tensor(prb[:, t, :, 0:k], prb[:, t, :, 0:k], last(rden[:, t, 0:8], k),
                                      mult).then_inc(s_prob, 1)

            softmax(prob, lambda t: [(slice(0, 8), prob[:, t, :, 0:P * (t + 1)],
                                      lambda: dve.wait_ge(s_msk, 2 if t == 0 else 6))], HD ** -0.5, 0)

            def attention_low(n):
                for b in range(2):
                    dve.wait_ge(s_pv_hi, 2 * n + b + 1)
                    dve.tensor_tensor(o_lo[:, 4 + 2 * b:6 + 2 * b, :], split3(bank(2 + b), 2),
                                      o_hi[:, 4 + 2 * b:6 + 2 * b, :].bitcast(F32), sub).then_inc(s_bout, 1)
            ahead(GATE[7])
            attention_low(0)

            def mix(PR, OU, n):
                for c in range(2):
                    ahead(PR[c][0])
                    ahead(PR[c][1])
                    dve.wait_ge(w_used, PR[c][1] + 1)
                    dve.wait_ge(s_gate, 16 * (n + 1))
                    if c:
                        dve.wait_ge(s_merged, 2 * n + 1)
                    g = (gate, gate2)[n]
                    dve.tensor_tensor(ga, g[:, 4 * c:4 * c + 4], split3(bank(4 * c, 2), 4), mult)
                    step(dve.tensor_tensor(gb, g[:, 8 + 4 * c:12 + 4 * c], split3(bank(4 * c + 2, 2), 4), mult))
                    dve.tensor_tensor(ga, ga, gb, add_).then_inc(s_merge, 1)
                    dve.wait_ge(s_merge_hi, 2 * n + c + 1)
                    dve.tensor_tensor(h_lo[:, 4 * c:4 * c + 4, :], ga, h_hi[:, 4 * c:4 * c + 4, :].bitcast(F32),
                                      sub).then_inc(s_merged, 1)
                for c in range(2):
                    ahead(OU[c][0])
                    ahead(OU[c][1])
                    dve.wait_ge(w_used, OU[c][1] + 1)
                    cols = slice(512 * c, 512 * c + 512)
                    m = mark(dve.tensor_tensor(x_tok[:, :, cols], x_tok[:, :, cols], split3(bank(2 * c, 2), 2), add_))
                dve.wait_ge(s_dve, m)
                dve.nop().then_inc(s_x_ready, 1)

            def ffn(F, first, weighted):
                for e in range(len(F)):
                    ahead(F[e][1])
                    dve.wait_ge(w_used, F[e][1] + 1)
                    dve.wait_ge(s_silu, first + e + 1)
                    if e >= 2:
                        dve.wait_ge(s_a, first + e - 1)
                    up = split3(bank(5 + 2 * (e % 2)), 2)
                    m = dve.tensor_tensor(act_p[:, e % 2], act_s[:, e % 2], up, mult)
                    if weighted and e == 0:
                        ahead(F[1][1])
                        dve.wait_ge(s_cr, 8)
                    if weighted:
                        step(m)
                        m = dve.tensor_tensor(act_p[:, e % 2], act_p[:, e % 2], mid(comb_rep[:, e, :], 2), mult)
                    m.then_inc(s_prod2, 1)
                    ahead(F[e][1] + 1)
                    dve.wait_ge(s_ahi, first + e + 1)
                    b = 2 * (e % 2)
                    dve.tensor_tensor(o_lo[:, b:b + 2, :], act_p[:, e % 2], o_hi[:, b:b + 2, :].bitcast(F32),
                                      sub).then_inc(s_a, 1)
                ahead(F[-1][2])
                dve.wait_ge(w_used, F[-1][2] + 1)
                step(dve.tensor_tensor(x_tok[:, :, :], x_tok[:, :, :], split3(bank(0, 4), 2), add_))
                dve.nop().then_inc(s_x_ready, 1)

            mix(PROJ, OUT, 0)
            norm(1, 1, R_N2)
            ahead(EXP[0][1])
            for j in range(4):
                m = mark(dve.memset(tie[:, j:j + 1], float(4 - j)))
            dve.wait_ge(s_dve, m)

            def one_hot(dst, src, top):
                step(dve.tensor_reduce(top, src, X, ALU.max))
                step(dve.tensor_tensor(dst, src, last(top, 4), ALU.is_equal))
                step(dve.tensor_tensor(dst, dst, mid(tie, 2), mult))
                step(dve.tensor_reduce(gs2, dst, X, ALU.max))
                step(dve.tensor_tensor(dst, dst, last(gs2, 4), ALU.is_equal))

            dve.wait_ge(s_rl_ps, 1)
            step(dve.tensor_tensor(rl, split3(bank(0)[:, 0:40], 2), mid(rep[:, C_RB:C_RB + 20], 2), add_))
            gl = rl[:, :, 0:4]
            one_hot(ga1, gl, gs1)
            step(dve.tensor_tensor(ttmp, rl[:, :, 4:20].rearrange("p t (g j) -> p t g j", j=4), last(ga1, 4), mult))
            step(dve.tensor_reduce(el, ttmp.rearrange("p t g j -> p t j g"), X, add_))
            dve.tensor_tensor(gl, gl, last(gs1, 4), sub).then_inc(s_rlm, 1)
            step(dve.tensor_reduce(gs3, el, X, ALU.max))
            dve.tensor_tensor(el, el, last(gs3, 4), sub).then_inc(s_rlm, 1)
            dve.wait_ge(s_rle, 2)
            step(dve.tensor_reduce(gs3, gl, X, add_))
            step(dve.reciprocal(gs3, gs3))
            one_hot(e1h, el, gs1)
            step(dve.scalar_tensor_tensor(ea, e1h, -4.0, el, mult, add_))
            one_hot(e2h, ea, gs1)
            step(dve.tensor_tensor(e1h, e1h, e2h, add_))
            step(dve.tensor_tensor(e1h, e1h, el, mult))
            step(dve.tensor_reduce(gs1, e1h, X, add_))
            step(dve.reciprocal(gs1, gs1))
            step(dve.tensor_tensor(gs1, gs1, gs3, mult))
            step(dve.tensor_tensor(e1h, e1h, last(gs1, 4), mult))
            dve.tensor_tensor(comb.rearrange("p t (g j) -> p t g j", j=4), last(ga1, 4),
                              e1h.unsqueeze(2).broadcast_to([P, NT, 4, 4]), mult).then_inc(s_comb, 1)
            ffn(EXP, 0, True)
            norm(2, None, None)

            norm(3, 2, R_NMIX)
            l0, l1 = chan[:, R_LB:R_LB + 4], chan[:, R_LB + 4:R_LB + 8]
            step(dve.tensor_tensor(lbt, l0, l1, ALU.max))
            dve.tensor_tensor(lb, l0, lbt, sub)
            dve.tensor_tensor(lbc, l1, lbt, sub).then_inc(s_lbs, 1)
            for c in range(4):
                ahead(HGQF[c])
            dve.wait_ge(s_lbe, 1)
            step(dve.tensor_tensor(lbt, lb, lbc, add_))
            step(dve.reciprocal(lbt, lbt))
            step(dve.tensor_tensor(lb, lb, lbt, mult))
            step(dve.tensor_tensor(lbc, lbc, lbt, mult))
            dve.wait_ge(s_hev, 4)
            for h in range(HG_HEADS):
                two = hk[:, 2 * h:2 * h + 2, :]
                m = dve.tensor_scalar(two, two, lbc[:, h:h + 1], lb[:, h:h + 1], mult, add_)
            m.then_inc(s_fg, 1)
            step(dve.memset(hsc, 0.0))
            dve.wait_ge(s_logf, 1)
            step(dve.tensor_scalar(hk, hk, -1.0, 1.0, mult, add_))
            dve.nop().then_inc(s_fg, 1)
            for u in range(8):
                m = mark(dve.tensor_tensor_scan(hb[:, u, :], ones[:, :], hd[:, u, :], 0.0, mult, add_))
            dve.wait_ge(s_dve, m)
            ahead(TOK2[0][0])
            ahead(TOK2[0][1])
            flat_b, flat_d, flat_e, flat_k, flat_q = (v.rearrange("p a b -> p (a b)") for v in (hb, hd, he, hk, hq))
            for n in range(len(LEVELS) + 1):
                if n < len(LEVELS):
                    s = LEVELS[n]
                    bl = split3(flat_b, 512 // s)
                    step(dve.tensor_tensor(split3(flat_d, 512 // s), bl,
                                           bl[:, :, s - 1:s].broadcast_to([P, 512 // s, 2 * s]), sub))
                    dve.scalar_tensor_tensor(flat_d, flat_d, -1.0, flat_d, mult, ALU.min).then_inc(s_hd, 1)
                dve.wait_ge(s_hsc_ps, n + 1)
                mask = ident[:, :] if n == 0 else lvl[:, n - 1, :]
                dve.copy_predicated(hsc, mid(mask, 8).bitcast(I32), split3(bank(2 * (n % 2), 2), 8)).then_inc(s_hsc, 1)
                if n < len(LEVELS):
                    dve.wait_ge(s_he, n + 1)
                    s = LEVELS[n]

                    def half(v, i):
                        return v.rearrange("p (b h r) -> p b h r", h=2, r=s)[:, :, i, :]
                    x_op = hx[:, (n + 1) % 2].rearrange("p a b -> p (a b)")
                    dve.tensor_tensor(half(x_op, 0), half(flat_k, 0), half(flat_e, 0), mult)
                    dve.tensor_tensor(half(x_op, 1), half(flat_q, 1), half(flat_e, 1), mult).then_inc(s_hx, 1)
                    if n + 1 == len(LEVELS):
                        dve.wait_ge(s_hx, n + 1)
                    ahead(LVL2[n])
            by_tile = [v.rearrange("p (h t) i -> p h t i", t=2) for v in (hb, he, hk, hq)]
            tb, te, tk, tq = by_tile
            dve.tensor_tensor(te[:, :, 0, :], tb[:, :, 0, P - 1:P].broadcast_to([P, HG_HEADS, P]), tb[:, :, 0, :], sub)
            dve.tensor_copy(te[:, :, 1, :], tb[:, :, 1, :]).then_inc(s_hio, 1)
            dve.wait_ge(s_hie, 1)
            dve.tensor_tensor(hqb, tq[:, :, 1, :], te[:, :, 1, :], mult)
            dve.tensor_tensor(hkd, tk[:, :, 0, :], te[:, :, 0, :], mult).then_inc(s_hkd, 1)
            dve.wait_ge(s_ff, 1)
            step(dve.tensor_tensor(sp1, z2[:, :, Z2_F:Z2_F + 8], mid(rep[:, C_FB:C_FB + 8], 2), add_))
            step(dve.tensor_scalar(sp1, sp1, -1.0, None, mult))
            softplus(1, 3)
            ahead(LVL2[7])
            step(dve.tensor_scalar(glog, sp1, -1.0, None, mult))
            dve.wait_ge(s_tok_ev, N_TOK_BLK + 4)
            for t in range(NT):
                qk = z2[:, t, Z2_Q:Z2_V]
                step(dve.tensor_tensor(fsq, qk, qk, mult))
                step(dve.tensor_reduce(nrm2[:, t, :], h64(fsq), X, add_))
            dve.tensor_scalar(nrm2, nrm2, 1.0 / HD, EPS, mult, add_).then_inc(s_l2s, 1)
            ahead(GATE2[0])
            dve.wait_ge(s_l2r, 2)
            step(dve.reciprocal(nrm2, nrm2))
            step(dve.tensor_scalar(nrm2[:, :, 0:8], nrm2[:, :, 0:8], HD ** -0.5, None, mult))
            for t in range(NT):
                qk = h64(z2[:, t, Z2_Q:Z2_V])
                m = mark(dve.tensor_tensor(qk, qk, last(nrm2[:, t, :], HD), mult))
            dve.wait_ge(s_dve, m)
            for t in range(NT):
                for first, c in ((Z2_Q, C_QN), (Z2_K, C_KN)):
                    v = h64(z2[:, t, first:first + 512])
                    m = dve.tensor_tensor(v, v, mid(rep[:, c:c + HD], 8), mult)
            m.then_inc(s_qn, 1)
            ahead(GATE2[1])
            o_norm(ho, hsq, 1, HG_HEADS, HG_D, rep[:, C_ONORM:C_ONORM + HG_D], z2[:, :, Z2_G:Z2_G + 512],
                   lambda: ahead(GATE2[2]))
            for t in range(NT):
                m = dve.tensor_tensor(f_mask[:, t], mid(after[:, :], 8), last(glog[:, t], P), mult)
            m.then_inc(s_fmask, 1)
            ahead(GATE2[3])
            out_low(1, 2)
            ahead(GATE2[4])
            ahead(GATE2[5])
            softmax(prob2, lambda t: [(by_keys(j)[1], split3(bank(j), len(heads_of(j))),
                                       lambda j=j: dve.wait_ge(s_fl_ps, j + 1))
                                      for j in range(6) if by_keys(j)[0] == t], 1.0, 2)
            ahead(GATE2[6])
            ahead(GATE2[7])
            attention_low(1)
            mix(PROJ2, OUT2, 1)
            norm(4, 3, R_NFFN)
            ffn(FFN, N_EXP, False)
            norm(5, 4, R_NPLE)
            dve.wait_ge(s_p_hi, 1)
            dve.tensor_tensor(o_lo[:, 0:2, :], split3(bank(4), 2), o_hi[:, 0:2, :].bitcast(F32), sub).then_inc(s_p_ready, 1)
            for c in range(2):
                ahead(PLEG[c][0])
                ahead(PLEG[c][1])
            dve.wait_ge(w_used, PLEP + 1)
            for c in range(2):
                cols = slice(512 * c, 512 * c + 512)
                dve.wait_ge(s_plg, c + 1)
                step(dve.tensor_tensor(res[:, :, cols], res[:, :, cols], split3(bank(4 + 2 * c, 2), 2), mult))
                dve.tensor_tensor(res[:, :, cols], res[:, :, cols], x_tok[:, :, cols], add_).then_inc(s_result, 1)


_INS = ["x", "positions", "norm1_g", "w_in", "b_gate", "conv_w", "a_log", "dt_bias", "a_norm_g",
        "w_proj_a", "w_proj_b", "w_out", "norm2_g", "w_router_group", "b_router_group",
        "w_router_expert", "b_router_expert", "w_exp_gate", "w_exp_up", "w_exp_down",
        "final_norm_g", "p_2", "norm_mix_g_2", "w_in_2", "hg_lb_logits_2", "hg_onorm_g_2",
        "fox_f_bias_2", "fox_q_norm_g_2", "fox_k_norm_g_2", "w_branch_a_2", "w_branch_b_2",
        "w_out_2", "norm_ffn_g_2", "w_ffn_gate_2", "w_ffn_up_2", "w_ffn_down_2", "norm_ple_g_2",
        "w_ple_gate_2", "w_ple_proj_2"]


def kernel(**inputs):
    import numpy as np
    import concourse.bacc as bacc
    from concourse.bass_utils import run_bass_kernel_spmd

    nc = bacc.Bacc("TRN2", target_bir_lowering=False, num_devices=1,
                   dynamic_dma_scratch_size=1024)
    arrays, args = {}, []

    def give(name, a):
        arrays[f"in_{name}"] = a
        args.append(nc.dram_tensor(f"in_{name}", a.shape, mybir.dt.from_np(a.dtype),
                                   kind="ExternalInput").ap())

    for name in _INS:
        give(name, np.ascontiguousarray(inputs[name]))
    half = HD // 2
    give("rope_freq", (np.float32(10000.0) ** (-np.arange(half, dtype=np.float32) / np.float32(half)))
         .astype(np.float32).reshape(1, half))
    out = nc.dram_tensor("out", (1, S, DM), F32, kind="ExternalOutput").ap()
    two_block_program(nc, *args, out)
    r = run_bass_kernel_spmd(nc, [arrays], core_ids=[0])
    return r.results[0]["out"]
```

```python
from contextlib import ExitStack

import concourse.bass as bass
from concourse import mybir

F32 = mybir.dt.float32
F32R = mybir.dt.float32r
BF16 = mybir.dt.bfloat16
I32 = mybir.dt.int32
ALU = mybir.AluOpType
ACT = mybir.ActivationFunctionType
X = mybir.AxisListType.X

P = 128
S = 256
NT = S // P
DM = 1024
KD = DM // P
EPS = 1e-6
BIG = 1e30
TAKEN = -3e38

A_W = 512
CONV_W = 3 * A_W
TOK0 = CONV_W
Z_Z, Z_BETA, Z_ALPHA, Z_BQ, Z_BV, Z_IQ, Z_IW, TOK_W = 0, 512, 520, 528, 1168, 1296, 1872, 1880
GATE0 = TOK0 + TOK_W
TOK_BLK = 470
N_TOK_BLK = TOK_W // TOK_BLK
HEADS, HD = 8, 64
KV_HEADS = 2
TOPK = 64
CHUNK = 64
N_GROUPS, PER_GROUP, D_EXP = 4, 4, 256
N_EXP = N_GROUPS * PER_GROUP
HG_HEADS, HG_D = 4, 128
TOK0_2 = 1024
TOK_W2 = 2568
Z2_I, Z2_G, Z2_Q, Z2_K, Z2_V, Z2_F = 0, 512, 1024, 1536, 2048, 2560
GATE0_2 = TOK0_2 + TOK_W2
D_FF = 2816
FF_PAIRS = D_FF // 256
PLE = 256

CH = 2048
RAW = 4
SPL = 3
LEVELS = [1, 2, 4, 8, 16, 32, 64]
N_CONST = 6 + len(LEVELS)

R_N1, R_N2, R_NMIX, R_NFFN, R_NPLE, R_BG, R_CONV, R_LB, R_ALL = 0, 8, 16, 24, 32, 40, 56, 104, 112
C_FIN, C_ALOG, C_DT, C_ANORM, C_RB, C_ONORM, C_FB, C_QN, C_KN, C_ALL = (
    0, 1024, 1032, 1040, 1104, 1124, 1252, 1260, 1324, 1388)


def two_block_program(nc, x, positions, norm1_g, w_in, b_gate, conv_w, a_log, dt_bias, a_norm_g,
                      w_proj_a, w_proj_b, w_out, norm2_g, w_router_group, b_router_group,
                      w_router_expert, b_router_expert, w_exp_gate, w_exp_up, w_exp_down,
                      final_norm_g, p_2, norm_mix_g_2, w_in_2, hg_lb_logits_2, hg_onorm_g_2,
                      fox_f_bias_2, fox_q_norm_g_2, fox_k_norm_g_2, w_branch_a_2, w_branch_b_2,
                      w_out_2, norm_ffn_g_2, w_ffn_gate_2, w_ffn_up_2, w_ffn_down_2,
                      norm_ple_g_2, w_ple_gate_2, w_ple_proj_2, rope_freq, out, dbg=None):
    ctx = ExitStack()
    with ctx:
        def sb(name, shape, dt=F32):
            return ctx.enter_context(nc.sbuf_tensor(name, shape, dt))

        def sem(name):
            return ctx.enter_context(nc.semaphore(name))

        chunks = []

        def rows_by(w, cols):
            return w[:, cols].rearrange("(k p) n -> p k n", p=P)

        def half_rows(w, half, cols):
            return w[half * 512:(half + 1) * 512, cols].rearrange("(k p) n -> p k n", p=P)

        def add(src):
            chunks.append((src, src.shape[1], src.shape[2]))
            return len(chunks) - 1

        wi, wi2 = w_in[0], w_in_2[0]
        CONV = [add(rows_by(wi, slice(256 * c, 256 * c + 256))) for c in range(6)]
        TOK = [[add(half_rows(wi, k, slice(TOK0 + TOK_BLK * b, TOK0 + TOK_BLK * (b + 1))))
                for k in range(2)] for b in range(N_TOK_BLK)]
        GATE = [add(rows_by(wi, slice(GATE0 + 256 * c, GATE0 + 256 * c + 256))) for c in range(8)]
        PROJ = [[add(rows_by(w[0], slice(512 * c, 512 * c + 512))) for c in range(2)]
                for w in (w_proj_a, w_proj_b)]
        OUT = [[add(half_rows(w_out[0], k, slice(512 * c, 512 * c + 512))) for k in range(2)]
               for c in range(2)]
        EXP = [[None] * 3 for _ in range(N_EXP)]
        for e in range(N_EXP + 1):
            if e < N_EXP:
                EXP[e][0] = add(w_exp_gate[0, e].rearrange("(k p) n -> p k n", p=P))
                EXP[e][1] = add(w_exp_up[0, e].rearrange("(k p) n -> p k n", p=P))
            if e >= 1:
                EXP[e - 1][2] = add(w_exp_down[0, e - 1].rearrange("(k p) n -> p k n", p=P))
        HGQF = [add(rows_by(wi2, slice(256 * c, 256 * c + 256))) for c in range(4)]
        TOK2 = [[add(half_rows(wi2, k, slice(TOK0_2 + 512 * b, TOK0_2 + 512 * (b + 1))))
                 for k in range(2)] for b in range(5)]
        GATE2 = [add(rows_by(wi2, slice(GATE0_2 + 256 * c, GATE0_2 + 256 * c + 256)))
                 for c in range(8)]
        PROJ2 = [[None, None] for _ in range(2)]
        for c in range(2):
            for j, w in enumerate((w_branch_a_2, w_branch_b_2)):
                PROJ2[j][c] = add(rows_by(w[0], slice(512 * c, 512 * c + 512)))
        OUT2 = [[add(half_rows(w_out_2[0], k, slice(512 * c, 512 * c + 512))) for k in range(2)]
                for c in range(2)]
        FFN = [[None] * 3 for _ in range(FF_PAIRS)]
        for e in range(FF_PAIRS + 1):
            if e < FF_PAIRS:
                FFN[e][0] = add(rows_by(w_ffn_gate_2[0], slice(256 * e, 256 * e + 256)))
                FFN[e][1] = add(rows_by(w_ffn_up_2[0], slice(256 * e, 256 * e + 256)))
            if e >= 1:
                FFN[e - 1][2] = add(w_ffn_down_2[0, 256 * (e - 1):256 * e, :]
                                    .rearrange("(k p) n -> p k n", p=P))
        PLEP = add(rows_by(w_ple_proj_2[0], slice(0, DM)))
        PLEG = [[add(half_rows(w_ple_gate_2[0], k, slice(512 * c, 512 * c + 512)))
                 for k in range(2)] for c in range(2)]
        N_CH = len(chunks)

        LVL2 = [TOK2[1 + n // 2][n % 2] for n in range(8)]

        raw = sb("raw", [P, RAW, CH])
        w_hi = sb("w_hi", [P, SPL, CH], F32R)
        w_lo = sb("w_lo", [P, SPL, CH], F32R)
        x_tok = sb("x_tok", [P, NT, DM])
        h_hi = sb("h_hi", [P, KD, S], F32R)
        h_lo = sb("h_lo", [P, KD, S], F32R)
        o_hi = sb("o_hi", [P, 8, S], F32R)
        o_lo = sb("o_lo", [P, 8, S], F32R)
        rt_hi = sb("rt_hi", [P, KD, 28], F32R)
        rt_lo = sb("rt_lo", [P, KD, 28], F32R)
        rt_raw = sb("rt_raw", [P, KD, 28])
        ident = sb("ident", [P, P])
        upto = sb("upto", [P, P])
        after = sb("after", [P, P])
        ones = sb("ones", [P, P])
        ident_bf = sb("ident_bf", [P, P], BF16)
        future_bf = sb("future_bf", [P, P], BF16)
        lvl = sb("lvl", [P, len(LEVELS), P])
        rows = sb("rows", [R_ALL, P])
        chan = sb("chan", [P, R_ALL])
        rep = sb("rep", [P, C_ALL])
        pos_i = sb("pos_i", [P, NT], I32)
        pos_f = sb("pos_f", [P, NT])
        freq_row = sb("freq_row", [1, 32])
        cs = sb("cs", [P, 2, NT, 32])
        small = sb("small", [P, 640])
        arena = sb("arena", [P, 21460])
        ps = ctx.enter_context(nc.psum_tensor("ps", [P, 8 * 512], F32))

        def bank(b, n=1):
            return ps[:, 512 * b:512 * (b + n)]

        def view(off, *shape):
            n = 1
            for s in shape:
                n *= s
            v = arena[:, off:off + n]
            if len(shape) == 2:
                v = v.rearrange("p (a b) -> p a b", a=shape[0])
            if len(shape) == 3:
                v = v.rearrange("p (a b c) -> p a b c", a=shape[0], b=shape[1])
            if len(shape) == 4:
                v = v.rearrange("p (a b c d) -> p a b c d", a=shape[0], b=shape[1], c=shape[2])
            return v

        def mid(ap, n):
            return ap.unsqueeze(1).broadcast_to([ap.shape[0], n, ap.shape[1]])

        def last(ap, n):
            return ap.unsqueeze(len(ap.shape)).broadcast_to(list(ap.shape) + [n])

        def split3(ap, a):
            return ap.rearrange("p (a b) -> p a b", a=a)

        def split4(ap, a, b):
            return ap.rearrange("p (a b c) -> p a b c", a=a, b=b)

        xn = view(0, NT, DM)
        junk = view(2048, NT, DM)
        rep_row = view(9940, C_ALL)[0:1]
        z_tok = view(0, NT, TOK_W)
        z_t = view(3760, 12, S + 3)
        y_t = view(6868, 12, S)
        qkv = view(9940, NT, CONV_W)
        q_t, k_t, kb_t = ([view(first + 512 * n, 2, S) for first in (14036, 19924)] for n in range(3))
        qk_t = view(18900, NT, 4, P)
        v_b, k_b, kb_g, k_dec = view(3760, NT, 512), view(4784, NT, 512), view(5808, 512), view(6320, 512)
        gate = view(6868, 16, S)
        q_dec, q_dec_t = view(13012, 512), view(17108, 4, P)
        g_mask, dec, a_t = view(10964, NT, 4, P), view(11988, NT, 4, P), view(13012, NT, 4, P)
        lev = view(10964, NT, 4, P), view(9940, NT, 4, P)
        inv, inv_t, prod = (view(14036 + 1024 * n, NT, 4, P) for n in range(3))
        v_new, o_tok = view(16084, NT, 512), view(4784, NT, 512)
        w_t, state = view(17620, 2, P), view(17876, 2, HD)
        sq = view(14036, NT, DM)
        o_sq = view(5808, NT, 512)
        rt1, rt2 = view(17620, 10, 32), view(17940, 10, 32)
        k_dup, ik_dup = view(18132, NT, 2, 2, HD), view(18644, NT, 2, HD)
        ro_t = view(15060, 11, S)
        score, work = view(3760, NT, S), view(4272, NT, S)
        prob = view(10964, NT, HEADS, S)
        rel = view(10964, NT, HEADS, S)
        prob_t = view(15060, 24, P)
        ga, gb = [view(18448 + 1024 * c, 4, S) for c in range(2)], (view(5808, 4, S), view(8208, 4, S))
        comb_rep = view(0, N_EXP, S)
        act_s = view(4096, 2, 2, S)
        act_p = view(5120, 2, 2, S)
        comb_t = view(6200, S)
        xg = view(8600, NT, DM)
        sel_e = view(6500, N_EXP, P)
        cols_t = view(20000, S)
        z2 = view(0, NT, TOK_W2)
        hq, hk, hb, hd, he = (view(5136 + 1024 * n, 8, P) for n in range(5))
        hx = view(10256, 2, 8, P)
        hsc = view(12304, 8, P)
        hqb, hkd, hkd_t, hs0 = (view(10256 + 512 * n, 4, P) for n in range(4))
        ho, hsq = view(9232, NT, 512), view(8208, NT, 512)
        fsq = view(13328, 1024)
        gate2 = view(14352, 16, S)
        qk2_t = view(5136, 8, S)
        f_mask = view(7184, NT, HEADS, P)
        prob2 = view(9232, NT, HEADS, S)
        prob2_t = view(5136, 24, P)
        p_tok = view(8192, NT, PLE)
        res = view(4096, NT, DM)

        nrm2 = split3(small[:, 472:504], 2)
        ssg4, ssg = split3(small[:, 512:516], 2), small[:, 516:518]
        rms4, rstd4 = small[:, 518:522], small[:, 522:526]
        ssq4 = split3(small[:, 506:510], 2)
        primed = small[:, 510:511]
        ssq, rms, rstd = small[:, 0:2], small[:, 2:4], small[:, 4:6]
        sp1, sp2, sp3 = split3(small[:, 16:32], 2), split3(small[:, 32:48], 2), split3(small[:, 48:64], 2)
        beta, glog = split3(small[:, 64:80], 2), split3(small[:, 80:96], 2)
        e_g, e_gl = split3(small[:, 96:112], 2), split3(small[:, 112:128], 2)
        nrm = split3(small[:, 128:160], 2)
        mx, nmx, den, rden = (split3(small[:, 160 + 16 * n:176 + 16 * n], 2) for n in range(4))
        top8 = small[:, 224:232]
        iw = split3(small[:, 232:248], 2)
        rl = split3(small[:, 248:288], 2)
        ga1, ga2 = split3(small[:, 288:296], 2), split3(small[:, 296:304], 2)
        gs1, gs2, gs3 = small[:, 304:306], small[:, 306:308], small[:, 308:310]
        el, e1h, e2h, ea = (split3(small[:, 312 + 8 * n:320 + 8 * n], 2) for n in range(4))
        tie = small[:, 344:348]
        comb = split3(small[:, 352:384], 2)
        lb, lbc, lbt = small[:, 384:388], small[:, 388:392], small[:, 392:396]
        alog = small[:, 396:404]
        sp4 = split3(small[:, 408:424], 2)
        ttmp = split4(small[:, 424:456], 2, 4)
        turns = split3(small[:, 512:576], 2)
        over = split3(small[:, 576:640], 2)
        top8b = small[:, 464:472]

        w_in_sem = [sem(f"chunk_loaded_{i}") for i in range(RAW)]
        w_high, w_ready, w_used = sem("w_high"), sem("w_ready"), sem("w_used")
        s_x, s_rows, s_rep, s_pos, s_rt = sem("x_loaded"), sem("rows_loaded"), sem("rep_loaded"), sem("pos_loaded"), sem("router_loaded")
        s_p = sem("p_loaded")
        s_pool, s_const = sem("pool_step"), sem("constants_ready")
        s_act, s_dve = sem("act_step"), sem("dve_step")
        s_chan_ps, s_chan = sem("channel_vectors_in_psum"), sem("channel_vectors_ready")
        s_rep_ps = sem("repeated_vectors_in_psum")
        s_rt_hi, s_rt_lo = sem("router_high"), sem("router_split")
        s_sq, s_ms, s_rt_n, s_xn, s_xt, s_hhi, s_h = (sem(n) for n in (
            "squares_summed", "mean_square", "root", "x_normed", "x_transposed", "h_high", "h_ready"))

        (s_conv_ev, s_tap, s_conv, s_silu_y, s_tok_ps, s_tok_ev, s_yt, s_qkv, s_beta, s_spe,
         s_spx, s_spl, s_spm, s_glog, s_gsum, s_eg, s_l2s, s_l2r, s_qn, s_heads_ps, s_heads,
         s_gmask, s_dps, s_dexp, s_kkqk, s_at, s_inv0, s_inv0_ps, s_inv0_ev, s_lev,          s_prod_ps, s_prod, s_dinv, s_inv, s_wt_ps, s_wt, s_u0, s_v0, s_st_ps, s_st, s_u1, s_v1,
         s_o_ps, s_o, s_ors, s_orr, s_zs, s_on, s_ot_ps, s_ohi, s_o_ready) = (sem(n) for n in (
            "conv_in_sbuf", "tap_step", "taps_done", "conv_silu_done", "tok_in_psum",
            "tok_in_sbuf", "conv_transposed", "qkv_ready", "beta_ready", "softplus_arg",
            "softplus_exp", "softplus_arg2", "softplus_ln", "log_decay_ready", "decay_sums_in_psum",
            "decay_exps_ready", "head_squares", "head_roots", "heads_normed", "head_tiles_in_psum",
            "head_tiles_ready", "decay_operand_ready", "decay_in_psum", "decay_exp_done",
            "scores_in_psum", "scores_ready", "inverse_start", "inverse_start_in_psum",
            "inverse_start_turned", "level_ready", "product_in_psum",
            "product_ready", "correction_in_psum", "inverse_updated", "w_in_psum", "w_turned",
            "u0_in_psum", "v0_ready", "state_in_psum", "state_ready", "v1_in_psum", "v1_ready",
            "delta_out_in_psum", "delta_out_ready", "out_squares", "out_roots", "z_silu_ready",
            "out_normed", "out_transposed", "out_high", "out_ready"))
        (s_trig, s_sin, s_roped, s_ro_ps, s_ro, s_rel_ps, s_rel, s_log_ps, s_msk, s_nmx, s_exp,
         s_prob, s_pt_ps, s_pt, s_pv_ps, s_pv_hi, s_bout) = (sem(n) for n in (
            "angles_ready", "trig_ready", "roped", "rope_turned", "rope_tiles_ready",
            "index_scores_in_psum", "index_relu_ready", "logits_in_psum", "logits_masked",
            "row_max_ready", "exp_ready", "prob_ready", "prob_turned", "prob_tiles_ready",
            "attention_in_psum", "attention_high", "attention_ready"))
        s_dinvd, s_invd = sem("correction_of_inverse_in_psum"), sem("inverse_rows_updated")
        s_x_half = sem("x_half_ready")
        s_xg = sem("x_times_gain_ready")
        X_HALVES = (1, 2, 4, 5)
        SQUARES = (2, 4, 4, 4, 4, 4)
        (s_gate, s_merge, s_merge_hi, s_merged,
         s_rl_ps, s_rlm, s_rle, s_comb, s_ct_ps, s_ct, s_cr_ps, s_cr, s_sel, s_silu, s_prod2,
         s_ahi, s_a, ) = (sem(n) for n in (
            "gate_ready", "merge_ready", "merge_high",
            "merged_ready", "router_in_psum", "router_shifted",
            "router_exps", "comb_ready", "comb_turned", "comb_rows_ready", "comb_rep_in_psum",
            "comb_rep_ready", "selectors_ready", "silu_ready", "product2_ready",
            "act_high", "act_ready", ))
        (s_hev, s_lbe, s_lbs, s_fg, s_logf, s_hd, s_he, s_hx, s_hsc_ps, s_hsc, s_hio, s_hie,
         s_hkd, s_hkt_ps, s_hkt, s_hs_ps, s_hs, s_ho_ps, s_ho) = (sem(n) for n in (
            "hg_in_sbuf", "lb_shifted", "lb_exps", "forget_ready", "log_forget_ready",
            "level_distance", "level_decay", "level_operand", "level_scores_in_psum",
            "level_scores_taken", "edge_distance", "edge_decay", "edge_operands", "kd_turned",
            "kd_ready", "hg_state_in_psum", "hg_state_ready", "hg_out_in_psum", "hg_out_ready"))
        s_ga = sem('first_branch_gated')
        s_cols_ps, s_cols = sem("small_columns_in_psum"), sem("small_columns_in_sbuf")
        s_ff, s_gate_ev, s_gate_ev2 = (sem(n) for n in (
            "forget_logits_in_sbuf", "gate_logits_in_sbuf", "gate_logits_in_sbuf_2"))
        (s_fq_ps, s_fq, s_fmask, s_fl_ps, s_p_ps, s_p_hi, s_p_ready, s_plg,          s_result, s_out) = (sem(n) for n in (
            "fox_heads_in_psum", "fox_heads_ready", "forget_operand", "fox_logits_in_psum",
            "p_turned", "p_high", "p_ready", "ple_gate_ready",
            "result_ready", "result_stored"))

        def by_keys(j):
            if j < 2:
                return 0, slice(j, 8, 2)
            h0 = (j - 2) % 2 + 4 * ((j - 2) // 2)
            return 1, slice(h0, h0 + 3, 2)

        def heads_of(j):
            return list(range(8))[by_keys(j)[1]]

        PROJ_BANK = (((6, 2), (4, 0)), ((0, 2), (4, 6)))

        def key_bank(t, h):
            return (h % 2, h // 2) if t == 0 else (2 + h % 2 + 2 * (h // 4), (h % 4) // 2)

        block = ctx.enter_context(nc.Block())

        @block.sync
        def _(sp):
            sp.dma_start(x_tok[:, :, :], x[0].rearrange("(t p) d -> p t d", p=P)).then_inc(s_x, 16)
            for i, (src, kt, n) in enumerate(chunks):
                slot = i % RAW
                if i == 1:
                    sp.wait_ge(s_rows, 128)
                    for c, v in ((C_FIN, final_norm_g.unsqueeze(0)), (C_ALOG, a_log), (C_DT, dt_bias),
                                 (C_ANORM, a_norm_g), (C_RB, b_router_group), (C_RB + 4, b_router_expert),
                                 (C_ONORM, hg_onorm_g_2), (C_FB, fox_f_bias_2), (C_QN, fox_q_norm_g_2),
                                 (C_KN, fox_k_norm_g_2)):
                        sp.dma_start(rep_row[0:1, c:c + v.shape[1]], v).then_inc(s_rep, 16)
                    sp.dma_start(freq_row[0:1, :], rope_freq).then_inc(s_rep, 16)
                if i == RAW:
                    sp.dma_start(rt_raw[:, :, 0:4], w_router_group[0].rearrange("(k p) n -> p k n", p=P)).then_inc(s_rt, 16)
                    sp.dma_start(rt_raw[:, :, 4:20], w_router_expert[0].rearrange("(k p) n -> p k n", p=P)).then_inc(s_rt, 16)
                    sp.dma_start(rt_raw[:, :, 20:28],
                                  wi2[:, TOK0_2 + Z2_F:GATE0_2].rearrange("(k p) n -> p k n", p=P)).then_inc(s_rt, 16)
                if i >= RAW:
                    sp.wait_ge(w_ready, i - RAW + 1)
                dst = raw[:, slot, 0:kt * n].rearrange("p (k n) -> p k n", k=kt)
                sp.dma_start(dst, src).then_inc(w_in_sem[slot], 16)
            for c in range(2):
                cols = slice(512 * c, 512 * c + 512)
                sp.wait_ge(s_result, c + 1)
                sp.dma_start(out[0][:, cols].rearrange("(t p) d -> p t d", p=P), res[:, :, cols]).then_inc(s_out, 16)
            sp.wait_ge(s_out, 32)

        @block.gpsimd
        def _(pool):
            n_pool = [0]

            def step(ins):
                n_pool[0] += 1
                ins.then_inc(s_pool, 1)
                pool.wait_ge(s_pool, n_pool[0])

            step(pool.memset(ident[:, :], 0.0))
            pool.affine_select(out=ident[:, :], in_=ident[:, :], compare_op=ALU.not_equal,
                               fill=1.0, base=0, pattern=[[-1, P]], channel_multiplier=1).then_inc(s_const, 1)
            pool.memset(ones[:, :], 1.0).then_inc(s_const, 1)
            pool.wait_ge(s_const, 2)
            pool.tensor_copy(ident_bf[:, :], ident[:, :]).then_inc(s_const, 1)
            pool.affine_select(out=upto[:, :], in_=ones[:, :], compare_op=ALU.is_ge, fill=0.0,
                               base=0, pattern=[[1, P]], channel_multiplier=-1).then_inc(s_const, 1)
            pool.affine_select(out=after[:, :], in_=ones[:, :], compare_op=ALU.is_gt, fill=0.0,
                               base=0, pattern=[[-1, P]], channel_multiplier=1).then_inc(s_const, 1)
            step(pool.memset(future_bf[:, :], 0.0))
            pool.affine_select(out=future_bf[:, :], in_=future_bf[:, :], compare_op=ALU.is_ge,
                               fill=-BIG, base=0, pattern=[[-1, P]],
                               channel_multiplier=1).then_inc(s_const, 1)
            for n, s in enumerate(LEVELS):
                blocks = P // (2 * s)
                m = lvl[:, n, :].rearrange("p (b h r) -> p b h r", b=blocks, h=2)
                pool.memset(m[:, :, 0, :], 0.0)
                step(pool.memset(m[:, :, 1, :], 1.0))
                step(pool.affine_select(out=lvl[:, n, :], in_=lvl[:, n, :], compare_op=ALU.is_ge,
                                        fill=0.0, base=0, pattern=[[-2 * s, blocks], [0, 2 * s]],
                                        channel_multiplier=1))
                pool.affine_select(out=lvl[:, n, :], in_=lvl[:, n, :], compare_op=ALU.is_ge,
                                   fill=0.0, base=s - 1, pattern=[[2 * s, blocks], [0, 2 * s]],
                                   channel_multiplier=-1).then_inc(s_const, 1)
            for gr in range(2):
                pool.wait_ge(s_at, gr + 1)
                for n in range(1, len(LEVELS)):
                    for t in range(NT):
                        if n >= 3:
                            pool.wait_ge(s_prod_ps, 12 * gr + 2 * (n - 3) + t + 1)
                        pool.tensor_tensor(lev[n % 2][:, t], a_t[:, t], mid(lvl[:, n, :], 4),
                                           ALU.mult).then_inc(s_lev, 1)
            pool.wait_ge(s_x_half, 2)
            step(pool.memset(sel_e[0:16], 0.0))
            pool.affine_select(out=sel_e[0:16], in_=sel_e[0:16], compare_op=ALU.not_equal,
                               fill=1.0, base=0, pattern=[[-1, N_EXP], [0, P]],
                               channel_multiplier=1).then_inc(s_sel, 1)

        @block.scalar
        def _(act):
            n_act, split_at = [0], [0]

            def step(ins):
                n_act[0] += 1
                ins.then_inc(s_act, 1)
                act.wait_ge(s_act, n_act[0])

            def ahead(i):
                while split_at[0] <= min(i + SPL - 1, N_CH - 1):
                    j = split_at[0]
                    _, kt, n = chunks[j]
                    act.wait_ge(w_in_sem[j % RAW], 16 * (j // RAW + 1))
                    if j >= SPL:
                        act.wait_ge(w_used, j - SPL + 1)
                    act.activation(w_hi[:, j % SPL, 0:kt * n], raw[:, j % RAW, 0:kt * n],
                                   ACT.Copy).then_inc(w_high, 1)
                    split_at[0] += 1

            def high(turn, row):
                for b in range(4):
                    act.wait_ge(s_xt, 4 * turn + b + 1)
                    for k in (2 * b, 2 * b + 1):
                        act.activation(h_hi[:, k, :], split3(bank(b), 2)[:, k % 2, :], ACT.Copy,
                                       scale=chan[:, row + k:row + k + 1]).then_inc(s_hhi, 1)

            def norm(n, turn, row):
                act.wait_ge(s_const, 2)
                act.activation(primed, ones[:, 0:1], ACT.Sqrt)
                if n in X_HALVES:
                    for c in range(2):
                        cols = slice(512 * c, 512 * c + 512)
                        act.wait_ge(s_x_half, 2 * X_HALVES.index(n) + c + 1)
                        for t in range(NT):
                            act.activation(junk[:, t, cols], x_tok[:, t, cols], ACT.Square,
                                           accum_out=ssq4[:, c, t:t + 1]).then_inc(s_sq, 1)
                else:
                    act.wait_ge(s_x, 16)
                    for t in range(NT):
                        act.activation(junk[:, t], x_tok[:, t], ACT.Square,
                                       accum_out=ssq[:, t:t + 1]).then_inc(s_sq, 1)
                act.wait_ge(s_ms, n + 1)
                act.activation(rms, rms, ACT.Sqrt).then_inc(s_rt_n, 1)
                if n == 0:
                    ahead(-2)
                if n == 0:
                    act.wait_ge(s_chan, 1)
                high(turn, row)

            def final_and_mix():
                act.activation(primed, ones[:, 0:1], ACT.Sqrt)
                for v, ready, base, sums, trash in ((x_tok, s_x_half, 2, ssq4, junk), (xg, s_xg, 0, ssg4, xn)):
                    for c in range(2):
                        cols = slice(512 * c, 512 * c + 512)
                        act.wait_ge(ready, base + c + 1)
                        for t in range(NT):
                            act.activation(trash[:, t, cols], v[:, t, cols], ACT.Square,
                                           accum_out=sums[:, c, t:t + 1]).then_inc(s_sq, 1)
                act.wait_ge(s_ms, 4)
                act.activation(rms4, rms4, ACT.Sqrt).then_inc(s_rt_n, 2)
                high(2, R_NMIX)

            for r, v in ((R_N1, norm1_g), (R_N2, norm2_g), (R_NMIX, norm_mix_g_2),
                         (R_NFFN, norm_ffn_g_2), (R_NPLE, norm_ple_g_2), (R_BG, b_gate)):
                n = v.shape[1] // P
                act.dma_start(rows[r:r + n, :], v[0].rearrange("(r p) -> r p", p=P)).then_inc(s_rows, 16)
            act.dma_start(rows[R_CONV:R_CONV + 48, :],
                          conv_w[0].rearrange("k (c p) -> (k c) p", p=P)).then_inc(s_rows, 16)
            act.dma_start(rows[R_LB:R_LB + 8, :],
                          hg_lb_logits_2.rearrange("k (c p) -> (k c) p", p=P)).then_inc(s_rows, 16)
            with nc.allow_non_contiguous_dma("256 positions, one word each"):
                act.dma_start(pos_i[:, :], positions[0].rearrange("(t p) -> p t", p=P)).then_inc(s_pos, 16)

            norm(0, 0, R_N1)
            ahead(0)

            def conv_silu(c):
                act.wait_ge(s_conv, c + 1)
                act.activation(y_t[:, 2 * c:2 * c + 2, :], y_t[:, 2 * c:2 * c + 2, :],
                               ACT.Silu).then_inc(s_silu_y, 1)

            for c in range(6):
                ahead(CONV[c])
                act.wait_ge(w_used, CONV[c] + 1)
                act.activation(z_t[:, 2 * c:2 * c + 2, 3:S + 3], split3(bank(c % 4), 2),
                               ACT.Copy).then_inc(s_conv_ev, 1)
                if c:
                    conv_silu(c - 1)
            conv_silu(5)
            act.wait_ge(s_rt, 48)
            act.activation(rt_hi[:, :, :], rt_raw[:, :, :], ACT.Copy).then_inc(s_rt_hi, 1)

            def tok_in(b):
                act.wait_ge(w_used, TOK[b][1] + 1)
                act.activation(z_tok[:, :, TOK_BLK * b:TOK_BLK * (b + 1)],
                               split3(bank(4 + 2 * (b % 2), 2), 2)[:, :, 0:TOK_BLK],
                               ACT.Copy).then_inc(s_tok_ev, 1)

            def softplus(n):
                act.wait_ge(s_spe, n + 1)
                act.activation(sp2, sp2, ACT.Exp).then_inc(s_spx, 1)
                act.wait_ge(s_spl, n + 1)
                act.activation(sp3, sp3, ACT.Ln).then_inc(s_spm, 1)

            def gate_out(G, c, dst, ev):
                act.wait_ge(w_used, G[c] + 1)
                act.activation(dst[:, 2 * c:2 * c + 2, :], split3(bank(6 + c % 2), 2),
                               ACT.Copy).then_inc(ev, 1)
                if c < 7:
                    ahead(G[c + 1])

            ahead(TOK[0][0])
            act.wait_ge(s_trig, 1)
            act.activation(cs[:, :, :, :], cs[:, :, :, :], ACT.Sin).then_inc(s_sin, 1)
            ahead(TOK[0][1])
            tok_in(0)
            ahead(TOK[1][0])
            for j in range(6):
                act.wait_ge(s_yt, j + 1)
                t, g = j // 3, j % 3
                act.activation(qkv[:, t, 512 * g:512 * g + 512], bank(j % 4), ACT.Copy).then_inc(s_qkv, 1)
            ahead(TOK[1][1])
            act.wait_ge(s_l2s, 1)
            act.activation(nrm, nrm, ACT.Sqrt).then_inc(s_l2r, 1)
            tok_in(1)
            ahead(TOK[2][0])
            act.wait_ge(s_tok_ev, 2)
            act.activation(beta, z_tok[:, :, Z_BETA:Z_BETA + 8], ACT.Sigmoid).then_inc(s_beta, 1)
            softplus(0)
            act.activation(alog, rep[:, C_ALOG:C_ALOG + 8], ACT.Exp).then_inc(s_spm, 1)
            ahead(TOK[2][1])
            tok_in(2)
            ahead(TOK[3][0])
            act.wait_ge(s_gsum, 1)
            act.activation(small[:, 96:128], bank(2)[:, 0:32], ACT.Exp).then_inc(s_eg, 1)
            tok_in(3)
            ahead(TOK[3][1])

            def turned(dst, n, first_bank, sig, done):
                for j in range(n):
                    act.wait_ge(sig, j + 1)
                    act.activation(dst(j), bank(first_bank(j)), ACT.Copy).then_inc(done, 1)

            def head_tile(j):
                if j == 6:
                    return q_dec_t.rearrange("p a b -> p (a b)")
                return (q_t, k_t, kb_t)[j // 2][j % 2].rearrange("p a b -> p (a b)")
            turned(head_tile, 7, lambda j: j % 6, s_heads_ps, s_heads)
            act.activation(z_tok[:, :, Z_Z:Z_Z + 512], z_tok[:, :, Z_Z:Z_Z + 512],
                           ACT.Silu).then_inc(s_zs, 1)
            ahead(GATE[0])
            gate_out(GATE, 0, gate, s_gate_ev)

            def decays(gr):
                for t in range(NT):
                    act.wait_ge(s_dps, 2 * gr + t + 1)
                    act.activation(dec[:, t].rearrange("p a b -> p (a b)"), bank(t),
                                   ACT.Exp).then_inc(s_dexp, 1)

            decays(0)
            for gr in range(2):
                gate_out(GATE, gr + 1, gate, s_gate_ev)
                for t in range(NT):
                    act.wait_ge(s_inv0_ps, 2 * gr + t + 1)
                    act.activation(inv[:, t].rearrange("p a b -> p (a b)"), bank(t),
                                   ACT.Copy).then_inc(s_inv0_ev, 1)
                for n in range(1, len(LEVELS)):
                    for t in range(NT):
                        act.wait_ge(s_prod_ps, 12 * gr + 2 * (n - 1) + t + 1)
                        if n >= 2 or gr:
                            act.wait_ge(s_dinv, 12 * gr + 2 * (n - 2) + t + 1)
                        act.activation(prod[:, t].rearrange("p a b -> p (a b)"), bank(t),
                                       ACT.Copy).then_inc(s_prod, 1)
                act.wait_ge(s_wt_ps, gr + 1)
                act.activation(w_t.rearrange("p a b -> p (a b)"), bank(2)[:, 0:256], ACT.Copy,
                               scale=-1.0).then_inc(s_wt, 1)
                act.wait_ge(s_u0, gr + 1)
                act.activation(v_new[:, 0, 256 * gr:256 * gr + 256], bank(3)[:, 0:256],
                               ACT.Copy).then_inc(s_v0, 1)
                act.wait_ge(s_st_ps, gr + 1)
                act.activation(state.rearrange("p a b -> p (a b)"), bank(4)[:, 0:128],
                               ACT.Copy).then_inc(s_st, 1)
                act.wait_ge(s_u1, gr + 1)
                for odd, b in ((0, 5), (1, 3)):
                    dst = v_new[:, 1, 256 * gr:256 * gr + 256].rearrange("p (a b d) -> p a b d", a=2, b=2)
                    act.activation(dst[:, :, odd, :], split3(bank(b)[:, 0:128], 2), ACT.Copy).then_inc(s_v1, 1)
                if gr == 0:
                    decays(1)
                act.wait_ge(s_o_ps, gr + 1)
                act.activation(o_tok[:, 0, 256 * gr:256 * gr + 256], bank(2)[:, 0:256],
                               ACT.Copy).then_inc(s_o, 1)
                for odd, b in ((0, 4), (1, 5)):
                    dst = o_tok[:, 1, 256 * gr:256 * gr + 256].rearrange("p (a b d) -> p a b d", a=2, b=2)
                    act.activation(dst[:, :, odd, :], split3(bank(b)[:, 0:128], 2), ACT.Copy).then_inc(s_o, 1)

            def out_high(n, first_bank):
                for b in range(2):
                    act.wait_ge(s_ot_ps, 2 * n + b + 1)
                    act.activation(o_hi[:, 2 * b:2 * b + 2, :], split3(bank(first_bank + b), 2),
                                   ACT.Copy).then_inc(s_ohi, 1)

            for j in range(6):
                act.wait_ge(s_ro_ps, j + 1)
                n = 2 if j < 5 else 1
                act.activation(ro_t[:, 2 * j:2 * j + n, :], split3(bank(j), 2)[:, 0:n, :],
                               ACT.Copy).then_inc(s_ro, 1)
            gate_out(GATE, 3, gate, s_gate_ev)
            act.wait_ge(s_ors, 1)
            act.activation(nrm[:, :, 0:8], nrm[:, :, 0:8], ACT.Sqrt).then_inc(s_orr, 1)
            for j in range(6):
                act.wait_ge(s_rel_ps, j + 1)
                t, hs = by_keys(j)
                act.activation(rel[:, t, hs, 0:P * (t + 1)], split3(bank(j), 4 if j < 2 else 2), ACT.Relu).then_inc(s_rel, 1)
            gate_out(GATE, 4, gate, s_gate_ev)
            out_high(0, 0)
            gate_out(GATE, 5, gate, s_gate_ev)
            gate_out(GATE, 6, gate, s_gate_ev)

            def exps(prb, src, scale, base):
                for t in range(NT):
                    act.wait_ge(s_nmx, base + t + 1)
                    for h in range(HEADS):
                        act.activation(prb[:, t, h, 0:P * (t + 1)], src(t, h), ACT.Exp,
                                       bias=nmx[:, t, h:h + 1], scale=scale,
                                       accum_out=den[:, t, h:h + 1]).then_inc(s_exp, 1)

            def prob_tiles(dst, base):
                for j in range(6):
                    act.wait_ge(s_pt_ps, base + j + 1)
                    act.activation(dst[:, 4 * j:4 * j + 4, :].rearrange("p a b -> p (a b)"),
                                   bank(j % 4), ACT.Copy).then_inc(s_pt, 1)

            def attention_high(base):
                for b in range(2):
                    act.wait_ge(s_pv_ps, base + b + 1)
                    act.activation(o_hi[:, 4 + 2 * b:6 + 2 * b, :], split3(bank(2 + b), 2),
                                   ACT.Copy).then_inc(s_pv_hi, 1)

            gate_out(GATE, 7, gate, s_gate_ev)
            act.wait_ge(s_gate_ev, 8)
            for c in range(16):
                act.activation(gate[:, c, :], gate[:, c, :], ACT.Sigmoid,
                               bias=chan[:, R_BG + c:R_BG + c + 1]).then_inc(s_gate, 1)
            exps(prob, lambda t, h: prob[:, t, h, 0:P * (t + 1)], HD ** -0.5, 0)
            ahead(PROJ[0][0])
            prob_tiles(prob_t, 0)
            attention_high(0)
            ahead(PROJ[0][1])


            def merge_high(PR, first):
                for c in range(2):
                    ahead(PR[1][c])
                    act.wait_ge(s_merge, first + c + 1)
                    act.activation(h_hi[:, 4 * c:4 * c + 4, :], ga[c], ACT.Copy).then_inc(s_merge_hi, 1)

            def keep(ch):
                for c in ch:
                    for i in c:
                        ahead(i)

            def ffn(F, first, routed):
                for e in range(len(F)):
                    ahead(F[e][0])
                    act.wait_ge(w_used, F[e][0] + 1)
                    act.activation(act_s[:, e % 2], split3(bank(4 + 2 * (e % 2)), 2),
                                   ACT.Silu).then_inc(s_silu, 1)
                    ahead(F[e][1])
                    if e < 2 and routed:
                        if e == 0:
                            act.wait_ge(s_ct_ps, 1)
                            act.activation(comb_t[0:16, :], bank(1)[0:16, 0:S], ACT.Copy).then_inc(s_ct, 1)
                        for b in range(4 * e, 4 * e + 4):
                            act.wait_ge(s_cr_ps, b + 1)
                            act.activation(comb_rep[:, 2 * b:2 * b + 2, :], split3(bank(b % 4), 2),
                                           ACT.Copy).then_inc(s_cr, 1)
                    act.wait_ge(s_prod2, first + e + 1)
                    b = 2 * (e % 2)
                    act.activation(o_hi[:, b:b + 2, :], act_p[:, e % 2], ACT.Copy).then_inc(s_ahi, 1)
                ahead(F[-1][2])

            merge_high(PROJ, 0)
            keep(OUT)
            norm(1, 1, R_N2)
            def cols_to_sbuf(b, n, count):
                act.wait_ge(s_cols_ps, count)
                act.activation(cols_t[0:n, :], bank(b)[0:n, 256:512], ACT.Copy).then_inc(s_cols, 1)

            cols_to_sbuf(0, 20, 1)
            ahead(EXP[0][0])
            act.wait_ge(s_rlm, 1)
            act.activation(rl[:, :, 0:4], rl[:, :, 0:4], ACT.Exp).then_inc(s_rle, 1)
            act.wait_ge(s_rlm, 2)
            act.activation(el, el, ACT.Exp).then_inc(s_rle, 1)
            ffn(EXP, 0, True)

            final_and_mix()
            for c in range(4):
                ahead(HGQF[c])
                act.wait_ge(w_used, HGQF[c] + 1)
                dst = (hq if c < 2 else hk).rearrange("p a b -> p (a b)")[:, 512 * (c % 2):512 * (c % 2) + 512]
                act.activation(dst, bank(c), ACT.Silu if c < 2 else ACT.Sigmoid).then_inc(s_hev, 1)
            act.wait_ge(s_lbs, 1)
            act.activation(small[:, 384:392], small[:, 384:392], ACT.Exp).then_inc(s_lbe, 1)
            act.wait_ge(s_fg, 1)
            act.activation(hd, hk, ACT.Ln).then_inc(s_logf, 1)

            def tok_out(b):
                act.wait_ge(w_used, TOK2[b][1] + 1)
                act.activation(z2[:, :, 512 * b:512 * b + 512], split3(bank(4 + 2 * (b % 2), 2), 2),
                               ACT.Copy).then_inc(s_tok_ev, 1)

            ahead(TOK2[0][0])
            ahead(TOK2[0][1])
            tok_out(0)
            cols_to_sbuf(6, 8, 2)
            act.wait_ge(s_tok_ps, 1)
            act.activation(z2[:, :, Z2_F:Z2_F + 8], split3(bank(6)[:, 0:16], 2),
                           ACT.Copy).then_inc(s_ff, 1)
            for n in range(len(LEVELS)):
                act.wait_ge(s_hd, n + 1)
                act.activation(he, hd, ACT.Exp).then_inc(s_he, 1)
                ahead(LVL2[n])
                if n in (2, 4, 6):
                    tok_out(n // 2)
            act.wait_ge(s_hio, 1)
            act.activation(he, he, ACT.Exp).then_inc(s_hie, 1)
            softplus(1)
            ahead(LVL2[7])
            tok_out(4)
            act.wait_ge(s_hkt_ps, 1)
            act.activation(hkd_t.rearrange("p a b -> p (a b)"), bank(0), ACT.Copy).then_inc(s_hkt, 1)
            ahead(GATE2[0])
            act.wait_ge(s_l2s, 2)
            act.activation(nrm2, nrm2, ACT.Sqrt).then_inc(s_l2r, 1)
            act.wait_ge(s_hs_ps, 1)
            act.activation(hs0.rearrange("p a b -> p (a b)"), bank(1), ACT.Copy).then_inc(s_hs, 1)
            gate_out(GATE2, 0, gate2, s_gate_ev2)
            act.wait_ge(s_ho_ps, 1)
            act.activation(ho, split3(bank(2, 2), 2), ACT.Copy).then_inc(s_ho, 1)
            gate_out(GATE2, 1, gate2, s_gate_ev2)
            act.wait_ge(s_ors, 2)
            act.activation(nrm[:, :, 0:4], nrm[:, :, 0:4], ACT.Sqrt).then_inc(s_orr, 1)
            act.activation(z2[:, :, Z2_G:Z2_G + 512], z2[:, :, Z2_G:Z2_G + 512],
                           ACT.Silu).then_inc(s_zs, 1)
            for j in range(4):
                act.wait_ge(s_fq_ps, j + 1)
                act.activation(qk2_t[:, 2 * j:2 * j + 2, :], split3(bank((4, 5, 0, 1)[j]), 2),
                               ACT.Copy).then_inc(s_fq, 1)
            gate_out(GATE2, 2, gate2, s_gate_ev2)
            out_high(1, 2)
            gate_out(GATE2, 3, gate2, s_gate_ev2)
            gate_out(GATE2, 4, gate2, s_gate_ev2)

            def logits_in_psum(t, h):
                b, n = key_bank(t, h)
                return split3(bank(b), 4 if t == 0 else 2)[:, n, :]
            exps(prob2, logits_in_psum, 1.0, 2)
            gate_out(GATE2, 5, gate2, s_gate_ev2)
            gate_out(GATE2, 6, gate2, s_gate_ev2)
            prob_tiles(prob2_t, 6)
            gate_out(GATE2, 7, gate2, s_gate_ev2)
            ahead(PROJ2[0][0])
            attention_high(2)
            ahead(PROJ2[1][0])
            act.wait_ge(s_gate_ev2, 8)
            act.activation(gate2[:, :, :], gate2[:, :, :], ACT.Sigmoid).then_inc(s_gate, 16)
            merge_high(PROJ2, 2)
            keep(OUT2)
            norm(4, 3, R_NFFN)
            act.dma_start(p_tok, p_2[0, 0].rearrange("(t p) d -> p t d", p=P)).then_inc(s_p, 16)
            ffn(FFN, N_EXP, False)
            act.wait_ge(s_p_ps, 1)
            act.activation(o_hi[:, 4:6, :], split3(bank(6), 2), ACT.Copy).then_inc(s_p_hi, 1)
            ahead(PLEP)
            norm(5, 4, R_NPLE)
            for c in range(2):
                ahead(PLEG[c][0])
                ahead(PLEG[c][1])
                act.wait_ge(w_used, PLEG[c][1] + 1)
                act.activation(res[:, :, 512 * c:512 * c + 512], split3(bank(2 * c, 2), 2),
                               ACT.Sigmoid).then_inc(s_plg, 1)

        @block.tensor
        def _(pe):
            def chunk(i):
                pe.wait_ge(w_ready, i + 1)
                _, kt, n = chunks[i]
                return [w[:, i % SPL, 0:kt * n].rearrange("p (k n) -> p k n", k=kt) for w in (w_hi, w_lo)]

            def weights_still(i, outs, a_hi, a_lo, turn=None):
                hi, lo = chunk(i)
                kt = chunks[i][1]
                for c, o in enumerate(outs):
                    cols = slice(P * c, P * c + P)
                    for k in range(kt):
                        if turn is not None and c == 0:
                            wait_h(turn, k)
                        pe.matmul(o, hi[:, k, cols], a_hi[:, k, :], start=(k == 0), stop=False)
                        pe.matmul(o, hi[:, k, cols], a_lo[:, k, :], start=False, stop=False)
                        last_mm = pe.matmul(o, lo[:, k, cols], a_hi[:, k, :], start=False,
                                            stop=(k == kt - 1))
                last_mm.then_inc(w_used, 1)

            def weights_move(i, outs, a_hi, a_lo, first, end, turn=None, k0=0):
                hi, lo = chunk(i)
                kt, n = chunks[i][1:]
                for (t, c), o in outs.items():
                    tok = slice(P * t, P * t + P)
                    cols = slice(512 * c, min(n, 512 * c + 512))
                    for k in range(kt):
                        if turn is not None and t == 0:
                            wait_h(turn, k0 + k)
                        pe.matmul(o, a_hi[:, k, tok], hi[:, k, cols], start=(first and k == 0), stop=False)
                        pe.matmul(o, a_hi[:, k, tok], lo[:, k, cols], start=False, stop=False)
                        last_mm = pe.matmul(o, a_lo[:, k, tok], hi[:, k, cols], start=False,
                                            stop=(end and k == kt - 1))
                last_mm.then_inc(w_used, 1)

            def turn_x(turn, meanwhile=lambda: None):
                for t in range(NT):
                    pe.wait_ge(s_xn, 2 * turn + t + 1)
                    for b in range(4):
                        for k in (2 * b, 2 * b + 1):
                            m = pe.transpose(split3(bank(b), 2)[:, k % 2, P * t:P * t + P],
                                             xn[:, t, P * k:P * k + P], ident[:, :])
                        if t == NT - 1:
                            m.then_inc(s_xt, 1)
                meanwhile()

            def wait_h(turn, k):
                pe.wait_ge(s_h, 8 * turn + max(k + 1, 2))

            pe.wait_ge(s_const, 1)
            pe.wait_ge(s_rows, 128)
            pe.transpose(bank(7)[:, 0:R_ALL], rows[:, :], ident[0:R_ALL, 0:R_ALL]).then_inc(s_chan_ps, 1)

            def repeat_rows():
                pe.wait_ge(s_const, 2)
                pe.wait_ge(s_rep, 176)
                for r in range(3):
                    n = min(512, C_ALL - 512 * r)
                    m = pe.matmul(bank(4 + r)[:, 0:n], ones[0:1, :], rep_row[0:1, 512 * r:512 * r + n],
                                  start=True, stop=True)
                m.then_inc(s_rep_ps, 1)
                pe.matmul(bank(6)[:, 400:432], ones[0:1, :], freq_row[0:1, :], start=True,
                          stop=True).then_inc(s_rep_ps, 1)

            turn_x(0, repeat_rows)

            for c in range(6):
                if c >= 4:
                    pe.wait_ge(s_conv_ev, c - 3)
                b = split3(bank(c % 4), 2)
                weights_still(CONV[c], [b[:, 0, :], b[:, 1, :]], h_hi, h_lo, 0 if c == 0 else None)

            def tok_block(T, b, width, base):
                if base + b >= 2:
                    pe.wait_ge(s_tok_ev, base + b - 1)
                outs = {(t, 0): bank(4 + 2 * (b % 2) + t)[:, 0:width] for t in range(NT)}
                weights_move(T[b][0], outs, h_hi, h_lo, True, False)
                weights_move(T[b][1], outs, h_hi[:, 4:8], h_lo[:, 4:8], False, True)

            def project(PR, n, c, j):
                outs = [split3(bank(PROJ_BANK[n][c][j] + q // 2), 2)[:, q % 2, :] for q in range(4)]
                weights_still(PR[j][c], outs, o_hi[:, 4 * j:4 * j + 4], o_lo[:, 4 * j:4 * j + 4])

            def mix(PR, OU, n):
                pe.wait_ge(s_bout, 2 * n + 2)
                project(PR, n, 0, 1)
                pe.wait_ge((s_gate_ev, s_gate_ev2)[n], 8)
                for j in ((1,), (0, 1))[n]:
                    project(PR, n, 1, j)
                pe.wait_ge(s_merged, 2 * n + 1)
                for c in range(2):
                    outs = {(t, 0): bank(PROJ_BANK[n][0][c] + t) for t in range(NT)}
                    for k in range(2):
                        if k == 1:
                            pe.wait_ge(s_merged, 2 * n + 2)
                        weights_move(OU[c][k], outs, h_hi[:, 4 * k:4 * k + 4], h_lo[:, 4 * k:4 * k + 4],
                                         k == 0, k == 1)

            def gate_chunk(G, c, ev):
                if c >= 2:
                    pe.wait_ge(ev, c - 1)
                b = split3(bank(6 + c % 2), 2)
                weights_still(G[c], [b[:, 0, :], b[:, 1, :]], h_hi, h_lo)

            def turn_y(js):
                for j in js:
                    if j >= 4:
                        pe.wait_ge(s_qkv, j - 3)
                    t, g = j // 3, j % 3
                    for c in range(4):
                        m = pe.transpose(bank(j % 4)[:, P * c:P * c + P],
                                         y_t[:, 4 * g + c, P * t:P * t + P], ident[:, :])
                    m.then_inc(s_yt, 1)

            pe.wait_ge(s_chan, 5)
            tok_block(TOK, 0, TOK_BLK, 0)
            pe.wait_ge(s_silu_y, 6)
            pe.wait_ge(s_conv_ev, 6)
            turn_y(range(4))
            outs = {(t, 0): bank(6 + t)[:, 0:TOK_BLK] for t in range(NT)}
            weights_move(TOK[1][0], outs, h_hi, h_lo, True, False)
            turn_y(range(4, 6))
            weights_move(TOK[1][1], outs, h_hi[:, 4:8], h_lo[:, 4:8], False, True)
            tok_block(TOK, 2, TOK_BLK, 0)
            pe.wait_ge(s_const, N_CONST)
            pe.wait_ge(s_glog, 1)
            pe.wait_ge(s_qkv, 3)
            for n, mask in enumerate((upto, after)):
                for t in range(NT):
                    o = 16 * n + 8 * t
                    m = pe.matmul(bank(2)[:, o:o + 8], mask[:, :], glog[:, t, :], start=True, stop=True)
            m.then_inc(s_gsum, 1)
            tok_block(TOK, 3, TOK_BLK, 0)
            pe.wait_ge(s_qn, 1)
            pe.wait_ge(s_qkv, 6)
            pe.wait_ge(s_eg, 1)
            pe.wait_ge(s_tok_ev, 3)
            for j in range(6):
                for c in range(4):
                    pair, t = 2 * (j % 2) + c // 2, c % 2
                    src = (qkv[:, t, P * pair:P * pair + P], qkv[:, t, 512 + P * pair:640 + P * pair],
                           k_b[:, t, P * pair:P * pair + P])[j // 2]
                    m = pe.transpose(bank(j)[:, P * c:P * c + P], src, ident[:, :])
                m.then_inc(s_heads_ps, 1)
            pe.wait_ge(s_qn, 2)
            pe.wait_ge(s_heads, 1)
            for c in range(4):
                m = pe.transpose(bank(0)[:, P * c:P * c + P], q_dec[:, P * c:P * c + P], ident[:, :])
            m.then_inc(s_heads_ps, 1)
            pe.wait_ge(s_tok_ev, N_TOK_BLK)
            gate_chunk(GATE, 0, s_gate_ev)

            def head(tile, h, t):
                r = 64 * (h % 2)
                return tile[h // 4][r:r + 64, h // 2 % 2, P * t:P * t + P]

            def decays(gr):
                pe.wait_ge(s_gmask, gr + 1)
                for t in range(NT):
                    for u in range(4):
                        m = pe.matmul(bank(t)[:, P * u:P * u + P], g_mask[:, t, u, :], upto[:, :],
                                      start=True, stop=True)
                    m.then_inc(s_dps, 1)

            pe.wait_ge(s_heads, 7)
            decays(0)
            for gr in range(2):
                if gr:
                    pe.wait_ge(s_o, 3 * gr)
                for n, right in enumerate((kb_t, q_t)):
                    for odd in range(2):
                        for t in range(NT):
                            for pl in range(2):
                                h = 4 * gr + 2 * pl + odd
                                o = bank(2 + 2 * n + odd)[:, P * (2 * t + pl):P * (2 * t + pl) + P]
                                m = pe.matmul(o, head(k_t, h, t), head(right, h, t), start=True, stop=True)
                m.then_inc(s_kkqk, 1)
                gate_chunk(GATE, gr + 1, s_gate_ev)
                pe.wait_ge(s_inv0, gr + 1)
                for t in range(NT):
                    for u in range(4):
                        m = pe.transpose(bank(t)[:, P * u:P * u + P], inv_t[:, t, u, :], ident[:, :])
                    m.then_inc(s_inv0_ps, 1)
                for n in range(1, len(LEVELS)):
                    for t in range(NT):
                        pe.wait_ge(s_lev, 12 * gr + 2 * (n - 1) + t + 1)
                        if n == 1:
                            pe.wait_ge(s_inv0_ev, 2 * gr + t + 1)
                        else:
                            pe.wait_ge(s_invd, 10 * gr + 2 * (n - 2) + t + 1)
                            pe.wait_ge(s_prod, 12 * gr + 2 * (n - 2) + t + 1)
                        for u in range(4):
                            m = pe.matmul(bank(t)[:, P * u:P * u + P], lev[n % 2][:, t, u, :],
                                          inv[:, t, u, :], start=True, stop=True)
                        m.then_inc(s_prod_ps, 1)
                    for t in range(NT):
                        pe.wait_ge(s_prod, 12 * gr + 2 * (n - 1) + t + 1)
                        if n >= 2:
                            pe.wait_ge(s_inv, 12 * gr + 2 * (n - 2) + t + 1)
                        if n < len(LEVELS) - 1:
                            for u in range(4):
                                m = pe.matmul(bank(2 + t)[:, P * u:P * u + P], inv_t[:, t, u, :],
                                              prod[:, t, u, :], start=True, stop=True)
                            m.then_inc(s_dinvd, 1)
                        for u in range(4):
                            m = pe.matmul(bank(4 + t)[:, P * u:P * u + P], prod[:, t, u, :],
                                          inv_t[:, t, u, :], start=True, stop=True)
                        m.then_inc(s_dinv, 1)
                pe.wait_ge(s_inv, 12 * gr + 12)
                for u in range(4):
                    h = 4 * gr + u
                    m = pe.matmul(bank(2)[64 * (h % 2):64 * (h % 2) + 64, P * (u // 2):P * (u // 2) + P],
                                  kb_g[:, HD * h:HD * h + HD], inv_t[:, 1, u, :], start=True, stop=True)
                m.then_inc(s_wt_ps, 1)
                for u in range(4):
                    h = 4 * gr + u
                    m = pe.matmul(bank(3)[:, HD * u:HD * u + HD], inv_t[:, 0, u, :],
                                  v_b[:, 0, HD * h:HD * h + HD], start=True, stop=True)
                m.then_inc(s_u0, 1)
                pe.wait_ge(s_v0, gr + 1)
                for u in range(4):
                    h = 4 * gr + u
                    m = pe.matmul(bank(4)[64 * (h % 2):64 * (h % 2) + 64, HD * (u // 2):HD * (u // 2) + HD],
                                  k_dec[:, HD * h:HD * h + HD], v_new[:, 0, HD * h:HD * h + HD],
                                  start=True, stop=True)
                m.then_inc(s_st_ps, 1)
                pe.wait_ge(s_st, gr + 1)
                pe.wait_ge(s_wt, gr + 1)
                for u in range(4):
                    h = 4 * gr + u
                    r = 64 * (h % 2)
                    o = bank(5 if r == 0 else 3)[:, HD * (u // 2):HD * (u // 2) + HD]
                    pe.matmul(o, inv_t[:, 1, u, :], v_b[:, 1, HD * h:HD * h + HD], start=True, stop=False)
                    m = pe.matmul(o, w_t[r:r + 64, u // 2, :], state[r:r + 64, u // 2, :],
                                  start=False, stop=True)
                m.then_inc(s_u1, 1)
                if gr == 0:
                    decays(1)
                for u in range(4):
                    h = 4 * gr + u
                    pe.matmul(bank(2)[:, HD * u:HD * u + HD], qk_t[:, 0, u, :],
                              v_new[:, 0, HD * h:HD * h + HD], start=True, stop=True)
                pe.wait_ge(s_v1, 2 * gr + 2)
                for u in range(4):
                    h = 4 * gr + u
                    r = 64 * (h % 2)
                    o = bank(4 if r == 0 else 5)[:, HD * (u // 2):HD * (u // 2) + HD]
                    pe.matmul(o, q_dec_t[r:r + 64, h // 2, :], state[r:r + 64, u // 2, :],
                              start=True, stop=False)
                    m = pe.matmul(o, qk_t[:, 1, u, :], v_new[:, 1, HD * h:HD * h + HD],
                                  start=False, stop=True)
                m.then_inc(s_o_ps, 1)

            def turn_out(o, first_bank):
                for b in range(2):
                    for c in (2 * b, 2 * b + 1):
                        for t in range(NT):
                            m = pe.transpose(split3(bank(first_bank + b), 2)[:, c % 2, P * t:P * t + P],
                                             o[:, t, P * c:P * c + P], ident[:, :])
                    m.then_inc(s_ot_ps, 1)
            pe.wait_ge(s_roped, 1)
            pe.wait_ge(s_o, 6)
            for j in range(6):
                for c in range(2 if j < 5 else 1):
                    b = 2 * j + c
                    for t in range(NT):
                        if b < 4:
                            src = z_tok[:, t, Z_BQ + P * b:Z_BQ + P * b + P]
                        elif b < 6:
                            src = k_dup[:, t, b - 4].rearrange("p a b -> p (a b)")
                        elif b < 10:
                            src = z_tok[:, t, Z_IQ + P * (b - 6):Z_IQ + P * (b - 6) + P]
                        else:
                            src = ik_dup[:, t].rearrange("p a b -> p (a b)")
                        m = pe.transpose(split3(bank(j), 2)[:, c, P * t:P * t + P], src, ident[:, :])
                m.then_inc(s_ro_ps, 1)
            gate_chunk(GATE, 3, s_gate_ev)
            pe.wait_ge(s_ro, 6)
            for j in range(6):
                t = by_keys(j)[0]
                hs = heads_of(j)
                for n, h in enumerate(hs):
                    r = 64 * (h % 2)
                    m = pe.matmul(split3(bank(j), len(hs))[:, n, :], ro_t[r:r + 64, 6 + h // 2, P * t:P * t + P],
                                  ro_t[r:r + 64, 10, 0:P * (t + 1)], start=True, stop=True)
                m.then_inc(s_rel_ps, 1)
            gate_chunk(GATE, 4, s_gate_ev)
            pe.wait_ge(s_on, 1)
            pe.wait_ge(s_rel, 6)
            turn_out(o_tok, 0)
            gate_chunk(GATE, 5, s_gate_ev)
            pe.wait_ge(s_o_ready, 2)
            for j in range(6):
                t = by_keys(j)[0]
                hs = heads_of(j)
                for n, h in enumerate(hs):
                    r = 64 * (h % 2)
                    m = pe.matmul(split3(bank(j), len(hs))[:, n, :],
                                  ro_t[r:r + 64, h // 2, P * t:P * t + P],
                                  ro_t[r:r + 64, 4 + h // 4, 0:P * (t + 1)], start=True, stop=True)
                m.then_inc(s_log_ps, 1)
            gate_chunk(GATE, 6, s_gate_ev)
            gate_chunk(GATE, 7, s_gate_ev)
            pe.wait_ge(s_gate_ev, 8)
            project(PROJ, 0, 0, 0)
            pe.wait_ge(s_msk, 6)
            project(PROJ, 0, 1, 0)

            def turn_probs(prb, base):
                for j in range(6):
                    pe.wait_ge(s_prob, base + (1 if j < 2 else 2))
                    if j >= 4:
                        pe.wait_ge(s_pt, 3 * base + j - 3)
                    for c in range(4):
                        n = 4 * j + c
                        src = prb[:, 0, n, 0:P] if j < 2 else prb[:, 1, (n - 8) // 2, P * (n % 2):P * (n % 2) + P]
                        m = pe.transpose(bank(j % 4)[:, P * c:P * c + P], src, ident[:, :])
                    m.then_inc(s_pt_ps, 1)

            def prob_times_v(prb_t, v, base):
                pe.wait_ge(s_pt, base + 6)
                for b in range(2):
                    for h in range(4 * b, 4 * b + 4):
                        r = 64 * (h % 2)
                        for t in range(NT):
                            o = split3(bank(2 + b), 2)[r:r + 64, (h // 2) % 2, P * t:P * t + P]
                            for s in range(t + 1):
                                m = pe.matmul(o, v(s, h), prb_t[:, h if t == 0 else 8 + 2 * h + s, :],
                                              start=(s == 0), stop=(s == t))
                    m.then_inc(s_pv_ps, 1)

            pe.wait_ge(s_msk, 6)
            turn_probs(prob, 0)
            prob_times_v(prob_t, lambda s, h: z_tok[:, s, Z_BV + HD * (h // 4):Z_BV + HD * (h // 4) + HD], 0)

            mix(PROJ, OUT, 0)
            turn_x(1)

            def small_cols(b, cols, sig_t, ev, sig, turn=None):
                n = cols.stop - cols.start
                o = bank(b)[0:n, 256:512]
                for k in range(KD):
                    if turn is not None:
                        wait_h(turn, k)
                    pe.matmul(o, rt_hi[:, k, cols], h_hi[:, k, :], start=(k == 0), stop=False)
                    pe.matmul(o, rt_hi[:, k, cols], h_lo[:, k, :], start=False, stop=False)
                    m = pe.matmul(o, rt_lo[:, k, cols], h_hi[:, k, :], start=False, stop=(k == KD - 1))
                m.then_inc(sig_t, 1)
                pe.wait_ge(*ev)
                for t in range(NT):
                    m = pe.transpose(bank(b)[:, n * t:n * t + n], cols_t[0:n, P * t:P * t + P], ident[0:n, 0:n])
                m.then_inc(sig, 1)

            pe.wait_ge(s_rt_lo, 1)
            small_cols(0, slice(0, 20), s_cols_ps, (s_cols, 1), s_rl_ps, 1)

            def spread_router(part):
                if part == 0:
                    pe.wait_ge(s_comb, 1)
                    for t in range(NT):
                        m = pe.transpose(bank(1)[0:16, P * t:P * t + P], comb[:, t, :], ident[:, :])
                    m.then_inc(s_ct_ps, 1)
                    pe.wait_ge(s_ct, 1)
                    pe.wait_ge(s_sel, 1)
                for b in range(4 * part, 4 * part + 4):
                    if b >= 4:
                        pe.wait_ge(s_cr, b - 3)
                    for c in range(2):
                        m = pe.matmul(split3(bank(b % 4), 2)[:, c, :], sel_e[0:16, 2 * b + c, :],
                                      comb_t[0:16, :], start=True, stop=True)
                    m.then_inc(s_cr_ps, 1)

            def ffn(F, first, early, turn=None, before_last=lambda: None):
                for e in range(len(F) + 1):
                    if e < len(F):
                        if e >= 2:
                            pe.wait_ge(s_prod2, first + e - 1)
                        for j in range(2):
                            b = split3(bank(4 + 2 * (e % 2) + j), 2)
                            weights_still(F[e][j], [b[:, 0, :], b[:, 1, :]], h_hi, h_lo,
                                          turn if e == j == 0 else None)
                            if e == 1 and early:
                                spread_router(j)
                    if e == 1 and early:
                        pe.wait_ge(s_cr, 8)
                    if e == len(F):
                        before_last()
                    if e >= 1:
                        pe.wait_ge(s_a, first + e)
                        b = 2 * ((e - 1) % 2)
                        outs = {(t, c): bank(2 * t + c) for t in range(NT) for c in range(2)}
                        weights_move(F[e - 1][2], outs, o_hi[:, b:b + 2], o_lo[:, b:b + 2],
                                         e == 1, e == len(F))

            ffn(EXP, 0, True)
            turn_x(2)

            for c in range(4):
                b = split3(bank(c), 2)
                weights_still(HGQF[c], [b[:, 0, :], b[:, 1, :]], h_hi, h_lo, 2 if c == 0 else None)
            tok_block(TOK2, 0, 512, N_TOK_BLK)
            small_cols(6, slice(20, 28), s_cols_ps, (s_cols, 2), s_tok_ps)
            pe.wait_ge(s_hev, 4)
            pe.wait_ge(s_fg, 2)
            for n in range(len(LEVELS) + 1):
                if n:
                    pe.wait_ge(s_hx, n)
                if n >= 2:
                    pe.wait_ge(s_hsc, n - 1)
                for u in range(8):
                    b = bank(2 * (n % 2) + u // 4)[:, P * (u % 4):P * (u % 4) + P]
                    left, right = (hk[:, u, :], hq[:, u, :]) if n == 0 else (hx[:, n % 2, u, :],) * 2
                    m = pe.matmul(b, left, right, start=True, stop=True)
                m.then_inc(s_hsc_ps, 1)
                b, k = 1 + n // 2, n % 2
                if n == 0:
                    pe.wait_ge(s_ff, 1)
                elif k == 0:
                    pe.wait_ge(s_tok_ev, N_TOK_BLK + b - 1)
                outs = {(t, 0): bank(4 + 2 * (b % 2) + t) for t in range(NT)}
                weights_move(LVL2[n], outs, h_hi[:, 4 * k:4 * k + 4], h_lo[:, 4 * k:4 * k + 4],
                             k == 0, k == 1)

            pe.wait_ge(s_hkd, 1)
            for h in range(HG_HEADS):
                m = pe.transpose(bank(0)[:, P * h:P * h + P], hkd[:, h, :], ident[:, :])
            m.then_inc(s_hkt_ps, 1)
            pe.wait_ge(s_tok_ev, N_TOK_BLK + 4)
            gate_chunk(GATE2, 0, s_gate_ev2)
            pe.wait_ge(s_hkt, 1)
            for h in range(HG_HEADS):
                m = pe.matmul(bank(1)[:, P * h:P * h + P], hkd_t[:, h, :],
                              z2[:, 0, Z2_I + P * h:Z2_I + P * h + P], start=True, stop=True)
            m.then_inc(s_hs_ps, 1)
            gate_chunk(GATE2, 1, s_gate_ev2)
            pe.wait_ge(s_hs, 1)
            pe.wait_ge(s_hsc, 8)
            for h in range(HG_HEADS):
                v = [z2[:, t, Z2_I + P * h:Z2_I + P * h + P] for t in range(NT)]
                pe.matmul(bank(2)[:, P * h:P * h + P], hsc[:, 2 * h, :], v[0], start=True, stop=True)
                pe.matmul(bank(3)[:, P * h:P * h + P], hqb[:, h, :], hs0[:, h, :], start=True, stop=False)
                m = pe.matmul(bank(3)[:, P * h:P * h + P], hsc[:, 2 * h + 1, :], v[1], start=False, stop=True)
            m.then_inc(s_ho_ps, 1)
            gate_chunk(GATE2, 2, s_gate_ev2)
            pe.wait_ge(s_qn, 3)
            pe.wait_ge(s_tok_ev, N_TOK_BLK + 5)
            for j in range(4):
                for c in range(4):
                    b, t = 2 * j + c // 2, c % 2
                    m = pe.transpose(bank((4, 5, 0, 1)[j])[:, P * c:P * c + P],
                                     z2[:, t, Z2_Q + P * b:Z2_Q + P * b + P], ident[:, :])
                m.then_inc(s_fq_ps, 1)
            gate_chunk(GATE2, 3, s_gate_ev2)
            pe.wait_ge(s_on, 2)
            turn_out(ho, 2)
            gate_chunk(GATE2, 4, s_gate_ev2)
            pe.wait_ge(s_fq, 4)
            pe.wait_ge(s_fmask, 1)
            pe.wait_ge(s_o_ready, 4)
            for j in range(6):
                t = by_keys(j)[0]
                hs = heads_of(j)
                for n, h in enumerate(hs):
                    r = 64 * (h % 2)
                    o = split3(bank(j), len(hs))[:, n, :]
                    pe.matmul(o, qk2_t[r:r + 64, h // 2, P * t:P * t + P],
                              qk2_t[r:r + 64, 4 + h // 2, 0:P * (t + 1)], start=True, stop=False)
                    if t == 1:
                        pe.matmul(o[:, 0:P], ones[:, :], f_mask[:, 0, h, :], start=False, stop=False)
                        pe.matmul(o[:, 0:P], upto[:, :], last(glog[:, 1, h], P),
                                  start=False, stop=False)
                    own = o[:, P * t:P * t + P]
                    pe.matmul(own, upto[:, :], f_mask[:, t, h, :], start=False, stop=False)
                    m = pe.matmul(own, ident_bf[:, :], future_bf[:, :], start=False, stop=True)
                m.then_inc(s_fl_ps, 1)
            gate_chunk(GATE2, 5, s_gate_ev2)
            gate_chunk(GATE2, 6, s_gate_ev2)
            turn_probs(prob2, 2)
            gate_chunk(GATE2, 7, s_gate_ev2)
            prob_times_v(prob2_t, lambda s, h: z2[:, s, Z2_V + HD * h:Z2_V + HD * h + HD], 6)
            project(PROJ2, 1, 0, 0)
            mix(PROJ2, OUT2, 1)
            turn_x(3)
            def turn_p():
                pe.wait_ge(s_p, 16)
                for k in range(2):
                    for t in range(NT):
                        m = pe.transpose(split3(bank(6), 2)[:, k, P * t:P * t + P],
                                         p_tok[:, t, P * k:P * k + P], ident[:, :])
                m.then_inc(s_p_ps, 1)

            ffn(FFN, N_EXP, False, 3, turn_p)
            pe.wait_ge(s_p_ready, 1)
            outs = {(t, c): bank(4 + 2 * c + t) for c in range(2) for t in range(NT)}
            weights_move(PLEP, outs, o_hi[:, 4:6], o_lo[:, 4:6], True, True)
            turn_x(4)
            for c in range(2):
                outs = {(t, 0): bank(2 * c + t) for t in range(NT)}
                turn = 4 if c == 0 else None
                weights_move(PLEG[c][0], outs, h_hi, h_lo, True, False, turn)
                weights_move(PLEG[c][1], outs, h_hi[:, 4:8], h_lo[:, 4:8], False, True, turn, 4)

        @block.vector
        def _(dve):
            n_dve, split_at = [0], [0]
            mult, add_, sub = ALU.mult, ALU.add, ALU.subtract

            def step(ins):
                n_dve[0] += 1
                ins.then_inc(s_dve, 1)
                dve.wait_ge(s_dve, n_dve[0])

            def mark(ins):
                n_dve[0] += 1
                ins.then_inc(s_dve, 1)
                return n_dve[0]

            def ahead(i):
                while split_at[0] <= min(i + SPL - 1, N_CH - 1):
                    j = split_at[0]
                    _, kt, n = chunks[j]
                    dve.wait_ge(w_high, j + 1)
                    dve.tensor_tensor(w_lo[:, j % SPL, 0:kt * n], raw[:, j % RAW, 0:kt * n],
                                      w_hi[:, j % SPL, 0:kt * n].bitcast(F32), sub).then_inc(w_ready, 1)
                    split_at[0] += 1

            def low(turn, row):
                for b in range(4):
                    dve.wait_ge(s_hhi, 8 * turn + 2 * b + 2)
                    for k in (2 * b, 2 * b + 1):
                        dve.scalar_tensor_tensor(h_lo[:, k, :], split3(bank(b), 2)[:, k % 2, :],
                                                 chan[:, row + k:row + k + 1],
                                                 h_hi[:, k, :].bitcast(F32), mult, sub).then_inc(s_h, 1)

            def norm(n, turn, row):
                dve.wait_ge(s_sq, sum(SQUARES[0:n + 1]))
                if n in X_HALVES:
                    step(dve.tensor_tensor(ssq, ssq4[:, 0], ssq4[:, 1], add_))
                dve.tensor_scalar(rms, ssq, 1.0 / DM, EPS, mult, add_).then_inc(s_ms, 1)
                dve.wait_ge(s_rt_n, n + 1)
                step(dve.reciprocal(rstd, rms))
                for t in range(NT):
                    dve.tensor_scalar(xn[:, t], x_tok[:, t], rstd[:, t:t + 1], None, mult).then_inc(s_xn, 1)
                if n == 0:
                    ahead(-2)
                low(turn, row)

            def final_and_mix():
                for c in range(2):
                    cols = slice(512 * c, 512 * c + 512)
                    dve.wait_ge(s_x_half, 3 + c)
                    dve.tensor_tensor(xg[:, :, cols], x_tok[:, :, cols],
                                      mid(rep[:, C_FIN + 512 * c:C_FIN + 512 * c + 512], NT), mult).then_inc(s_xg, 1)
                dve.wait_ge(s_sq, sum(SQUARES[0:4]))
                step(dve.tensor_tensor(ssq, ssq4[:, 0], ssq4[:, 1], add_))
                step(dve.tensor_scalar(rms4[:, 0:2], ssq, 1.0 / DM, EPS, mult, add_))
                dve.tensor_tensor(ssg, ssg4[:, 0], ssg4[:, 1], add_)
                step(dve.tensor_scalar(rms4[:, 2:4], rms4[:, 0:2], EPS, None, mult))
                dve.scalar_tensor_tensor(rms4[:, 2:4], ssg, 1.0 / DM, rms4[:, 2:4], mult, add_).then_inc(s_ms, 2)
                dve.wait_ge(s_rt_n, 4)
                step(dve.reciprocal(rstd4, rms4))
                for t in range(NT):
                    dve.tensor_scalar(xn[:, t], xg[:, t], rstd4[:, 2 + t:3 + t], None, mult).then_inc(s_xn, 1)
                for t in range(NT):
                    m = mark(dve.tensor_scalar(x_tok[:, t], xg[:, t], rstd4[:, t:t + 1], None, mult))
                dve.wait_ge(s_dve, m)
                low(2, R_NMIX)

            dve.wait_ge(s_chan_ps, 1)
            dve.tensor_copy(chan[:, :], bank(7)[:, 0:R_ALL]).then_inc(s_chan, 1)
            dve.wait_ge(s_chan, 1)
            norm(0, 0, R_N1)
            ahead(0)

            dve.wait_ge(s_rep_ps, 2)
            for r in range(3):
                n = min(512, C_ALL - 512 * r)
                dve.tensor_copy(rep[:, 512 * r:512 * r + n], bank(4 + r)[:, 0:n]).then_inc(s_chan, 1)
            dve.tensor_copy(over[:, 0, :], bank(6)[:, 400:432]).then_inc(s_chan, 1)

            step(dve.memset(z_t[:, :, 0:3], 0.0))
            for c in range(6):
                ahead(CONV[c])
                dve.wait_ge(s_conv_ev, c + 1)
                for k in range(4):
                    for ct in (2 * c, 2 * c + 1):
                        w = chan[:, R_CONV + 12 * k + ct:R_CONV + 12 * k + ct + 1]
                        taps = z_t[:, ct, k:k + S]
                        if k == 0:
                            m = dve.tensor_scalar(y_t[:, ct, :], taps, w, None, mult)
                        else:
                            dve.wait_ge(s_tap, 8 * c + 2 * (k - 1) + ct % 2 + 1)
                            m = dve.scalar_tensor_tensor(y_t[:, ct, :], taps, w, y_t[:, ct, :], mult, add_)
                        m.then_inc(s_tap, 1)
                dve.wait_ge(s_tap, 8 * c + 8)
                dve.nop().then_inc(s_conv, 1)
            ahead(TOK[0][0])
            dve.wait_ge(s_chan, 5)
            dve.wait_ge(s_pos, 16)
            step(dve.tensor_copy(pos_f[:, :], pos_i[:, :]))
            step(dve.tensor_tensor(cs[:, 1], last(pos_f[:, :], 32), mid(over[:, 0, :], 2), mult))
            magic = 12582912.0
            step(dve.tensor_scalar(turns, cs[:, 1], 0.15915494309189535, magic, mult, add_))
            step(dve.tensor_scalar(turns, turns, magic, None, sub))
            for part in (6.28125, 0.0019350051879882812, 3.0199159819567e-07):
                step(dve.scalar_tensor_tensor(cs[:, 1], turns, -part, cs[:, 1], mult, add_))
            step(dve.tensor_scalar(cs[:, 0], cs[:, 1], 1.5707963267948966, None, add_))
            step(dve.tensor_scalar(over, cs[:, 0], 3.141592653589793, -6.283185307179586,
                                   ALU.is_gt, mult))
            step(dve.tensor_tensor(cs[:, 0], cs[:, 0], over, add_))
            dve.tensor_scalar(cs[:, :, :, :], cs[:, :, :, :], 3.1415925, -3.1415925, ALU.min,
                              ALU.max).then_inc(s_trig, 1)
            ahead(TOK[0][1])
            dve.wait_ge(s_rt_hi, 1)
            dve.tensor_tensor(rt_lo[:, :, :], rt_raw[:, :, :], rt_hi[:, :, :].bitcast(F32),
                              sub).then_inc(s_rt_lo, 1)

            def softplus(n, ln_count):
                dve.scalar_tensor_tensor(sp2, sp1, -1.0, sp1, mult, ALU.min).then_inc(s_spe, 1)
                dve.wait_ge(s_spx, n + 1)
                dve.tensor_scalar(sp3, sp2, 1.0, None, add_).then_inc(s_spl, 1)
                dve.wait_ge(s_spm, ln_count)
                step(dve.scalar_tensor_tensor(sp1, sp1, 0.0, sp3, ALU.max, add_))

            ahead(TOK[1][0])
            dve.wait_ge(s_qkv, 6)
            step(dve.tensor_tensor(sq, qkv[:, :, 0:DM], qkv[:, :, 0:DM], mult))
            nrm_all = small[:, 128:160]
            step(dve.tensor_reduce(nrm_all, sq.rearrange("p t (h d) -> p (t h) d", d=HD), X, add_))
            dve.tensor_scalar(nrm_all, nrm_all, EPS, None, add_).then_inc(s_l2s, 1)
            ahead(TOK[1][1])
            dve.wait_ge(s_l2r, 1)
            step(dve.reciprocal(nrm_all, nrm_all))
            step(dve.tensor_scalar(nrm[:, :, 0:8], nrm[:, :, 0:8], HD ** -0.5, None, mult))
            for t in range(NT):
                heads = qkv[:, t, 0:DM].rearrange("p (h d) -> p h d", d=HD)
                m = mark(dve.tensor_tensor(heads, heads, last(nrm[:, t, :], HD), mult))
            dve.wait_ge(s_dve, m)
            ahead(TOK[2][0])
            dve.wait_ge(s_tok_ev, 2)
            step(dve.tensor_tensor(sp1, z_tok[:, :, Z_ALPHA:Z_ALPHA + 8],
                                   mid(rep[:, C_DT:C_DT + 8], 2), add_))
            softplus(0, 2)
            dve.scalar_tensor_tensor(glog, sp1, -1.0, mid(alog, 2), mult, mult).then_inc(s_glog, 1)
            ahead(TOK[2][1])
            dve.wait_ge(s_beta, 1)

            def h64(ap):
                return ap.rearrange("p (h d) -> p h d", d=HD)
            for t in range(NT):
                dve.tensor_tensor(h64(v_b[:, t]), h64(qkv[:, t, 1024:1536]), last(beta[:, t], HD), mult)
                m = dve.tensor_tensor(h64(k_b[:, t]), h64(qkv[:, t, 512:1024]), last(beta[:, t], HD), mult)
            m.then_inc(s_qn, 1)
            ahead(TOK[3][0])
            dve.wait_ge(s_eg, 1)
            dve.wait_ge(s_qn, 1)
            dve.tensor_tensor(h64(q_dec), h64(qkv[:, 1, 0:512]), last(e_g[:, 1], HD), mult)
            dve.tensor_tensor(h64(k_dec), h64(qkv[:, 0, 512:1024]), last(e_gl[:, 0], HD), mult)
            dve.tensor_tensor(h64(kb_g), h64(k_b[:, 1]), last(e_g[:, 1], HD), mult).then_inc(s_qn, 1)

            def rope(t, part):
                first, heads = ((Z_BQ, 10), (Z_IQ, 9))[part]
                v = h64(z_tok[:, t, first:first + HD * heads])
                a, b = v[:, :, 0:32], v[:, :, 32:64]
                cos, sin = (mid(cs[:, n, t, :], heads) for n in range(2))
                ta, tb = rt1[:, 0:heads], rt2[:, 0:heads]
                dve.tensor_tensor(ta, a, sin, mult)
                step(dve.tensor_tensor(tb, b, sin, mult))
                dve.tensor_tensor(a, a, cos, mult)
                step(dve.tensor_tensor(b, b, cos, mult))
                dve.tensor_tensor(a, a, tb, sub)
                step(dve.tensor_tensor(b, b, ta, add_))

            def decay_operand(gr):
                for t in range(NT):
                    m = dve.tensor_tensor(g_mask[:, t], mid(after[:, :], 4),
                                          last(glog[:, t, 4 * gr:4 * gr + 4], P), mult)
                m.then_inc(s_gmask, 1)

            dve.wait_ge(s_const, N_CONST)
            dve.wait_ge(s_heads_ps, 6)
            dve.wait_ge(s_qn, 2)
            decay_operand(0)
            ahead(TOK[3][1])
            ahead(GATE[0])
            for gr in range(2):
                dve.wait_ge(s_dexp, 2 * gr + 2)
                d8, a8, p8, t8 = (v.rearrange("p t u i -> p (t u) i") for v in (dec, a_t, prod, inv_t))
                step(dve.tensor_tensor(d8, d8, mid(upto[:, :], 8), mult))
                dve.wait_ge(s_kkqk, gr + 1)
                for dst, first in ((qk_t, 4), (a_t, 2)):
                    for odd in range(2):
                        of = [v.rearrange("p t (a b) i -> p (t a) b i", b=2)[:, :, odd, :] for v in (dst, dec)]
                        m = dve.tensor_tensor(of[0], split3(bank(first + odd), 4), of[1], mult)
                m.then_inc(s_at, 1)
                dve.wait_ge(s_at, gr + 1)
                step(dve.tensor_tensor(p8, a8, mid(lvl[:, 0, :], 8), mult))
                step(dve.tensor_tensor(t8, mid(ident[:, :], 8), p8, sub))
                dve.nop().then_inc(s_inv0, 1)
                ahead(GATE[gr + 1])
                for n in range(1, len(LEVELS)):
                    for t in range(NT):
                        k = 12 * gr + 2 * (n - 1) + t + 1
                        if n == 1:
                            dve.wait_ge(s_inv0_ev, 2 * gr + t + 1)
                        if n < len(LEVELS) - 1:
                            dve.wait_ge(s_dinvd, 10 * gr + 2 * (n - 1) + t + 1)
                            dve.tensor_tensor(inv[:, t], inv[:, t], split3(bank(2 + t), 4),
                                              sub).then_inc(s_invd, 1)
                        dve.wait_ge(s_dinv, k)
                        dve.tensor_tensor(inv_t[:, t], inv_t[:, t], split3(bank(4 + t), 4),
                                          sub).then_inc(s_inv, 1)
                        dve.wait_ge(s_inv, k)
                    if gr == 0 and n < 5:
                        if n == 1:
                            dve.wait_ge(s_sin, 1)
                            dve.wait_ge(s_tok_ev, N_TOK_BLK)
                        rope((n - 1) // 2, (n - 1) % 2)
                if gr == 0:
                    ahead(GATE[2])
                    decay_operand(1)

            def o_norm(o, o_sq, n, heads, dim, gain, z, middle):
                o3 = o.rearrange("p t (h d) -> p (t h) d", d=dim)
                dve.wait_ge(s_o if n == 0 else s_ho, 6 if n == 0 else 1)
                step(dve.tensor_tensor(o_sq, o, o, mult))
                nr = nrm[:, :, 0:heads]
                step(dve.tensor_reduce(nr, o_sq.rearrange("p t (h d) -> p t h d", d=dim), X, add_))
                dve.tensor_scalar(nr, nr, 1.0 / dim, EPS, mult, add_).then_inc(s_ors, 1)
                middle()
                dve.wait_ge(s_orr, n + 1)
                step(dve.reciprocal(nr, nr))
                for t in range(NT):
                    ot = o[:, t].rearrange("p (h d) -> p h d", d=dim)
                    m = mark(dve.tensor_tensor(ot, ot, last(nrm[:, t, 0:heads], dim), mult))
                dve.wait_ge(s_dve, m)
                step(dve.tensor_tensor(o3, o3, mid(gain, 2 * heads), mult))
                dve.wait_ge(s_zs, n + 1)
                dve.tensor_tensor(o, o, z, mult).then_inc(s_on, 1)

            def out_low(n, first_bank):
                for b in range(2):
                    dve.wait_ge(s_ohi, 2 * n + b + 1)
                    dve.tensor_tensor(o_lo[:, 2 * b:2 * b + 2, :], split3(bank(first_bank + b), 2),
                                      o_hi[:, 2 * b:2 * b + 2, :].bitcast(F32), sub).then_inc(s_o_ready, 1)

            for t in range(NT):
                dve.tensor_copy(k_dup[:, t], h64(z_tok[:, t, Z_BQ + 512:Z_BV]).unsqueeze(2)
                                .broadcast_to([P, 2, 2, HD]))
                m = dve.tensor_copy(ik_dup[:, t], mid(z_tok[:, t, Z_IQ + 512:Z_IW], 2))
            m.then_inc(s_roped, 1)
            o_norm(o_tok, o_sq, 0, HEADS, HD, rep[:, C_ANORM:C_ANORM + HD],
                   z_tok[:, :, Z_Z:Z_Z + 512], lambda: ahead(GATE[4]))

            step(dve.tensor_scalar(iw, z_tok[:, :, Z_IW:Z_IW + 8], (HEADS ** -0.5) * (HD ** -0.5), None, mult))
            for h in range(HEADS):
                for t in range(NT):
                    k = P * (t + 1)
                    dve.wait_ge(s_rel, key_bank(t, h)[0] + 1)
                    if h == 0:
                        m = mark(dve.tensor_scalar(score[:, t, 0:k], rel[:, t, h, 0:k], iw[:, t, h:h + 1], None, mult))
                    else:
                        dve.wait_ge(s_dve, n_dve[0] - 1)
                        m = mark(dve.scalar_tensor_tensor(score[:, t, 0:k], rel[:, t, h, 0:k], iw[:, t, h:h + 1],
                                                          score[:, t, 0:k], mult, add_))
            dve.wait_ge(s_dve, m)
            ahead(GATE[5])
            out_low(0, 0)
            ahead(GATE[6])
            for t in range(NT):
                m = mark(dve.memset(score[0:CHUNK, t, P * t + CHUNK:P * t + P], -BIG))
            dve.wait_ge(s_dve, m)
            tops = (top8, top8b)
            for r in range(TOPK // 8):
                for t in range(NT):
                    src = (score if r == 0 else work)[:, t, 0:P * (t + 1)]
                    if r:
                        dve.wait_ge(s_dve, n_dve[0] - 1 + t)
                    m = mark(dve.max(tops[t], src))
                for t in range(NT):
                    src = (score if r == 0 else work)[:, t, 0:P * (t + 1)]
                    dve.wait_ge(s_dve, m - 1 + t)
                    mark(dve.match_replace(work[:, t, 0:P * (t + 1)], tops[t], src, TAKEN))
            dve.wait_ge(s_dve, n_dve[0])
            for t in range(NT):
                k = P * (t + 1)
                m = mark(dve.tensor_scalar(work[:, t, 0:k], work[:, t, 0:k], -2e38, -BIG, ALU.is_gt, mult))
            dve.wait_ge(s_dve, m)
            for j in range(6):
                t, hs = by_keys(j)
                k, n = P * (t + 1), len(heads_of(j))
                dve.wait_ge(s_log_ps, j + 1)
                dve.tensor_tensor(prob[:, t, hs, 0:k], split3(bank(j), n),
                                  mid(work[:, t, 0:k], n), add_).then_inc(s_msk, 1)

            def softmax(prb, srcs, scale, base):
                for t in range(NT):
                    for hs, src, wait in srcs(t):
                        wait()
                        m = mark(dve.reduce_max(mx[:, t, hs], src, X))
                    dve.wait_ge(s_dve, m)
                    dve.tensor_scalar(nmx[:, t, 0:8], mx[:, t, 0:8], -scale, None, mult).then_inc(s_nmx, 1)
                for t in range(NT):
                    k = P * (t + 1)
                    dve.wait_ge(s_exp, 8 * (base + t + 1))
                    step(dve.reciprocal(rden[:, t, 0:8], den[:, t, 0:8]))
                    dve.tensor_tensor(prb[:, t, :, 0:k], prb[:, t, :, 0:k], last(rden[:, t, 0:8], k),
                                      mult).then_inc(s_prob, 1)

            ahead(GATE[7])
            softmax(prob, lambda t: [(slice(0, 8), prob[:, t, :, 0:P * (t + 1)],
                                      lambda: dve.wait_ge(s_msk, 2 if t == 0 else 6))], HD ** -0.5, 0)

            def gate_first(PR, n, halves):
                dve.wait_ge(s_gate, 16 * (n + 1))
                for c in halves:
                    dve.wait_ge(w_used, PR[0][c] + 1)
                    dve.tensor_tensor(ga[c], (gate, gate2)[n][:, 4 * c:4 * c + 4],
                                      split3(bank(PROJ_BANK[n][c][0], 2), 4), mult).then_inc(s_ga, 1)
                dve.wait_ge(s_ga, 2 * n + halves[-1] + 1)

            def attention_low(n):
                for b in range(2):
                    dve.wait_ge(s_pv_hi, 2 * n + b + 1)
                    dve.tensor_tensor(o_lo[:, 4 + 2 * b:6 + 2 * b, :], split3(bank(2 + b), 2),
                                      o_hi[:, 4 + 2 * b:6 + 2 * b, :].bitcast(F32), sub).then_inc(s_bout, 1)
            ahead(PROJ[0][0])
            gate_first(PROJ, 0, (0, 1))
            attention_low(0)
            ahead(PROJ[0][1])

            def mix(PR, OU, n):
                for c in range(2):
                    if n == 1:
                        gate_first(PR, n, (c,))
                    ahead(PR[1][c])
                    dve.wait_ge(w_used, PR[1][c] + 1)
                    step(dve.tensor_tensor(gb[n], (gate, gate2)[n][:, 8 + 4 * c:12 + 4 * c],
                                           split3(bank(PROJ_BANK[n][c][1], 2), 4), mult))
                    dve.tensor_tensor(ga[c], ga[c], gb[n], add_).then_inc(s_merge, 1)
                    dve.wait_ge(s_merge_hi, 2 * n + c + 1)
                    dve.tensor_tensor(h_lo[:, 4 * c:4 * c + 4, :], ga[c], h_hi[:, 4 * c:4 * c + 4, :].bitcast(F32),
                                      sub).then_inc(s_merged, 1)
                for c in range(2):
                    ahead(OU[c][0])
                    ahead(OU[c][1])
                    dve.wait_ge(w_used, OU[c][1] + 1)
                    cols = slice(512 * c, 512 * c + 512)
                    dve.tensor_tensor(x_tok[:, :, cols], x_tok[:, :, cols], split3(bank(PROJ_BANK[n][0][c], 2), 2),
                                      add_).then_inc(s_x_half, 1)

            def p_low():
                dve.wait_ge(s_p_hi, 1)
                dve.tensor_tensor(o_lo[:, 4:6, :], split3(bank(6), 2), o_hi[:, 4:6, :].bitcast(F32),
                                  sub).then_inc(s_p_ready, 1)
                ahead(PLEP)

            def ffn(F, first, weighted, before_sum=lambda: None):
                for e in range(len(F)):
                    ahead(F[e][1])
                    dve.wait_ge(w_used, F[e][1] + 1)
                    dve.wait_ge(s_silu, first + e + 1)
                    if e >= 2:
                        dve.wait_ge(s_a, first + e - 1)
                    up = split3(bank(5 + 2 * (e % 2)), 2)
                    m = dve.tensor_tensor(act_p[:, e % 2], act_s[:, e % 2], up, mult)
                    if weighted:
                        dve.wait_ge(s_cr, e // 2 + 1)
                        step(m)
                        m = dve.tensor_tensor(act_p[:, e % 2], act_p[:, e % 2], mid(comb_rep[:, e, :], 2), mult)
                    m.then_inc(s_prod2, 1)
                    ahead(F[e][1] + 1)
                    dve.wait_ge(s_ahi, first + e + 1)
                    b = 2 * (e % 2)
                    dve.tensor_tensor(o_lo[:, b:b + 2, :], act_p[:, e % 2], o_hi[:, b:b + 2, :].bitcast(F32),
                                      sub).then_inc(s_a, 1)
                ahead(F[-1][2])
                before_sum()
                dve.wait_ge(w_used, F[-1][2] + 1)
                down = bank(0, 4).rearrange("p (t c n) -> p t c n", t=NT, c=2)
                for c in range(2):
                    cols = slice(512 * c, 512 * c + 512)
                    dve.tensor_tensor(x_tok[:, :, cols], x_tok[:, :, cols], down[:, :, c],
                                      add_).then_inc(s_x_half, 1)

            mix(PROJ, OUT, 0)
            norm(1, 1, R_N2)
            ahead(EXP[0][0])
            for j in range(4):
                m = mark(dve.memset(tie[:, j:j + 1], float(4 - j)))
            dve.wait_ge(s_dve, m)

            def one_hot(dst, src, top):
                step(dve.tensor_reduce(top, src, X, ALU.max))
                step(dve.tensor_tensor(dst, src, last(top, 4), ALU.is_equal))
                step(dve.tensor_tensor(dst, dst, mid(tie, 2), mult))
                step(dve.tensor_reduce(gs2, dst, X, ALU.max))
                step(dve.tensor_tensor(dst, dst, last(gs2, 4), ALU.is_equal))

            dve.wait_ge(s_rl_ps, 1)
            step(dve.tensor_tensor(rl, split3(bank(0)[:, 0:40], 2), mid(rep[:, C_RB:C_RB + 20], 2), add_))
            gl = rl[:, :, 0:4]
            one_hot(ga1, gl, gs1)
            step(dve.tensor_tensor(ttmp, rl[:, :, 4:20].rearrange("p t (g j) -> p t g j", j=4), last(ga1, 4), mult))
            step(dve.tensor_reduce(el, ttmp.rearrange("p t g j -> p t j g"), X, add_))
            dve.tensor_tensor(gl, gl, last(gs1, 4), sub).then_inc(s_rlm, 1)
            step(dve.tensor_reduce(gs3, el, X, ALU.max))
            dve.tensor_tensor(el, el, last(gs3, 4), sub).then_inc(s_rlm, 1)
            dve.wait_ge(s_rle, 2)
            step(dve.tensor_reduce(gs3, gl, X, add_))
            step(dve.reciprocal(gs3, gs3))
            one_hot(e1h, el, gs1)
            step(dve.scalar_tensor_tensor(ea, e1h, -4.0, el, mult, add_))
            one_hot(e2h, ea, gs1)
            step(dve.tensor_tensor(e1h, e1h, e2h, add_))
            step(dve.tensor_tensor(e1h, e1h, el, mult))
            step(dve.tensor_reduce(gs1, e1h, X, add_))
            step(dve.reciprocal(gs1, gs1))
            step(dve.tensor_tensor(gs1, gs1, gs3, mult))
            step(dve.tensor_tensor(e1h, e1h, last(gs1, 4), mult))
            dve.tensor_tensor(comb.rearrange("p t (g j) -> p t g j", j=4), last(ga1, 4),
                              e1h.unsqueeze(2).broadcast_to([P, NT, 4, 4]), mult).then_inc(s_comb, 1)
            ffn(EXP, 0, True)

            final_and_mix()
            l0, l1 = chan[:, R_LB:R_LB + 4], chan[:, R_LB + 4:R_LB + 8]
            step(dve.tensor_tensor(lbt, l0, l1, ALU.max))
            dve.tensor_tensor(lb, l0, lbt, sub)
            dve.tensor_tensor(lbc, l1, lbt, sub).then_inc(s_lbs, 1)
            for c in range(4):
                ahead(HGQF[c])
            dve.wait_ge(s_lbe, 1)
            step(dve.tensor_tensor(lbt, lb, lbc, add_))
            step(dve.reciprocal(lbt, lbt))
            step(dve.tensor_tensor(lb, lb, lbt, mult))
            step(dve.tensor_tensor(lbc, lbc, lbt, mult))
            dve.wait_ge(s_hev, 4)
            for h in range(HG_HEADS):
                two = hk[:, 2 * h:2 * h + 2, :]
                m = dve.tensor_scalar(two, two, lbc[:, h:h + 1], lb[:, h:h + 1], mult, add_)
            m.then_inc(s_fg, 1)
            step(dve.memset(hsc, 0.0))
            dve.wait_ge(s_logf, 1)
            step(dve.tensor_scalar(hk, hk, -1.0, 1.0, mult, add_))
            dve.nop().then_inc(s_fg, 1)
            for u in range(8):
                m = mark(dve.tensor_tensor_scan(hb[:, u, :], ones[:, :], hd[:, u, :], 0.0, mult, add_))
            dve.wait_ge(s_dve, m)
            ahead(TOK2[0][0])
            ahead(TOK2[0][1])
            flat_b, flat_d, flat_e, flat_k, flat_q = (v.rearrange("p a b -> p (a b)") for v in (hb, hd, he, hk, hq))
            for n in range(len(LEVELS) + 1):
                if n < len(LEVELS):
                    s = LEVELS[n]
                    bl = split3(flat_b, 512 // s)
                    step(dve.tensor_tensor(split3(flat_d, 512 // s), bl,
                                           bl[:, :, s - 1:s].broadcast_to([P, 512 // s, 2 * s]), sub))
                    dve.scalar_tensor_tensor(flat_d, flat_d, -1.0, flat_d, mult, ALU.min).then_inc(s_hd, 1)
                dve.wait_ge(s_hsc_ps, n + 1)
                mask = ident[:, :] if n == 0 else lvl[:, n - 1, :]
                dve.copy_predicated(hsc, mid(mask, 8).bitcast(I32), split3(bank(2 * (n % 2), 2), 8)).then_inc(s_hsc, 1)
                if n < len(LEVELS):
                    dve.wait_ge(s_he, n + 1)
                    s = LEVELS[n]

                    def half(v, i):
                        return v.rearrange("p (b h r) -> p b h r", h=2, r=s)[:, :, i, :]
                    x_op = hx[:, (n + 1) % 2].rearrange("p a b -> p (a b)")
                    dve.tensor_tensor(half(x_op, 0), half(flat_k, 0), half(flat_e, 0), mult)
                    dve.tensor_tensor(half(x_op, 1), half(flat_q, 1), half(flat_e, 1), mult).then_inc(s_hx, 1)
                    if n + 1 == len(LEVELS):
                        dve.wait_ge(s_hx, n + 1)
                    ahead(LVL2[n])
            by_tile = [v.rearrange("p (h t) i -> p h t i", t=2) for v in (hb, he, hk, hq)]
            tb, te, tk, tq = by_tile
            dve.tensor_tensor(te[:, :, 0, :], tb[:, :, 0, P - 1:P].broadcast_to([P, HG_HEADS, P]), tb[:, :, 0, :], sub)
            dve.tensor_copy(te[:, :, 1, :], tb[:, :, 1, :]).then_inc(s_hio, 1)
            dve.wait_ge(s_hie, 1)
            dve.tensor_tensor(hqb, tq[:, :, 1, :], te[:, :, 1, :], mult)
            dve.tensor_tensor(hkd, tk[:, :, 0, :], te[:, :, 0, :], mult).then_inc(s_hkd, 1)
            dve.wait_ge(s_ff, 1)
            step(dve.tensor_tensor(sp1, z2[:, :, Z2_F:Z2_F + 8], mid(rep[:, C_FB:C_FB + 8], 2), add_))
            step(dve.tensor_scalar(sp1, sp1, -1.0, None, mult))
            softplus(1, 3)
            ahead(LVL2[7])
            step(dve.tensor_scalar(glog, sp1, -1.0, None, mult))
            dve.wait_ge(s_tok_ev, N_TOK_BLK + 4)
            for t in range(NT):
                qk = z2[:, t, Z2_Q:Z2_V]
                step(dve.tensor_tensor(fsq, qk, qk, mult))
                step(dve.tensor_reduce(nrm2[:, t, :], h64(fsq), X, add_))
            dve.tensor_scalar(nrm2, nrm2, 1.0 / HD, EPS, mult, add_).then_inc(s_l2s, 1)
            ahead(GATE2[0])
            dve.wait_ge(s_l2r, 2)
            step(dve.reciprocal(nrm2, nrm2))
            step(dve.tensor_scalar(nrm2[:, :, 0:8], nrm2[:, :, 0:8], HD ** -0.5, None, mult))
            for t in range(NT):
                qk = h64(z2[:, t, Z2_Q:Z2_V])
                m = mark(dve.tensor_tensor(qk, qk, last(nrm2[:, t, :], HD), mult))
            dve.wait_ge(s_dve, m)
            for t in range(NT):
                for first, c in ((Z2_Q, C_QN), (Z2_K, C_KN)):
                    v = h64(z2[:, t, first:first + 512])
                    m = dve.tensor_tensor(v, v, mid(rep[:, c:c + HD], 8), mult)
            m.then_inc(s_qn, 1)
            ahead(GATE2[1])
            o_norm(ho, hsq, 1, HG_HEADS, HG_D, rep[:, C_ONORM:C_ONORM + HG_D], z2[:, :, Z2_G:Z2_G + 512],
                   lambda: ahead(GATE2[2]))
            for t in range(NT):
                m = dve.tensor_tensor(f_mask[:, t], mid(after[:, :], 8), last(glog[:, t], P), mult)
            m.then_inc(s_fmask, 1)
            ahead(GATE2[3])
            out_low(1, 2)
            ahead(GATE2[4])
            ahead(GATE2[5])
            softmax(prob2, lambda t: [(by_keys(j)[1], split3(bank(j), len(heads_of(j))),
                                       lambda j=j: dve.wait_ge(s_fl_ps, j + 1))
                                      for j in range(6) if by_keys(j)[0] == t], 1.0, 2)
            ahead(GATE2[6])
            ahead(GATE2[7])
            ahead(PROJ2[0][0])
            attention_low(1)
            ahead(PROJ2[1][0])
            mix(PROJ2, OUT2, 1)
            norm(4, 3, R_NFFN)
            ffn(FFN, N_EXP, False, p_low)
            norm(5, 4, R_NPLE)
            for c in range(2):
                ahead(PLEG[c][0])
                ahead(PLEG[c][1])
            for c in range(2):
                cols = slice(512 * c, 512 * c + 512)
                dve.wait_ge(s_plg, c + 1)
                step(dve.tensor_tensor(res[:, :, cols], res[:, :, cols], split3(bank(4 + 2 * c, 2), 2), mult))
                dve.tensor_tensor(res[:, :, cols], res[:, :, cols], x_tok[:, :, cols], add_).then_inc(s_result, 1)


_INS = ["x", "positions", "norm1_g", "w_in", "b_gate", "conv_w", "a_log", "dt_bias", "a_norm_g",
        "w_proj_a", "w_proj_b", "w_out", "norm2_g", "w_router_group", "b_router_group",
        "w_router_expert", "b_router_expert", "w_exp_gate", "w_exp_up", "w_exp_down",
        "final_norm_g", "p_2", "norm_mix_g_2", "w_in_2", "hg_lb_logits_2", "hg_onorm_g_2",
        "fox_f_bias_2", "fox_q_norm_g_2", "fox_k_norm_g_2", "w_branch_a_2", "w_branch_b_2",
        "w_out_2", "norm_ffn_g_2", "w_ffn_gate_2", "w_ffn_up_2", "w_ffn_down_2", "norm_ple_g_2",
        "w_ple_gate_2", "w_ple_proj_2"]


def kernel(**inputs):
    import numpy as np
    import concourse.bacc as bacc
    from concourse.bass_utils import run_bass_kernel_spmd

    nc = bacc.Bacc("TRN2", target_bir_lowering=False, num_devices=1,
                   dynamic_dma_scratch_size=1024)
    arrays, args = {}, []

    def give(name, a):
        arrays[f"in_{name}"] = a
        args.append(nc.dram_tensor(f"in_{name}", a.shape, mybir.dt.from_np(a.dtype),
                                   kind="ExternalInput").ap())

    for name in _INS:
        give(name, np.ascontiguousarray(inputs[name]))
    half = HD // 2
    give("rope_freq", (np.float32(10000.0) ** (-np.arange(half, dtype=np.float32) / np.float32(half)))
         .astype(np.float32).reshape(1, half))
    out = nc.dram_tensor("out", (1, S, DM), F32, kind="ExternalOutput").ap()
    two_block_program(nc, *args, out)
    r = run_bass_kernel_spmd(nc, [arrays], core_ids=[0])
    return r.results[0]["out"]
```
